# Optimizing a Trainium2 kernel written in Bass

```python
import jax, jax.numpy as jnp
from jax import lax
import numpy as np

D_MODEL = 1024
BATCH = 1
SEQ = 512
DEPTH = 1

RET_HEADS = 4
RET_DK = 64
RET_DV = 128
RET_CHUNK = 128
DSA_HEADS = 8
DSA_KV_HEADS = 2
DSA_HD = 64
IDX_HEADS = 8
IDX_HD = 64
TOPK_MAX = 256
Q_BLOCK = 128
N_EXPERTS = 32
TOP_K = 4
D_EXPERT = D_MODEL
SWIGLU_LIMIT = 7.0
SWIGLU_ALPHA = 1.702
MOE_BLOCK = 128
EPS = 1e-6

RET_W = RET_HEADS * RET_DV
DSA_W = DSA_HEADS * DSA_HD
MIX_W = RET_W + DSA_W
IN_SPLITS = (RET_HEADS * RET_DK,
             RET_HEADS * RET_DK,
             RET_W,
             RET_W,
             DSA_HEADS * DSA_HD,
             DSA_KV_HEADS * DSA_HD,
             DSA_KV_HEADS * DSA_HD,
             IDX_HEADS * IDX_HD,
             IDX_HD,
             IDX_HEADS)
IN_COLS = sum(IN_SPLITS)

kernel_name = 'hybrid_retention_dsa_moe_layer'

def rms_norm(x, g):
    xf = x.astype(jnp.float32)
    y = xf * lax.rsqrt(jnp.mean(xf * xf, axis=-1, keepdims=True) + EPS)
    return (y * g.astype(jnp.float32)).astype(x.dtype)

def retention(q, k, v):
    B, S, H, dk = q.shape
    dv = v.shape[-1]
    dt = q.dtype
    C = min(RET_CHUNK, S)
    N = S // C
    log_g = jnp.log1p(-jnp.exp2(-5.0 - jnp.arange(H, dtype=jnp.float32)))
    pos = jnp.arange(C, dtype=jnp.float32)
    diff = pos[:, None] - pos[None, :]
    d_inner = jnp.where(diff[None] >= 0,
                        jnp.exp(jnp.maximum(diff, 0.0)[None] * log_g[:, None, None]), 0.0)
    q_decay = jnp.exp((pos + 1.0)[None] * log_g[:, None])
    k_decay = jnp.exp((C - 1.0 - pos)[None] * log_g[:, None])
    chunk_decay = jnp.exp(C * log_g).astype(dt)
    qc = q.reshape(B, N, C, H, dk)
    kc = (k * (dk ** -0.5)).reshape(B, N, C, H, dk)
    vc = v.reshape(B, N, C, H, dv)
    s = jnp.einsum('bnihd,bnjhd->bnhij', qc, kc) * d_inner.astype(dt)
    o_in = jnp.einsum('bnhij,bnjhe->bnihe', s, vc)
    kv = jnp.einsum('bnjhd,bnjhe,hj->nbhde', kc, vc, k_decay.astype(dt))

    def step(R, kv_n):
        return R * chunk_decay[None, :, None, None] + kv_n, R

    _, r_prev = lax.scan(step, jnp.zeros((B, H, dk, dv), dt), kv)
    o_cross = jnp.einsum('bnihd,nbhde,hi->bnihe', qc, r_prev, q_decay.astype(dt))
    return (o_in + o_cross).reshape(B, S, H, dv)

def sparse_attention(q, k, v, q_idx, k_idx, w_idx):
    B, S, H, d = q.shape
    G = k.shape[2]
    R = H // G
    n_sel = min(TOPK_MAX, S // 4)
    QB = min(Q_BLOCK, S)
    NB = S // QB
    slopes = jnp.exp2(-8.0 * (jnp.arange(H, dtype=jnp.float32) + 1.0) / H).reshape(G, R)
    key_pos = jnp.arange(S)

    def to_blocks(a):
        return a.reshape((B, NB, QB) + a.shape[2:]).swapaxes(0, 1)

    def block(args):
        qb, qib, wb, blk = args
        t = blk * QB + jnp.arange(QB)
        rel = jnp.einsum('bqhe,bse->bqhs', qib, k_idx)
        score = jnp.einsum('bqhs,bqh->bqs', jax.nn.relu(rel), wb).astype(jnp.float32)
        causal = key_pos[None, :] <= t[:, None]
        score = jnp.where(causal[None], score, -jnp.inf)
        _, sel = lax.top_k(score, n_sel)
        k_sel = jax.vmap(lambda kk, ii: kk[ii])(k, sel)
        v_sel = jax.vmap(lambda vv, ii: vv[ii])(v, sel)
        qg = qb.reshape(B, QB, G, R, d)
        logits = jnp.einsum('bqgrd,bqkgd->bqgrk', qg, k_sel).astype(jnp.float32) * (d ** -0.5)
        dist = (t[None, :, None] - sel).astype(jnp.float32)
        logits = logits - slopes[None, None, :, :, None] * dist[:, :, None, None, :]
        logits = jnp.where((dist >= 0)[:, :, None, None, :], logits, -jnp.inf)
        p = jax.nn.softmax(logits, axis=-1).astype(v.dtype)
        o = jnp.einsum('bqgrk,bqkgd->bqgrd', p, v_sel)
        return o.reshape(B, QB, H * d)

    out = lax.map(block, (to_blocks(q), to_blocks(q_idx), to_blocks(w_idx), jnp.arange(NB)))
    return out.swapaxes(0, 1).reshape(B, S, H * d)

def moe(h, router_w, router_b, w_gu, b_gu, w_down, b_down):
    N, D = h.shape
    logits = (h @ router_w + router_b).astype(jnp.float32)
    top_vals, top_idx = lax.top_k(logits, TOP_K)
    gates = jax.nn.softmax(top_vals, axis=-1).astype(h.dtype)
    NK = N * TOP_K
    flat_e = top_idx.reshape(-1)
    flat_tok = jnp.repeat(jnp.arange(N), TOP_K)
    flat_g = gates.reshape(-1)
    order = jnp.argsort(flat_e)
    sorted_e = flat_e[order]
    counts = jnp.bincount(flat_e, length=N_EXPERTS)
    starts = jnp.cumsum(counts) - counts
    padded_counts = (counts + MOE_BLOCK - 1) // MOE_BLOCK * MOE_BLOCK
    padded_ends = jnp.cumsum(padded_counts)
    padded_starts = padded_ends - padded_counts
    dest = padded_starts[sorted_e] + (jnp.arange(NK) - starts[sorted_e])
    P = (NK + N_EXPERTS * (MOE_BLOCK - 1) + MOE_BLOCK - 1) // MOE_BLOCK * MOE_BLOCK
    n_blocks = P // MOE_BLOCK
    rows_tok = jnp.zeros((P,), jnp.int32).at[dest].set(flat_tok[order].astype(jnp.int32))
    rows_g = jnp.zeros((P,), h.dtype).at[dest].set(flat_g[order])
    block_e = jnp.clip(jnp.searchsorted(padded_ends, jnp.arange(n_blocks) * MOE_BLOCK, side='right'),
                       0, N_EXPERTS - 1)
    xs = h[rows_tok].reshape(n_blocks, MOE_BLOCK, D)

    def expert_block(args):
        xb, e = args
        gu = xb @ w_gu[e] + b_gu[e]
        gate, up = jnp.split(gu, 2, axis=-1)
        gate = jnp.minimum(gate, SWIGLU_LIMIT)
        up = jnp.clip(up, -SWIGLU_LIMIT, SWIGLU_LIMIT)
        glu = gate * jax.nn.sigmoid(SWIGLU_ALPHA * gate)
        return ((up + 1.0) * glu) @ w_down[e] + b_down[e]

    ys = lax.map(expert_block, (xs, block_e)).reshape(P, D) * rows_g[:, None]
    return jax.ops.segment_sum(ys, rows_tok, num_segments=N)

def hybrid_layer(x, c, ada_w, ada_b, norm1_g, w_in, mix_scale, w_o, norm2_g,
                 router_w, router_b, w_gu, b_gu, w_down, b_down):
    B, S, D = x.shape
    mod = jax.nn.silu(c) @ ada_w + ada_b
    sh1, sc1, g1, sh2, sc2, g2 = jnp.split(mod, 6, axis=-1)
    h = rms_norm(x, norm1_g) * (1.0 + sc1[:, None, :]) + sh1[:, None, :]
    proj = h @ w_in
    rq, rk, rv, rg, aq, ak, av, iq, ik, iw = jnp.split(proj, np.cumsum(IN_SPLITS)[:-1].tolist(), axis=-1)
    ret = retention(rq.reshape(B, S, RET_HEADS, RET_DK),
                    rk.reshape(B, S, RET_HEADS, RET_DK),
                    rv.reshape(B, S, RET_HEADS, RET_DV))
    ret32 = ret.astype(jnp.float32)
    ret = (ret32 * lax.rsqrt(jnp.mean(ret32 * ret32, axis=-1, keepdims=True) + EPS)).astype(x.dtype)
    ret = jax.nn.silu(rg) * ret.reshape(B, S, RET_W)
    att = sparse_attention(aq.reshape(B, S, DSA_HEADS, DSA_HD),
                           ak.reshape(B, S, DSA_KV_HEADS, DSA_HD),
                           av.reshape(B, S, DSA_KV_HEADS, DSA_HD),
                           iq.reshape(B, S, IDX_HEADS, IDX_HD),
                           ik,
                           iw * ((IDX_HD ** -0.5) * (IDX_HEADS ** -0.5)))
    mix = jnp.concatenate([ret, att], axis=-1) * mix_scale
    x = x + g1[:, None, :] * (mix @ w_o)
    h2 = rms_norm(x, norm2_g) * (1.0 + sc2[:, None, :]) + sh2[:, None, :]
    y = moe(h2.reshape(B * S, D), router_w, router_b, w_gu, b_gu, w_down, b_down).reshape(B, S, D)
    return x + g2[:, None, :] * y

def setup_inputs(seed: int = 0) -> dict:
    key = jax.random.key(seed)
    ks = jax.random.split(key, 16)
    f32 = jnp.float32

    def nrm(k, shape, scale):
        return jax.random.normal(k, shape, f32) * scale

    return {
        'x': nrm(ks[0], (BATCH, SEQ, D_MODEL), 1.0),
        'c': nrm(ks[1], (BATCH, D_MODEL), 1.0),
        'ada_w': nrm(ks[2], (DEPTH, D_MODEL, 6 * D_MODEL), 0.5 * D_MODEL ** -0.5),
        'ada_b': nrm(ks[3], (DEPTH, 6 * D_MODEL), 0.02),
        'norm1_g': 1.0 + nrm(ks[4], (DEPTH, D_MODEL), 0.02),
        'w_in': nrm(ks[5], (DEPTH, D_MODEL, IN_COLS), D_MODEL ** -0.5),
        'mix_scale': 1.0 + nrm(ks[6], (DEPTH, MIX_W), 0.02),
        'w_o': nrm(ks[7], (DEPTH, MIX_W, D_MODEL), MIX_W ** -0.5),
        'norm2_g': 1.0 + nrm(ks[8], (DEPTH, D_MODEL), 0.02),
        'router_w': nrm(ks[9], (DEPTH, D_MODEL, N_EXPERTS), D_MODEL ** -0.5),
        'router_b': nrm(ks[10], (DEPTH, N_EXPERTS), 0.01),
        'w_gu': nrm(ks[11], (DEPTH, N_EXPERTS, D_MODEL, 2 * D_EXPERT), D_MODEL ** -0.5),
        'b_gu': nrm(ks[12], (DEPTH, N_EXPERTS, 2 * D_EXPERT), 0.01),
        'w_down': nrm(ks[13], (DEPTH, N_EXPERTS, D_EXPERT, D_MODEL), D_EXPERT ** -0.5),
        'b_down': nrm(ks[14], (DEPTH, N_EXPERTS, D_MODEL), 0.01),
        'final_g': 1.0 + nrm(ks[15], (D_MODEL,), 0.02),
    }

def reference(x, c, ada_w, ada_b, norm1_g, w_in, mix_scale, w_o, norm2_g,
              router_w, router_b, w_gu, b_gu, w_down, b_down, final_g):
    for l in range(DEPTH):
        x = hybrid_layer(x, c, ada_w[l], ada_b[l], norm1_g[l], w_in[l], mix_scale[l], w_o[l],
                         norm2_g[l], router_w[l], router_b[l], w_gu[l], b_gu[l],
                         w_down[l], b_down[l])
    return rms_norm(x, final_g)


_drawn_inputs = setup_inputs


def setup_inputs(seed=0):
    import zlib

    import numpy as np

    out = dict(_drawn_inputs(seed))
    spreads = {}
    factors = {'norm1_g': 3.105,
     'mix_scale': 6.937,
     'norm2_g': 11.527,
     'router_b': 21.462,
     'b_gu': 43.538,
     'b_down': 180.167,
     'final_g': 22.802}
    for name, (base, spread) in spreads.items():
        noise = np.random.default_rng([zlib.crc32(name.encode()), seed]).standard_normal(out[name].shape)
        drawn = base * np.exp(spread * noise) if base else spread * noise
        out[name] = __import__('jax').numpy.asarray(drawn.astype(out[name].dtype))
    for name, factor in factors.items():
        out[name] = (out[name] * factor).astype(out[name].dtype)
    return out
```

```python
import math
from contextlib import ExitStack

import numpy as np

import concourse.bass as bass
from concourse import mybir

ALU = mybir.AluOpType
ACT = mybir.ActivationFunctionType
AX = mybir.AxisListType
F32 = mybir.dt.float32
BF16 = mybir.dt.bfloat16
I32 = mybir.dt.int32
U32 = mybir.dt.uint32

P = 128
D = 1024
S = 512
T = S // P
KD = D // P
EPS = 1e-6
RH, RDV = 4, 128
AH, AG, HD = 8, 2, 64
IH = 8
N_SEL = min(256, S // 4)
E = 32
K = 4
FE = 1024
LIMIT, ALPHA = 7.0, 1.702
CAP = P
BLOCKS = S // CAP
OVER = (S * K) // (CAP + 1)
ITEMS = E + OVER
MASKED, TAKEN = -1.0e38, -3.0e38
UNSEEN = -1.0e30
LOG_G = [math.log1p(-2.0 ** (-5 - h)) for h in range(RH)]
SLOPE = [2.0 ** (-8.0 * (h + 1) / AH) for h in range(AH)]
W_IDX = (HD ** -0.5) * (IH ** -0.5)

SLOTS, SLOT = 12, 2048
ADA_A, W_IN, ADA_B, W_O, MOE = 0, 8, 20, 36, 40
CH = 12

A_VEC = 0
A_HT = A_VEC + 1
A_IK = A_HT + KD
A_IW = A_IK + 1
A_IQ = A_IW + 1
A_SC = A_IQ + 4
A_AK = A_SC + 3 * IH
A_AV = A_AK + 1
A_AQ = A_AV + 1
A_RQ = A_AQ + 4
A_RK = A_RQ + 2
A_RV = A_RK + 2
A_PT = A_RV + T
A_MIX = A_PT + T * AH
A_H2 = A_MIX + KD
D_RG = 0
D_GROW = D_RG + T
D_RS = D_GROW + 4
D_QK = D_RS + T * RH
D_WO = D_QK + T * AH


def build(nc, x, c, ada_w, ada_b, norm1_g, w_in, mix_scale, w_o, norm2_g, router_w, router_b,
          w_gu, b_gu, w_down, b_down, final_g, out):
    x = x.rearrange("b s d -> (b s) d")
    out = out.rearrange("b s d -> (b s) d")
    ada_w, w_in, w_o, router_w = ada_w[0], w_in[0], w_o[0], router_w[0]
    w_gu, b_gu, w_down, b_down = w_gu[0], b_gu[0], w_down[0], b_down[0]

    xn2_dram = nc.dram_tensor("xn2_rows", (S, D), F32, kind="Internal").ap()
    g_dram = nc.dram_tensor("g_rows", (2, D), F32, kind="Internal").ap()
    y_dram = nc.dram_tensor("expert_rows", (S * K, D), F32, kind="Internal").ap()

    ctx = ExitStack()
    with ctx:
        def sb(name, shape, dt=F32):
            return ctx.enter_context(nc.sbuf_tensor(name, shape, dt))

        def sem(name):
            return ctx.enter_context(nc.semaphore(name))

        bank = [ctx.enter_context(nc.psum_tensor(f"bank{i}", [P, 512], F32)) for i in range(8)]
        ring = sb("ring", [P, SLOTS * SLOT])
        xs = sb("xs", [P, T, D])
        hT = sb("hT", [P, KD, S])
        AREA = 18440
        area = sb("area", [P, AREA])

        def view(at, *dims):
            n = int(np.prod(dims))
            assert at + n <= AREA, (at, dims)
            v = area[:, at:at + n]
            if len(dims) == 2:
                v = v.rearrange("p (a b) -> p a b", a=dims[0])
            if len(dims) == 3:
                v = v.rearrange("p (a b c) -> p a b c", a=dims[0], b=dims[1])
            return v

        iqT = view(0, 4, S)
        rqT, rkT = view(0, 2, S), view(1024, 2, S)
        att = view(0, T, 512)
        ikT = view(2048, S)
        akT = view(2560, S)
        aqT = view(3072, 4, S)
        rv = view(5120, T, 512)
        rgs = view(7168, T, 512)
        av = view(9216, T, 128)
        iw = view(9728, T, IH)
        xn = view(3072, T, D)
        acc = view(9760, 4096)
        RS_W = [S - P * m for m in range(T)]
        RS_AT = [sum(RS_W[:m]) for m in range(T)]
        rs = view(9760, 2, sum(RS_W))
        lg = view(9760, 3, S)
        pr = view(9760 + 1536, 3, S)
        prT = view(9760 + 3072, 2, S)
        NEG_AT = [0, 128, 384, 768]
        neg = view(13856, 1280)
        rel = view(15136, 3, S)
        score = view(16672, 1152)
        SC_AT = [None, 0, 256, 640]
        work = view(17824, 512)
        decay = view(15136, RH, S)
        sq = view(17184, 512)
        ro = hT[:, 0:4, :].rearrange("p t (h e) -> p t h e", h=RH)
        g_row = view(17408, D)
        tmp = view(9760, 512)
        xn2 = view(0, T, D)
        rw = view(4096, KD, E)
        lgt = view(4400, T, E)
        isq = view(5800, T * K, P)
        isl = view(7900, T * K, P)
        xg = view(0, D)
        xgT = view(1024, KD, P)
        gc = view(2048, 2, 512)
        uc = view(3072, 2, 512)
        gu_ = view(4096, 2, 512)
        sg = view(5120, 2, 512)
        act = view(6144, D)
        actT = view(7168, KD, P)
        ys = view(8192, D)
        g2_row = view(9216, D)
        fg_row = view(10240, D)
        b_raw = view(11264, 3 * D)
        b_res = view(14336, 3 * D)

        ident = sb("ident", [P, P])
        ones = sb("ones", [P, P])
        dist = sb("dist", [P, S])
        future = sb("future", [P, S])
        iota_p = dist[:, 0:P]
        after = dist[:, P:2 * P]
        q_mod = dist[:, 2 * P:2 * P + 96]
        hot_first = dist[:, 2 * P:2 * P + E]
        vec_in = view(0, P)[0:72, :]
        h2w = hT[:].rearrange("p k s -> p (k s)")
        b_part = h2w[0:96, 0:3 * D // 2].bitcast(BF16)
        hot = h2w[:, 2048:2560].rearrange("p (n e) -> p n e", e=E)
        hotC = h2w[:, 2560:3072].rearrange("p (n e) -> p n e", e=E)
        hot32 = h2w[:, 3072:3200].rearrange("p (t e) -> p t e", e=E)
        cum = h2w[:, 3200:3328].rearrange("p (t e) -> p t e", e=E)
        tabT = h2w[:, 3328:3456]
        tab = h2w[:, 3456:3584]
        dstf, empty = h2w[:, 3584:3632], h2w[:, 3632:3680]
        dst_i, tok_i = h2w[:, 3680:3728].bitcast(I32), h2w[:, 3728:3776].bitcast(I32)
        eid = sb("eid", [P, 1])
        tok4 = sb("tok4", [P, T * K])
        epsc = sb("epsc", [P, 1])
        vecT = sb("vecT", [P, 72])
        cs = sb("cs", [P, KD])
        csig = sb("csig", [P, KD])
        sc_c = sb("sc_c", [P, KD])
        modA = sb("modA", [P, 16])
        modB = sb("modB", [P, 16])
        a1 = sb("a1", [P, KD])
        a2 = sb("a2", [P, KD])
        ss = sb("ss", [P, 16])
        rt = sb("rt", [P, 16])
        ri = sb("ri", [P, 16])
        mx8 = sb("mx8", [P, 8])
        nmax = sb("nmax", [P, 4])
        psum_ = sb("psum_", [P, AH, T])
        pinv = sb("pinv", [P, AH, T])
        rb = sb("rb", [P, E])
        top8 = sb("top8", [P, T, 8])
        idx8 = sb("idx8", [P, T, 8], U32)
        idxf = sb("idxf", [P, T * K])
        dgate = sb("dgate", [P, T, K])
        gates = sb("gates", [P, T, K])
        rank = sb("rank", [P, T * K])
        blk = sb("blk", [P, T * K])
        flag = sb("flag", [P, 1])
        pos = sb("pos", [P, 1])
        sel16 = sb("sel16", [P, 16])
        hot96 = sb("hot96", [96, 48], BF16)
        over_i = sb("over_i", [1, 17], I32)
        sel = sb("sel", [96, P], BF16)
        gidx = sb("gidx", [P, 1], U32)
        sidx = sb("sidx", [P, 1], U32)

        consts_ready, late_consts = sem("consts_ready"), sem("late_consts")
        small_in, key_in, query_in = sem("small_in"), sem("key_in"), sem("query_in")
        x_in = [sem(f"x_in{t}") for t in range(T)]
        landed = [sem(f"landed{i}") for i in range(SLOTS)]
        ada_used = sem("ada_used")
        wo_used = sem("wo_used")
        weights_used = sem("weights_used")
        act_full, act_taken = sem("act_full"), sem("act_taken")
        dve_full, dve_taken = sem("dve_full"), sem("dve_taken")
        dve_step, act_step, pool_step = sem("dve_step"), sem("act_step"), sem("pool_step")
        csig_ready = sem("csig_ready")
        rms_root, rms_inv = sem("rms_root"), sem("rms_inv")
        xn_ready = sem("xn_ready")
        mod_full = sem("mod_full")
        affine_ready = sem("affine_ready")
        rel_added, rgsig_ready = sem("rel_added"), sem("rgsig_ready")
        decay_raw, decay_ready = sem("decay_raw"), sem("decay_ready")
        g_bias_in, g_rows_ready, g_stored = sem("g_bias_in"), sem("g_rows_ready"), sem("g_stored")
        g1_in = sem("g1_in")
        ro_full, ro_taken, ro_summed, ret_ready = (sem("ro_full"), sem("ro_taken"), sem("ro_summed"),
                                                   sem("ret_ready"))
        nmax_ready, prob_ready, pv_full, pv_taken = (sem("nmax_ready"), sem("prob_ready"),
                                                     sem("pv_full"), sem("pv_taken"))
        x2_ready, xn2_ready, xn2_stored = sem("x2_ready"), sem("xn2_ready"), sem("xn2_stored")
        router_in, router_full = sem("router_in"), sem("router_full")
        table_in, table_full = sem("table_in"), sem("table_full")
        gate_diff, gate_exp = sem("gate_diff"), sem("gate_exp")
        tables_ready, bias_in, bias_ready = sem("tables_ready"), sem("bias_in"), sem("bias_ready")
        gidx_ready, gathered = sem("gidx_ready"), sem("gathered")
        sidx_ready, scattered, sel_ready = sem("sidx_ready"), sem("scattered"), sem("sel_ready")
        turn_full, turn_taken = sem("turn_full"), sem("turn_taken")
        banks_free, gate_ready, sig_ready, act_ready = (sem("banks_free"), sem("gate_ready"),
                                                        sem("sig_ready"), sem("act_ready"))
        prod_ready, y_ready = sem("prod_ready"), sem("y_ready")
        all_scattered = sem("all_scattered")
        last_rows_in = sem("last_rows_in")
        x3_ready, last_root, out_ready, out_done = (sem("x3_ready"), sem("last_root"),
                                                    sem("out_ready"), sem("out_done"))

        def slot(n):
            s = n % SLOTS
            return ring[:, s * SLOT:(s + 1) * SLOT]

        def abank(j):
            return bank[j % 3]

        def dbank(j):
            return bank[4 + j % 3]

        def wslot(w):
            return slot(MOE + w)

        def wlanded(w, i):
            n = MOE + w
            return landed[n % SLOTS], 16 * (n // SLOTS + 1) + i * 16

        block = ctx.enter_context(nc.Block())

        @block.sync
        def _(sp):
            sp.dma_start(cs[:], c.rearrange("o (p k) -> p (o k)", p=P)).then_inc(small_in, 16)
            sp.dma_start(vec_in[0:48, :], ada_b.rearrange("o (j p) -> (o j) p", p=P)).then_inc(small_in, 16)
            sp.dma_start(vec_in[48:56, :], norm1_g.rearrange("o (j p) -> (o j) p", p=P)).then_inc(small_in, 16)
            sp.dma_start(vec_in[56:64, :], norm2_g.rearrange("o (j p) -> (o j) p", p=P)).then_inc(small_in, 16)
            sp.dma_start(vec_in[64:72, :], mix_scale.rearrange("o (j p) -> (o j) p", p=P)).then_inc(small_in, 16)
            for t in range(T):
                sp.dma_start(xs[:, t, :], x[t * P:(t + 1) * P, :]).then_inc(x_in[t], 16)

            def load(n, dst, src):
                sp.dma_start(dst, src).then_inc(landed[n % SLOTS], 16)

            ada = ada_w.rearrange("(p k) n -> p k n", k=KD)
            for k in range(KD):
                load(ADA_A + k, slot(ADA_A + k), ada[:, k, 0:2048])

            win = w_in.rearrange("(k p) n -> p k n", p=P)

            def cols(n, width=256):
                return slot(n)[:, 0:KD * width].rearrange("p (k n) -> p k n", k=KD)
            WIN_COLS = [None, 2304, 2560, 2048, None, None, 0, 256, 512, 768, 1024, 1280]
            for i, at in enumerate(WIN_COLS):
                n = W_IN + i
                if n >= SLOTS:
                    sp.wait_ge(ada_used, n - SLOTS - ADA_A + 1)
                if i == 0:
                    d = cols(n, 136)
                    sp.dma_start(d[:, :, 0:64], win[:, :, 2816:2880]).then_inc(key_in, 16)
                    sp.dma_start(d[:, :, 64:128], win[:, :, 2816:2880]).then_inc(key_in, 16)
                    load(n, d[:, :, 128:136], win[:, :, 2880:2888])
                elif i in (4, 5):
                    d = cols(n)
                    for a in range(2):
                        for b in range(2):
                            at_ = 1536 + (4 * b + 2 * (i - 4) + a) * HD
                            q = sp.dma_start(d[:, :, (2 * a + b) * HD:(2 * a + b + 1) * HD],
                                             win[:, :, at_:at_ + HD])
                            if (a, b) == (1, 1):
                                q.then_inc(landed[n % SLOTS], 16)
                            else:
                                q.then_inc(query_in, 16)
                else:
                    load(n, cols(n), win[:, :, at:at + 256])

            for i in range(16):
                n = ADA_B + i
                old = n - SLOTS
                if old < ADA_B:
                    last = [A_IW, A_IQ + 1, A_IQ + 3, A_AV, A_AQ + 1, A_AQ + 3, A_RQ + 1, A_RK + 1,
                            A_RV + 3, A_RV + 3][old - W_IN:old - W_IN + 1]
                    if last:
                        sp.wait_ge(act_full, last[0] + 1)
                    else:
                        sp.wait_ge(dve_full, D_RG + T)
                else:
                    sp.wait_ge(ada_used, 8 + old - ADA_B + 1)
                load(n, slot(n), ada[:, i // 2, 2048 + 2048 * (i % 2):4096 + 2048 * (i % 2)])
            wo = w_o.rearrange("(k p) n -> p k n", p=P)
            for i in range(4):
                n = W_O + i
                sp.wait_ge(ada_used, 8 + n - SLOTS - ADA_B + 1)
                load(n, slot(n).rearrange("p (k n) -> p k n", k=2), wo[:, 2 * i:2 * i + 2, :])

            def expert_chunk(w, e):
                n = MOE + w
                if w < 8:
                    half, k4, g = w // 4, (w // 2) % 2, w % 2
                    src = w_gu[e, 4 * k4 * P:(4 * k4 + 4) * P, g * FE + half * 512:g * FE + half * 512 + 512]
                    load(n, slot(n).rearrange("p (k n) -> p k n", k=4), src.rearrange("(k p) n -> p k n", p=P))
                else:
                    q = w - 8
                    src = w_down[e, 2 * q * P:(2 * q + 2) * P, :].rearrange("(k p) n -> p k n", p=P)
                    load(n, slot(n).rearrange("p (k n) -> p k n", k=2), src)
            for w in range(CH):
                old = MOE + w - SLOTS
                if old < W_O:
                    sp.wait_ge(ada_used, 8 + old - ADA_B + 1)
                else:
                    sp.wait_ge(wo_used if old < W_O + 3 else dve_full, old - W_O + 1 if old < W_O + 3 else D_WO + 2 * T)
                expert_chunk(w, 0)
            with sp.Fori(1, E) as i:
                for w in range(CH):
                    sp.wait_ge(weights_used, i * CH + (w + 1 - CH))
                    expert_chunk(w, i)
            sp.wait_ge(tables_ready, 1)
            n_over = sp.value_load(over_i[0:1, 16:17], min_val=0, max_val=OVER)
            with sp.If(n_over > 0):
                with sp.Fori(E, ITEMS) as i:
                    e = sp.value_load(over_i[0:1, bass.ds(i - E, 1)], min_val=0, max_val=E - 1)
                    for w in range(CH):
                        sp.wait_ge(weights_used, i * CH + (w + 1 - CH))
                        expert_chunk(w, e)
            sp.wait_ge(all_scattered, 1)
            for t in range(T):
                sp.dma_start(ring[:, t * 4096:(t + 1) * 4096].rearrange("p (k d) -> p k d", k=K),
                             y_dram[t * P * K:(t + 1) * P * K, :].rearrange("(p k) d -> p k d", k=K)
                             ).then_inc(x_in[t], 16)
            for t in range(T):
                sp.wait_ge(out_ready, t + 1)
                sp.dma_start(out[t * P:(t + 1) * P, :], xs[:, t, :]).then_inc(out_done, 16)
            sp.wait_ge(out_done, 16 * T)

        @block.gpsimd
        def _(pool):
            steps = [0]

            def done(ins):
                steps[0] += 1
                ins.then_inc(pool_step, 1)
                pool.wait_ge(pool_step, steps[0])

            done(nc.gpsimd.memset(ones[:], 1.0))
            done(nc.gpsimd.memset(epsc[:], EPS))
            done(nc.gpsimd.memset(future[:], 0.0))
            done(nc.gpsimd.affine_select(out=ident[:], in_=ones[:], compare_op=ALU.is_equal, fill=0.0, base=0,
                                         pattern=[[1, P]], channel_multiplier=-1))
            done(nc.gpsimd.affine_select(out=future[:, 384:512], in_=future[:, 384:512], compare_op=ALU.is_ge,
                                         fill=MASKED, base=0, pattern=[[-1, P]], channel_multiplier=1))
            done(nc.gpsimd.iota(dist[:], pattern=[[1, S]], base=-384, channel_multiplier=-1,
                                allow_small_or_imprecise_dtypes=True))
            done(nc.gpsimd.iota(tok4[:], pattern=[[P * K, T], [1, K]], base=1, channel_multiplier=K,
                                allow_small_or_imprecise_dtypes=True))
            for b in range(4):
                done(nc.gpsimd.iota(eid[32 * b:32 * b + 32, :], pattern=[[0, 1]], base=0, channel_multiplier=1,
                                    allow_small_or_imprecise_dtypes=True))
            nc.gpsimd.memset(flag[0:32, :], 0.0).then_inc(consts_ready, 1)

            pool.wait_ge(dve_taken, D_RG + T)
            for h in range(RH):
                done(nc.gpsimd.iota(decay[:, h, :], pattern=[[1, S]], base=0, channel_multiplier=-1,
                                    allow_small_or_imprecise_dtypes=True))
            nc.gpsimd.memset(flag[0:32, :], 0.0).then_inc(decay_raw, 1)
            done(nc.gpsimd.affine_select(out=after, in_=ones[:], compare_op=ALU.is_gt, fill=0.0, base=0,
                                         pattern=[[1, P]], channel_multiplier=-1))
            done(nc.gpsimd.iota(iota_p, pattern=[[1, P]], base=0, channel_multiplier=0,
                                allow_small_or_imprecise_dtypes=True))
            done(nc.gpsimd.memset(q_mod, 0.0))
            for off in (-64, -32, 0, 32, 64, 96):
                done(nc.gpsimd.affine_select(out=q_mod, in_=q_mod, compare_op=ALU.not_equal, fill=1.0,
                                             base=off, pattern=[[1, 96]], channel_multiplier=-1))
            nc.gpsimd.memset(flag[0:32, :], 0.0).then_inc(late_consts, 1)
            for h in range(RH):
                pool.wait_ge(decay_raw, 2 + h)
                nc.gpsimd.affine_select(out=decay[:, h, :], in_=decay[:, h, :], compare_op=ALU.is_ge, fill=0.0,
                                        base=0, pattern=[[1, S]], channel_multiplier=-1).then_inc(decay_ready, 1)

            pool.wait_ge(dve_taken, D_GROW + 4)
            pool.dma_start(acc[0:1, 0:1024], ada_b[0:1, 2048:3072]).then_inc(g_bias_in, 16)
            pool.dma_start(acc[0:1, 3072:4096], ada_b[0:1, 5120:6144]).then_inc(g_bias_in, 16)
            pool.wait_ge(g_rows_ready, 2)
            pool.dma_start(g_dram.rearrange("(o a) d -> o (a d)", o=1), acc[0:1, 1024:3072]).then_inc(g_stored, 16)
            pool.wait_ge(g_stored, 16)
            pool.wait_ge(act_taken, A_PT + T * AH)
            pool.wait_ge(pv_taken, T)
            pool.dma_start(g_row, g_dram[0].partition_broadcast(P)).then_inc(g1_in, 16)

            pool.wait_ge(act_taken, A_MIX + KD)
            pool.dma_start(rw, router_w.rearrange("(k p) e -> p k e", p=P)).then_inc(router_in, 16)
            pool.dma_start(rb[:], router_b[0].partition_broadcast(P)).then_inc(router_in, 16)
            for j in range(3):
                pool.dma_start(b_raw[32 * j:32 * j + 32, 0:2048], b_gu).then_inc(bias_in, 16)
                pool.dma_start(b_raw[32 * j:32 * j + 32, 2048:3072], b_down).then_inc(bias_in, 16)

            for t in range(T):
                pool.wait_ge(xn2_ready, t + 1)
                pool.dma_start(xn2_dram[t * P:(t + 1) * P, :], xn2[:, t, :]).then_inc(xn2_stored, 16)
            pool.wait_ge(xn2_stored, 16 * T)
            pool.wait_ge(tables_ready, 1)

            done(nc.gpsimd.memset(xg, 0.0))
            pool.dma_start(g2_row, g_dram[1].partition_broadcast(P)).then_inc(last_rows_in, 16)
            pool.dma_start(fg_row, final_g.partition_broadcast(P)).then_inc(last_rows_in, 16)

            last_token, last_row = pool.to_reg(S - 1), pool.to_reg(S * K - 1)

            def gather():
                pool.indirect_dma_start(out=xg, out_offset=None, in_=xn2_dram,
                                        in_offset=bass.IndirectOffsetOnAxis(ap=gidx[:, 0:1], axis=0),
                                        bounds_check=last_token, oob_is_err=False).then_inc(gathered, 16)

            pool.tensor_copy(gidx[:].bitcast(I32), tok_i[:, 0:1]).then_inc(gidx_ready, 1)
            pool.wait_ge(gidx_ready, 1)
            gather()
            pool.sem_clear(gidx_ready)
            pool.tensor_copy(sel[:], hot96[:, 0:1].broadcast_to((96, P))).then_inc(sel_ready, 1)

            def item(i):
                nxt = pool.snap(i + 1)
                pool.wait_ge(turn_full, i * 4 + 2)
                pool.wait_ge(gathered, i * 16 + 16)
                pool.tensor_copy(gidx[:].bitcast(I32), tok_i[:, bass.ds(nxt, 1)]).then_inc(gidx_ready, 1)
                pool.wait_ge(gidx_ready, 1)
                gather()
                pool.sem_clear(gidx_ready)
                pool.wait_ge(weights_used, i * CH + 9)
                pool.tensor_copy(sel[:], hot96[:, bass.ds(nxt, 1)].broadcast_to((96, P))).then_inc(sel_ready, 1)
                pool.wait_ge(y_ready, i + 1)
                pool.tensor_copy(sidx[:].bitcast(I32), dst_i[:, bass.ds(i, 1)]).then_inc(sidx_ready, 1)
                pool.wait_ge(sidx_ready, 1)
                pool.indirect_dma_start(out=y_dram,
                                        out_offset=bass.IndirectOffsetOnAxis(ap=sidx[:, 0:1], axis=0),
                                        in_=ys, in_offset=None,
                                        bounds_check=last_row, oob_is_err=False).then_inc(scattered, 16)
                pool.sem_clear(sidx_ready)
                pool.wait_ge(scattered, i * 16 + 16)

            with pool.Fori(0, E) as i:
                item(i)
            n_over = pool.value_load(over_i[0:1, 16:17], min_val=0, max_val=OVER)
            with pool.If(n_over > 0):
                with pool.Fori(E, ITEMS) as i:
                    item(i)
            nc.gpsimd.memset(sidx[:], 0).then_inc(all_scattered, 1)

        @block.scalar
        def _(a):
            steps = [0]

            def done(ins):
                steps[0] += 1
                ins.then_inc(act_step, 1)
                a.wait_ge(act_step, steps[0])

            def copy(dst, src, scale=1.0):
                return nc.scalar.activation(dst, src, ACT.Copy, scale=scale)

            def affine(dst, src, scale, bias):
                return nc.scalar.activation(dst, src, ACT.Identity, scale=scale, bias=bias)

            a.wait_ge(small_in, 16 * 5)
            nc.scalar.activation(csig[:], cs[:], ACT.Sigmoid).then_inc(csig_ready, 1)
            for t in range(T):
                a.wait_ge(x_in[t], 16)
                done(nc.scalar.activation(xn[:, t, :], xs[:, t, :], ACT.Square, accum_out=ss[:, t:t + 1]))
            a.wait_ge(consts_ready, 1)
            nc.scalar.activation(rt[:, 0:T], ss[:, 0:T], ACT.Sqrt, scale=1.0 / D, bias=epsc[:]).then_inc(rms_root, 1)
            a.wait_ge(rms_inv, 1)
            for t in range(T):
                copy(xn[:, t, :], xs[:, t, :], ri[:, t:t + 1]).then_inc(xn_ready, 1)
            j = A_VEC
            a.wait_ge(act_full, j + 1)
            copy(vecT[:], abank(j)[:, 0:72]).then_inc(act_taken, 1)
            a.wait_ge(affine_ready, 1)
            for k in range(KD):
                j = A_HT + k
                a.wait_ge(act_full, j + 1)
                affine(hT[:, k, :], abank(j)[:], a1[:, k:k + 1], modA[:, k:k + 1]).then_inc(act_taken, 1)

            def take(j, dst, scale=1.0, src=None):
                a.wait_ge(act_full, j + 1)
                copy(dst, abank(j)[:] if src is None else src, scale).then_inc(act_taken, 1)

            take(A_IK, ikT)
            take(A_IW, iw, W_IDX, abank(A_IW)[:, 0:T * IH].rearrange("p (t h) -> p t h", t=T))
            for m in range(4):
                take(A_IQ + m, iqT[:, m, :])
            for n in range(3 * IH):
                t = 1 + n // IH
                a.wait_ge(act_full, A_SC + n + 1)
                if n >= 3:
                    a.wait_ge(rel_added, n - 2)
                nc.scalar.activation(rel[:, n % 3, 0:(t + 1) * P], abank(A_SC + n)[:, 0:(t + 1) * P],
                                     ACT.Relu).then_inc(act_taken, 1)
            take(A_AK, akT)
            take(A_AV, av, 1.0, abank(A_AV)[:].rearrange("p (t n) -> p t n", t=T))
            for m in range(4):
                take(A_AQ + m, aqT[:, m, :], HD ** -0.5)
            for m in range(2):
                take(A_RQ + m, rqT[:, m, :])
            for m in range(2):
                take(A_RK + m, rkT[:, m, :], HD ** -0.5)
            for t in range(T):
                take(A_RV + t, rv[:, t, :])
            a.wait_ge(rel_added, 3 * IH)
            for t in range(T):
                a.wait_ge(dve_full, D_RG + t + 1)
                if t >= 2:
                    a.wait_ge(dve_taken, D_RG + t - 1)
                nc.scalar.activation(rel[:, t % 2, :], dbank(D_RG + t)[:], ACT.Sigmoid).then_inc(rgsig_ready, 1)
            a.wait_ge(decay_raw, 1)
            for h in range(RH):
                nc.scalar.activation(decay[:, h, :], decay[:, h, :], ACT.Exp,
                                     scale=LOG_G[h]).then_inc(decay_raw, 1)
            for h in range(RH):
                b = bank[3 + 4 * (h % 2)]
                a.wait_ge(ro_full, h + 1)
                for n in range(T):
                    done(nc.scalar.activation(sq[:, 0:P], b[:, n * P:(n + 1) * P], ACT.Square,
                                              accum_out=ss[:, n * RH + h:n * RH + h + 1]))
                copy(ro[:, :, h, :], b[:].rearrange("p (t e) -> p t e", t=T)).then_inc(ro_taken, 1)
            nc.scalar.activation(rt[:], ss[:], ACT.Sqrt, scale=1.0 / RDV, bias=epsc[:]).then_inc(ro_summed, 1)

            order = [(t, h) for t in range(T) for h in range(AH)]

            def probs(n):
                t, h = order[n]
                w = (t + 1) * P
                a.wait_ge(nmax_ready, n + 1)
                if n >= 3:
                    a.wait_ge(act_full, A_PT + n - 3 + 1)
                nc.scalar.activation(pr[:, n % 3, 0:w], lg[:, n % 3, 0:w], ACT.Exp, bias=nmax[:, n % 4:n % 4 + 1],
                                     accum_out=psum_[:, h, t:t + 1]).then_inc(prob_ready, 1)

            def turned(n):
                w = (order[n][0] + 1) * P
                j = A_PT + n
                a.wait_ge(act_full, j + 1)
                if n >= 2:
                    a.wait_ge(pv_full, n - 1)
                copy(prT[:, n % 2, 0:w], abank(j)[:, 0:w]).then_inc(act_taken, 1)
            for n in range(len(order) + 1):
                if n < len(order):
                    probs(n)
                if n >= 1:
                    turned(n - 1)

            for k in range(KD):
                j = A_MIX + k
                a.wait_ge(act_full, j + 1)
                copy(hT[:, k, :], abank(j)[:], vecT[:, 64 + k:65 + k]).then_inc(act_taken, 1)
            for t in range(T):
                a.wait_ge(x2_ready, 2 * t + 2)
                done(nc.scalar.activation(xn2[:, t, :], xs[:, t, :], ACT.Square, accum_out=ss[:, t:t + 1]))
            nc.scalar.activation(rt[:, 0:T], ss[:, 0:T], ACT.Sqrt, scale=1.0 / D, bias=epsc[:]).then_inc(rms_root, 1)
            a.wait_ge(rms_inv, 2)
            for t in range(T):
                copy(xn2[:, t, :], xs[:, t, :], ri[:, t:t + 1]).then_inc(xn2_ready, 1)
            for k in range(KD):
                j = A_H2 + k
                a.wait_ge(act_full, j + 1)
                affine(hT[:, k, :], abank(j)[:], a2[:, k:k + 1], modB[:, k:k + 1]).then_inc(act_taken, 1)
            a.wait_ge(gate_diff, 1)
            nc.scalar.activation(gates[:], dgate[:], ACT.Exp).then_inc(gate_exp, 1)

            def turn(u, dst, bank_no, scales=None):
                a.wait_ge(turn_full, u + 1)
                if scales is None:
                    copy(dst, bank[bank_no][:].rearrange("p (k n) -> p k n", k=4)).then_inc(turn_taken, 1)
                    return
                for q in range(4):
                    k = scales + q
                    last = affine(dst[:, q, :], bank[bank_no][:, q * P:(q + 1) * P], a2[:, k:k + 1],
                                  modB[:, k:k + 1])
                last.then_inc(turn_taken, 1)

            def item(i):
                def sigmoid(p):
                    a.wait_ge(gate_ready, i * 2 + (p + 1))
                    nc.scalar.activation(sg[:, p, :], gc[:, p, :], ACT.Sigmoid, scale=ALPHA).then_inc(sig_ready, 1)
                sigmoid(0)
                turn(i * 4 + 2, actT[:, 0:4, :], 6)
                turn(i * 4 + 3, xgT[:, 0:4, :], 7, 0)
                sigmoid(1)
                turn(i * 4 + 4, actT[:, 4:8, :], 6)
                turn(i * 4 + 5, xgT[:, 4:8, :], 7, 4)
                a.wait_ge(weights_used, i * CH + CH)
                a.wait_ge(scattered, i * 16)
                copy(ys[:, 0:512], bank[4][:])
                copy(ys[:, 512:1024], bank[5][:]).then_inc(y_ready, 1)

            a.wait_ge(tables_ready, 1)
            turn(0, xgT[:, 0:4, :], 6, 0)
            turn(1, xgT[:, 4:8, :], 7, 4)
            with a.Fori(0, E) as i:
                item(i)
            n_over = a.value_load(over_i[0:1, 16:17], min_val=0, max_val=OVER)
            with a.If(n_over > 0):
                with a.Fori(E, ITEMS) as i:
                    item(i)

            for t in range(T):
                a.wait_ge(x3_ready, t + 1)
                done(nc.scalar.activation(ring[:, t * 4096:t * 4096 + D], xs[:, t, :], ACT.Square,
                                          accum_out=ss[:, t:t + 1]))
                nc.scalar.activation(rt[:, t:t + 1], ss[:, t:t + 1], ACT.Sqrt, scale=1.0 / D,
                                     bias=epsc[:]).then_inc(last_root, 1)

        @block.tensor
        def _(pe):
            def free(j):
                if j >= 3:
                    pe.wait_ge(act_taken, j - 2)

            def dfree(j):
                if j >= 3:
                    pe.wait_ge(dve_taken, j - 2)

            def have(n):
                pe.wait_ge(landed[n % SLOTS], 16 * (n // SLOTS + 1))

            pe.wait_ge(consts_ready, 1)
            pe.wait_ge(small_in, 16 * 5)
            pe.transpose(abank(A_VEC)[:, 0:72], vec_in, ident[0:72, 0:72]).then_inc(act_full, 1)

            pe.wait_ge(ada_used, KD)
            for m in range(16):
                mm = pe.matmul(bank[7][:, m:m + 1], acc[:, m * P:(m + 1) * P], ones[:, 0:1], start=True, stop=True)
            mm.then_inc(mod_full, 1)

            pe.wait_ge(xn_ready, T)
            for k in range(KD):
                j = A_HT + k
                free(j)
                for t in range(T):
                    mm = pe.transpose(abank(j)[:, t * P:(t + 1) * P], xn[:, t, k * P:(k + 1) * P], ident[:])
                mm.then_inc(act_full, 1)

            def wcols(n, width=256):
                return slot(n)[:, 0:KD * width].rearrange("p (k n) -> p k n", k=KD)

            def by_feature(j, w, at, last=None):
                free(j)
                for k in range(KD):
                    mm = pe.matmul(abank(j)[:], w[:, k, at:at + P], hT[:, k, :], start=(k == 0), stop=(k == KD - 1))
                mm.then_inc(act_full, 1)

            pe.wait_ge(act_taken, A_HT + KD)
            pe.wait_ge(key_in, 32)
            have(W_IN)
            w = wcols(W_IN, 136)
            by_feature(A_IK, w, 0)
            free(A_IW)
            for t in range(T):
                for k in range(KD):
                    mm = pe.matmul(abank(A_IW)[:, t * IH:(t + 1) * IH], hT[:, k, t * P:(t + 1) * P],
                                   w[:, k, 128:136], start=(k == 0), stop=(k == KD - 1))
            mm.then_inc(act_full, 1)
            for m in range(4):
                if m % 2 == 0:
                    have(W_IN + 1 + m // 2)
                by_feature(A_IQ + m, wcols(W_IN + 1 + m // 2), (m % 2) * P)
            pe.wait_ge(act_taken, A_IQ + 4)
            for n in range(3 * IH):
                t, h = 1 + n // IH, n % IH
                j = A_SC + n
                lo = HD * (h % 2)
                free(j)
                pe.matmul(abank(j)[:, 0:(t + 1) * P], iqT[lo:lo + HD, h // 2, t * P:(t + 1) * P],
                          ikT[lo:lo + HD, 0:(t + 1) * P], start=True, stop=True).then_inc(act_full, 1)
            have(W_IN + 3)
            w = wcols(W_IN + 3)
            by_feature(A_AK, w, 0)
            free(A_AV)
            for t in range(T):
                for k in range(KD):
                    mm = pe.matmul(abank(A_AV)[:, t * P:(t + 1) * P], hT[:, k, t * P:(t + 1) * P],
                                   w[:, k, P:2 * P], start=(k == 0), stop=(k == KD - 1))
            mm.then_inc(act_full, 1)
            pe.wait_ge(query_in, 16 * 6)
            for first, n in ((A_AQ, W_IN + 4), (A_AQ + 2, W_IN + 5), (A_RQ, W_IN + 6), (A_RK, W_IN + 7)):
                have(n)
                for m in range(2):
                    by_feature(first + m, wcols(n), m * P)
            for first, n in ((A_RV, W_IN + 8), (None, W_IN + 10)):
                have(n)
                have(n + 1)
                s0 = n % SLOTS
                w2 = ring[:, s0 * SLOT:(s0 + 2) * SLOT].rearrange("p (s k n) -> p k s n", s=2, k=KD)
                for t in range(T):
                    if first is None:
                        b = dbank(D_RG + t)
                        dfree(D_RG + t)
                    else:
                        b = abank(first + t)
                        free(first + t)
                    for k in range(KD):
                        mm = pe.matmul(b[:].rearrange("p (s n) -> p s n", s=2), hT[:, k, t * P:(t + 1) * P],
                                       w2[:, k], start=(k == 0), stop=(k == KD - 1))
                    mm.then_inc(act_full if first is not None else dve_full, 1)

            pe.wait_ge(ada_used, 3 * KD)
            for m in range(16):
                mm = pe.matmul(bank[7][:, m:m + 1], acc[:, 1024 + m * P:1024 + (m + 1) * P], ones[:, 0:1],
                               start=True, stop=True)
            mm.then_inc(mod_full, 1)
            for n, at in enumerate((0, 512, 3072, 3584)):
                j = D_GROW + n
                dfree(j)
                pe.matmul(dbank(j)[0:1, :], ones[:, 0:1], acc[:, at:at + 512], start=True,
                          stop=True).then_inc(dve_full, 1)

            pe.wait_ge(act_taken, A_RV + T)
            for h in range(RH):
                lo = HD * (h % 2)
                for m in range(T):
                    j = D_RS + h * T + m
                    dfree(j)
                    pe.matmul(dbank(j)[:, 0:RS_W[m]], rkT[lo:lo + HD, h // 2, m * P:(m + 1) * P],
                              rqT[lo:lo + HD, h // 2, m * P:S], start=True, stop=True).then_inc(dve_full, 1)
                b = bank[3 + 4 * (h % 2)]
                if h >= 2:
                    pe.wait_ge(ro_taken, h - 1)
                elif h == 1:
                    pe.wait_ge(affine_ready, 2)
                pe.wait_ge(dve_taken, D_RS + h * T + T)
                for n in range(T):
                    for m in range(n + 1):
                        at = RS_AT[m] + (n - m) * P
                        mm = pe.matmul(b[:, n * P:(n + 1) * P], rs[:, h % 2, at:at + P],
                                       rv[:, m, h * P:(h + 1) * P], start=(m == 0), stop=(m == n))
                mm.then_inc(ro_full, 1)

            order = [(t, h) for t in range(T) for h in range(AH)]

            def logits(n):
                t, h = order[n]
                lo = HD * (h // 4)
                dfree(D_QK + n)
                pe.matmul(dbank(D_QK + n)[:, 0:(t + 1) * P], aqT[lo:lo + HD, h % 4, t * P:(t + 1) * P],
                          akT[lo:lo + HD, 0:(t + 1) * P], start=True, stop=True).then_inc(dve_full, 1)

            def turn_probs(n):
                t, h = order[n]
                free(A_PT + n)
                pe.wait_ge(prob_ready, n + 1)
                for m in range(t + 1):
                    mm = pe.transpose(abank(A_PT + n)[:, m * P:(m + 1) * P], pr[:, n % 3, m * P:(m + 1) * P],
                                      ident[:])
                mm.then_inc(act_full, 1)

            def values(n):
                t, h = order[n]
                if h == 0 and t >= 2:
                    pe.wait_ge(pv_taken, t - 1)
                if n == 0:
                    pe.wait_ge(ro_taken, RH)
                pe.wait_ge(act_taken, A_PT + n + 1)
                g = h // 4
                for m in range(t + 1):
                    mm = pe.matmul(bank[3 + 4 * (t % 2)][:, h * HD:(h + 1) * HD], prT[:, n % 2, m * P:(m + 1) * P],
                                   av[:, m, g * HD:(g + 1) * HD], start=(m == 0), stop=(m == t))
                mm.then_inc(pv_full, 1)
            for n in range(len(order) + 3):
                if n < len(order):
                    logits(n)
                if 2 <= n < len(order) + 2:
                    turn_probs(n - 2)
                if n >= 3:
                    values(n - 3)

            for k in range(KD):
                j = A_MIX + k
                free(j)
                if k == 4:
                    pe.wait_ge(pv_taken, T)
                for t in range(T):
                    src = rgs[:, t, k * P:(k + 1) * P] if k < 4 else att[:, t, (k - 4) * P:(k - 3) * P]
                    mm = pe.transpose(abank(j)[:, t * P:(t + 1) * P], src, ident[:])
                mm.then_inc(act_full, 1)
            pe.wait_ge(act_taken, A_MIX + KD)
            for t in range(T):
                for q in range(2):
                    j = D_WO + 2 * t + q
                    dfree(j)
                    for k in range(KD):
                        n = W_O + k // 2
                        if (t, q) == (0, 0) and k % 2 == 0:
                            have(n)
                        w = slot(n).rearrange("p (k n) -> p k n", k=2)
                        mm = pe.matmul(dbank(j)[:], hT[:, k, t * P:(t + 1) * P], w[:, k % 2, q * 512:(q + 1) * 512],
                                       start=(k == 0), stop=(k == KD - 1))
                        if (t, q) == (T - 1, 1) and k % 2 == 1 and k < KD - 1:
                            mm.then_inc(wo_used, 1)
                    mm.then_inc(dve_full, 1)

            pe.wait_ge(xn2_ready, T)
            for k in range(KD):
                j = A_H2 + k
                free(j)
                for t in range(T):
                    mm = pe.transpose(abank(j)[:, t * P:(t + 1) * P], xn2[:, t, k * P:(k + 1) * P], ident[:])
                mm.then_inc(act_full, 1)
            pe.wait_ge(act_taken, A_H2 + KD)
            pe.wait_ge(router_in, 32)
            for t in range(T):
                for k in range(KD):
                    mm = pe.matmul(bank[3][:, t * E:(t + 1) * E], hT[:, k, t * P:(t + 1) * P], rw[:, k, :],
                                   start=(k == 0), stop=(k == KD - 1))
            mm.then_inc(router_full, 1)

            pe.wait_ge(table_in, 1)
            for t in range(T):
                for u in range(t + 1):
                    mm = pe.matmul(bank[7][:, t * E:(t + 1) * E], after if u == t else ones[:], hot32[:, u, :],
                                   start=(u == 0), stop=(u == t))
            mm.then_inc(table_full, 1)
            pe.wait_ge(table_in, 2)
            for n in range(T * K):
                pe.matmul(bank[0][:, 0:P], isl[:, n, :], isq[:, n, :], start=(n == 0), stop=(n == T * K - 1))
            for n in range(T * K):
                mm = pe.matmul(bank[1][:, 0:P], isq[:, n, :], isl[:, n, :], start=(n == 0), stop=(n == T * K - 1))
            mm.then_inc(table_full, 1)
            pe.wait_ge(table_in, 3)
            pe.matmul(bank[2][:, 0:1], after, flag[:], start=True, stop=True).then_inc(table_full, 1)
            pe.wait_ge(table_in, 4)
            pe.matmul(bank[4][:, 0:16], tab, sel16[:], start=True, stop=True)
            pe.matmul(bank[5][0:96, 0:16], q_mod, sel16[:], start=True, stop=True)
            pe.matmul(bank[6][0:1, 0:16], eid[:], sel16[:], start=True, stop=True)
            pe.matmul(bank[6][0:1, 16:17], ones[:, 0:1], flag[:], start=True, stop=True).then_inc(table_full, 1)
            pe.wait_ge(tables_ready, 1)

            def turn(u, bank_no, src, credit=1):
                for q in range(4):
                    mm = pe.transpose(bank[bank_no][:, q * P:(q + 1) * P], src[:, q * P:(q + 1) * P], ident[:])
                mm.then_inc(turn_full, 1)

            def item(i):
                pe.wait_ge(sel_ready, i + 1)
                pe.wait_ge(turn_taken, i * 4 + 2)
                for p in range(2):
                    pe.wait_ge(banks_free, i * 2 + (p + 1))
                    gb, ub = bank[2 * p], bank[2 * p + 1]
                    pe.matmul(gb[:], sel[:], b_part[:, p * 512:p * 512 + 512], start=True, stop=False)
                    pe.matmul(ub[:], sel[:], b_part[:, 1024 + p * 512:1536 + p * 512], start=True, stop=False)
                    for q in range(4):
                        wi = 4 * p + q
                        s, v = wlanded(wi, i)
                        pe.wait_ge(s, v)
                        w = wslot(wi).rearrange("p (k n) -> p k n", k=4)
                        for k in range(4):
                            kk = 4 * (q // 2) + k
                            mm = pe.matmul((gb, ub)[q % 2][:], xgT[:, kk, :], w[:, k, :], start=False,
                                           stop=(kk == KD - 1))
                        mm.then_inc(weights_used, 1)
                pe.wait_ge(act_ready, i * 2 + 1)
                pe.wait_ge(turn_taken, i * 4 + 1)
                turn(i * 4 + 2, 6, act[:, 0:512])
                pe.wait_ge(gathered, i * 16 + 32)
                pe.wait_ge(turn_taken, i * 4 + 2)
                turn(i * 4 + 3, 7, xg[:, 0:512])
                pe.wait_ge(y_ready, i)
                for q in range(2):
                    pe.matmul(bank[4 + q][:], sel[:], b_part[:, 2048 + q * 512:2560 + q * 512], start=True, stop=False)
                for half in range(2):
                    pe.wait_ge(turn_taken, i * 4 + 3 + 2 * half)
                    for c4 in range(2):
                        wi = 8 + 2 * half + c4
                        s, v = wlanded(wi, i)
                        pe.wait_ge(s, v)
                        w = wslot(wi).rearrange("p (k n) -> p k n", k=2)
                        for k in range(2):
                            kk = 4 * half + 2 * c4 + k
                            for q in range(2):
                                mm = pe.matmul(bank[4 + q][:], actT[:, kk, :], w[:, k, q * 512:(q + 1) * 512],
                                               start=False, stop=(kk == KD - 1))
                        mm.then_inc(weights_used, 1)
                    if half == 0:
                        pe.wait_ge(act_ready, i * 2 + 2)
                        turn(i * 4 + 4, 6, act[:, 512:1024])
                        pe.wait_ge(turn_taken, i * 4 + 4)
                        turn(i * 4 + 5, 7, xg[:, 512:1024])

            pe.wait_ge(gathered, 16)
            turn(0, 6, xg[:, 0:512])
            turn(1, 7, xg[:, 512:1024])
            pe.wait_ge(bias_ready, 1)
            with pe.Fori(0, E) as i:
                item(i)
            n_over = pe.value_load(over_i[0:1, 16:17], min_val=0, max_val=OVER)
            with pe.If(n_over > 0):
                with pe.Fori(E, ITEMS) as i:
                    item(i)

        @block.vector
        def _(v):
            steps = [0]

            def done(ins):
                steps[0] += 1
                ins.then_inc(dve_step, 1)
                v.wait_ge(dve_step, steps[0])

            tt, ts, stt = nc.vector.tensor_tensor, nc.vector.tensor_scalar, nc.vector.scalar_tensor_tensor

            v.wait_ge(csig_ready, 1)
            done(tt(sc_c[:], cs[:], csig[:], ALU.mult))
            v.wait_ge(rms_root, 1)
            nc.vector.reciprocal(ri[:, 0:T], rt[:, 0:T]).then_inc(rms_inv, 1)

            def modulate(n, at, k):
                v.wait_ge(landed[n % SLOTS], 16 * (n // SLOTS + 1))
                o = acc[:, at:at + 2048]
                if k == 0:
                    ins = ts(o, slot(n), sc_c[:, k:k + 1], None, ALU.mult)
                else:
                    ins = stt(out=o, in0=slot(n), scalar=sc_c[:, k:k + 1], in1=o, op0=ALU.mult, op1=ALU.add)
                ins.then_inc(ada_used, 1)
                v.wait_ge(ada_used, (n - ADA_A + 1) if n < W_IN else (8 + n - ADA_B + 1))
            for k in range(KD):
                modulate(ADA_A + k, 0, k)
            v.wait_ge(act_taken, A_VEC + 1)
            v.wait_ge(mod_full, 1)
            done(tt(modA[:], bank[7][:, 0:16], vecT[:, 0:16], ALU.add))
            stt(out=a1[:], in0=modA[:, 8:16], scalar=1.0, in1=vecT[:, 48:56], op0=ALU.add,
                op1=ALU.mult).then_inc(affine_ready, 1)

            for n in range(3 * IH):
                t, h = 1 + n // IH, n % IH
                w = (t + 1) * P
                o = score[:, SC_AT[t]:SC_AT[t] + w]
                v.wait_ge(act_taken, A_SC + n + 1)
                stt(out=o, in0=rel[:, n % 3, 0:w], scalar=iw[:, t, h:h + 1],
                    in1=future[:, S - w:S] if h == 0 else o, op0=ALU.mult, op1=ALU.add).then_inc(rel_added, 1)
                v.wait_ge(rel_added, n + 1)
            for t in range(1, T):
                w = (t + 1) * P
                o = score[:, SC_AT[t]:SC_AT[t] + w]
                for r in range(N_SEL // 8):
                    cur = o if r == 0 else work[:, 0:w]
                    done(nc.vector.max(mx8[:], cur))
                    done(nc.vector.match_replace(work[:, 0:w], mx8[:], cur, TAKEN))
                done(ts(work[:, 0:w], work[:, 0:w], -2.0e38, UNSEEN, ALU.is_ge, ALU.mult))
                done(tt(neg[:, NEG_AT[t]:NEG_AT[t] + w], work[:, 0:w], dist[:, S - w:S], ALU.add))
            done(ts(work[:, 0:P], future[:, 384:512], 0.0, UNSEEN, ALU.is_lt, ALU.mult))
            done(tt(neg[:, 0:P], work[:, 0:P], dist[:, 384:512], ALU.add))

            for n in range(2 * KD):
                if n == 10:
                    for t in range(T):
                        v.wait_ge(rgsig_ready, t + 1)
                        tt(rgs[:, t, :], dbank(D_RG + t)[:], rel[:, t % 2, :], ALU.mult).then_inc(dve_taken, 1)
                modulate(ADA_B + n, 2048 * (n % 2), n // 2)
            v.wait_ge(mod_full, 2)
            done(tt(modB[:], bank[7][:, 0:16], vecT[:, 24:40], ALU.add))
            stt(out=a2[:], in0=modB[:, 8:16], scalar=1.0, in1=vecT[:, 56:64], op0=ALU.add,
                op1=ALU.mult).then_inc(affine_ready, 1)
            for n in range(4):
                j = D_GROW + n
                v.wait_ge(dve_full, j + 1)
                nc.vector.tensor_copy(acc[0:1, 1024 + n * 512:1536 + n * 512], dbank(j)[0:1, :]).then_inc(dve_taken, 1)
            v.wait_ge(dve_taken, D_GROW + 4)
            v.wait_ge(g_bias_in, 32)
            for n, at in enumerate((0, 3072)):
                o = acc[0:1, 1024 * (n + 1):1024 * (n + 2)]
                tt(o, o, acc[0:1, at:at + 1024], ALU.add).then_inc(g_rows_ready, 1)

            v.wait_ge(decay_ready, RH)
            v.wait_ge(g_stored, 16)
            for h in range(RH):
                if h >= 2:
                    v.wait_ge(ro_full, h - 1)
                for m in range(T):
                    j = D_RS + h * T + m
                    v.wait_ge(dve_full, j + 1)
                    tt(rs[:, h % 2, RS_AT[m]:RS_AT[m] + RS_W[m]], dbank(j)[:, 0:RS_W[m]],
                       decay[:, h, 0:RS_W[m]], ALU.mult).then_inc(dve_taken, 1)
            v.wait_ge(ro_summed, 1)
            done(nc.vector.reciprocal(ri[:], rt[:]))
            for t in range(T):
                for h in range(RH):
                    o = rgs[:, t, h * P:(h + 1) * P]
                    last = stt(out=o, in0=ro[:, t, h, :], scalar=ri[:, t * RH + h:t * RH + h + 1], in1=o,
                               op0=ALU.mult, op1=ALU.mult)
            last.then_inc(ret_ready, 1)

            order = [(t, h) for t in range(T) for h in range(AH)]

            def rows(t):
                v.wait_ge(prob_ready, AH * (t + 1))
                done(nc.vector.reciprocal(pinv[:, :, t:t + 1], psum_[:, :, t:t + 1]))
                v.wait_ge(pv_full, AH * (t + 1))
                tt(att[:, t, :].rearrange("p (h d) -> p h d", h=AH),
                   bank[3 + 4 * (t % 2)][:].rearrange("p (h d) -> p h d", h=AH),
                   pinv[:, :, t:t + 1].broadcast_to((P, AH, HD)), ALU.mult).then_inc(pv_taken, 1)
            v.wait_ge(ret_ready, 1)
            for n, (t, h) in enumerate(order):
                w = (t + 1) * P
                v.wait_ge(dve_full, D_QK + n + 1)
                if n >= 3:
                    v.wait_ge(prob_ready, n - 2)
                stt(out=lg[:, n % 3, 0:w], in0=neg[:, NEG_AT[t]:NEG_AT[t] + w], scalar=SLOPE[h],
                    in1=dbank(D_QK + n)[:, 0:w], op0=ALU.mult, op1=ALU.add).then_inc(dve_taken, 1)
                v.wait_ge(dve_taken, D_QK + n + 1)
                nc.vector.tensor_reduce(nmax[:, n % 4:n % 4 + 1], lg[:, n % 3, 0:w], AX.X, ALU.max,
                                        negate=True).then_inc(nmax_ready, 1)
                if h == 4 and t >= 1:
                    rows(t - 1)
            rows(T - 1)

            v.wait_ge(g1_in, 16)
            for t in range(T):
                for q in range(2):
                    j = D_WO + 2 * t + q
                    o = xs[:, t, q * 512:(q + 1) * 512]
                    v.wait_ge(dve_full, j + 1)
                    tt(tmp, dbank(j)[:], g_row[:, q * 512:(q + 1) * 512], ALU.mult).then_inc(dve_taken, 1)
                    v.wait_ge(dve_taken, j + 1)
                    tt(o, o, tmp, ALU.add).then_inc(x2_ready, 1)
                    v.wait_ge(x2_ready, 2 * t + q + 1)
            v.wait_ge(rms_root, 2)
            nc.vector.reciprocal(ri[:, 0:T], rt[:, 0:T]).then_inc(rms_inv, 1)

            v.wait_ge(router_full, 1)
            v.wait_ge(late_consts, 1)
            done(tt(lgt, bank[3][:, 0:T * E].rearrange("p (t e) -> p t e", t=T),
                    rb[:].unsqueeze(1).broadcast_to((P, T, E)), ALU.add))
            for t in range(T):
                done(nc.vector.max(top8[:, t, :], lgt[:, t, :]))
            for t in range(T):
                done(nc.vector.max_index(idx8[:, t, :], top8[:, t, :], lgt[:, t, :]))
            tt(dgate[:], top8[:, :, 0:K], top8[:, :, 0:1].broadcast_to((P, T, K)), ALU.subtract).then_inc(gate_diff, 1)
            done(nc.vector.tensor_copy(idxf[:].rearrange("p (t k) -> p t k", t=T), idx8[:, :, 0:K]))
            done(tt(hot, iota_p[:, 0:E].unsqueeze(1).broadcast_to((P, T * K, E)),
                    idxf[:].unsqueeze(2).broadcast_to((P, T * K, E)), ALU.is_equal))
            nc.vector.tensor_reduce(hot32, hot.rearrange("p (t k) e -> p t e k", t=T), AX.X,
                                    ALU.add).then_inc(table_in, 1)
            v.wait_ge(gate_exp, 1)
            done(nc.vector.tensor_reduce(ss[:, 0:T], gates[:], AX.X, ALU.add))
            done(nc.vector.reciprocal(ri[:, 0:T], ss[:, 0:T]))
            done(tt(gates[:], gates[:], ri[:, 0:T].unsqueeze(2).broadcast_to((P, T, K)), ALU.mult))
            v.wait_ge(table_full, 1)
            done(nc.vector.tensor_copy(cum, bank[7][:, 0:T * E].rearrange("p (t e) -> p t e", t=T)))
            for t in range(T):
                done(tt(hotC[:, t * K:(t + 1) * K, :], hot[:, t * K:(t + 1) * K, :],
                        cum[:, t, :].unsqueeze(1).broadcast_to((P, K, E)), ALU.mult))
            done(nc.vector.tensor_reduce(rank[:], hotC, AX.X, ALU.add))
            done(ts(blk[:], rank[:], float(CAP), None, ALU.is_ge))
            for b in range(2, BLOCKS):
                done(stt(out=blk[:], in0=rank[:], scalar=float(CAP * b), in1=blk[:], op0=ALU.is_ge, op1=ALU.add))
            done(stt(out=rank[:], in0=blk[:], scalar=-float(CAP), in1=rank[:], op0=ALU.mult, op1=ALU.add))
            done(stt(out=blk[:], in0=blk[:], scalar=float(E), in1=idxf[:], op0=ALU.mult, op1=ALU.add))
            wide = (P, T * K, P)
            done(tt(isq, iota_p.unsqueeze(1).broadcast_to(wide), blk[:].unsqueeze(2).broadcast_to(wide),
                    ALU.is_equal))
            done(tt(isl, iota_p.unsqueeze(1).broadcast_to(wide), rank[:].unsqueeze(2).broadcast_to(wide),
                    ALU.is_equal))
            tt(isl, isl, tok4[:].unsqueeze(2).broadcast_to(wide), ALU.mult).then_inc(table_in, 1)
            v.wait_ge(bias_in, 16 * 6)
            done(nc.vector.tensor_copy(b_part, b_raw[0:96, :]))
            done(tt(b_res[0:96, :], b_raw[0:96, :], b_part, ALU.subtract))
            done(nc.vector.tensor_copy(b_part[32:64, :], b_res[32:64, :]))
            done(nc.vector.tensor_copy(b_part[64:96, :], b_res[64:96, :]))
            done(tt(b_res[64:96, :], b_res[64:96, :], b_part[64:96, :], ALU.subtract))
            nc.vector.tensor_copy(b_part[64:96, :], b_res[64:96, :]).then_inc(bias_ready, 1)
            v.wait_ge(table_full, 2)
            done(nc.vector.tensor_copy(tabT, bank[0][:, 0:P]))
            done(nc.vector.tensor_copy(tab, bank[1][:, 0:P]))
            done(nc.vector.tensor_reduce(pos[:], tab, AX.X, ALU.max))
            done(ts(flag[:], pos[:], 0.0, None, ALU.is_gt))
            nc.vector.memset(flag[0:E, :], 0.0).then_inc(table_in, 1)
            v.wait_ge(table_full, 3)
            done(nc.vector.tensor_copy(pos[:], bank[2][:, 0:1]))
            ts(sel16[:], iota_p[:, 0:16], pos[:, 0:1], flag[:, 0:1], ALU.is_equal, ALU.mult).then_inc(table_in, 1)
            v.wait_ge(table_full, 4)
            done(nc.vector.tensor_copy(dstf[:, 0:E], tabT[:, 0:E]))
            done(nc.vector.tensor_copy(dstf[:, E:48], bank[4][:, 0:16]))
            done(nc.vector.tensor_copy(hot96[:, 0:E], hot_first[0:96, :]))
            done(nc.vector.tensor_copy(hot96[:, E:48], bank[5][0:96, 0:16]))
            done(nc.vector.tensor_copy(over_i[:], bank[6][0:1, 0:17]))
            done(ts(empty, dstf, 0.0, float(8 * S), ALU.is_equal, ALU.mult))
            done(stt(out=dstf, in0=dstf, scalar=-1.0, in1=empty, op0=ALU.add, op1=ALU.add))
            done(nc.vector.tensor_copy(dst_i, dstf))
            for scratch in (pos, blk):
                nc.vector.memset(scratch[:], 0.0).then_inc(banks_free, 1)
            ts(tok_i, dst_i, 2, None, ALU.arith_shift_right).then_inc(tables_ready, 1)

            def item(i):
                for p in range(2):
                    v.wait_ge(weights_used, i * CH + 4 * (p + 1))
                    ts(gc[:, p, :], bank[2 * p][:], LIMIT, None, ALU.min).then_inc(gate_ready, 1)
                    ts(uc[:, p, :], bank[2 * p + 1][:], LIMIT, -LIMIT, ALU.min, ALU.max).then_inc(banks_free, 1)
                    v.wait_ge(banks_free, i * 2 + (p + 3))
                    stt(out=gu_[:, p, :], in0=uc[:, p, :], scalar=1.0, in1=gc[:, p, :], op0=ALU.add,
                        op1=ALU.mult).then_inc(prod_ready, 1)
                    v.wait_ge(prod_ready, i * 2 + (p + 1))
                    v.wait_ge(sig_ready, i * 2 + (p + 1))
                    tt(act[:, p * 512:(p + 1) * 512], gu_[:, p, :], sg[:, p, :], ALU.mult).then_inc(act_ready, 1)

            with v.Fori(0, E) as i:
                item(i)
            n_over = v.value_load(over_i[0:1, 16:17], min_val=0, max_val=OVER)
            with v.If(n_over > 0):
                with v.Fori(E, ITEMS) as i:
                    item(i)

            v.wait_ge(last_rows_in, 32)
            for t in range(T):
                z = ring[:, t * 4096:(t + 1) * 4096].rearrange("p (k d) -> p k d", k=K)
                v.wait_ge(x_in[t], 32)
                done(ts(z[:, 0, :], z[:, 0, :], gates[:, t, 0:1], None, ALU.mult))
                for k in range(1, K):
                    done(stt(out=z[:, 0, :], in0=z[:, k, :], scalar=gates[:, t, k:k + 1], in1=z[:, 0, :],
                             op0=ALU.mult, op1=ALU.add))
                done(tt(z[:, 0, :], z[:, 0, :], g2_row, ALU.mult))
                tt(xs[:, t, :], xs[:, t, :], z[:, 0, :], ALU.add).then_inc(x3_ready, 1)
            for t in range(T):
                v.wait_ge(last_root, t + 1)
                done(nc.vector.reciprocal(ri[:, t:t + 1], rt[:, t:t + 1]))
                stt(out=xs[:, t, :], in0=xs[:, t, :], scalar=ri[:, t:t + 1], in1=fg_row, op0=ALU.mult,
                    op1=ALU.mult).then_inc(out_ready, 1)


_INS = ["x", "c", "ada_w", "ada_b", "norm1_g", "w_in", "mix_scale", "w_o", "norm2_g", "router_w",
        "router_b", "w_gu", "b_gu", "w_down", "b_down", "final_g"]
_OUTS = [((1, S, D), "float32")]


def kernel(**inputs):
    import concourse.bacc as bacc
    from concourse.bass_utils import run_bass_kernel_spmd as run

    nc = bacc.Bacc("TRN2", target_bir_lowering=False, num_devices=1)
    arrays, args = {}, []
    for name in _INS:
        a = np.ascontiguousarray(inputs[name])
        arrays[f"in_{name}"] = a
        args.append(nc.dram_tensor(f"in_{name}", a.shape, mybir.dt.from_np(a.dtype), kind="ExternalInput").ap())
    for i, (shape, dtype) in enumerate(_OUTS):
        args.append(nc.dram_tensor(f"out_{i}", shape, mybir.dt.from_np(np.dtype(dtype)),
                                   kind="ExternalOutput").ap())
    build(nc, *args)
    r = run(nc, [arrays], core_ids=[0])
    return r.results[0]["out_0"]
```

```python
import math
from contextlib import ExitStack

import numpy as np

import concourse.bass as bass
from concourse import mybir

ALU = mybir.AluOpType
ACT = mybir.ActivationFunctionType
AX = mybir.AxisListType
F32 = mybir.dt.float32
F32R = mybir.dt.float32r
BF16 = mybir.dt.bfloat16
I32 = mybir.dt.int32
U32 = mybir.dt.uint32

P = 128
D = 1024
S = 512
T = S // P
KD = D // P
EPS = 1e-6
RH, RDV = 4, 128
AH, AG, HD = 8, 2, 64
IH = 8
N_SEL = min(256, S // 4)
E = 32
K = 4
FE = 1024
LIMIT, ALPHA = 7.0, 1.702
CAP = P
BLOCKS = S // CAP
OVER = (S * K) // (CAP + 1)
ITEMS = E + OVER
MASKED, TAKEN = -1.0e38, -3.0e38
UNSEEN = -1.0e30
LOG_G = [math.log1p(-2.0 ** (-5 - h)) for h in range(RH)]
SLOPE = [2.0 ** (-8.0 * (h + 1) / AH) for h in range(AH)]
W_IDX = (HD ** -0.5) * (IH ** -0.5)

SLOTS, SLOT = 12, 2048
KEPT = 8
SEQUENCE = "A" * 8 + "WWWWBBBBWWBBWWBBBBWWBBBBWWBBOOOO"
LOAD_A, LOAD_W, LOAD_B, LOAD_O = [[n for n, m in enumerate(SEQUENCE) if m == which] for which in "AWBO"]
GU, DN = 8, 4
HALVES = 2 * GU
HALF = SLOT // 2
B_EVERY = 3
AHEAD = 4

A_VEC = 0
A_HT = A_VEC + 1
A_IK = A_HT + KD
A_IW = A_IK + 1
A_IQ = A_IW + 1
A_SC = A_IQ + 4
A_AK = A_SC + 3 * IH
A_AV = A_AK + 1
A_AQ = A_AV + 1
A_RQ = A_AQ + 4
A_RK = A_RQ + 2
A_RV = A_RK + 2
A_PT = A_RV + T
A_MIX = A_PT + T * AH
A_H2 = A_MIX + KD
D_RG = 0
D_GROW = D_RG + T
D_RS = D_GROW + 4
D_QK = D_RS + T * RH
D_WO = D_QK + T * AH


def build(nc, x, c, ada_w, ada_b, norm1_g, w_in, mix_scale, w_o, norm2_g, router_w, router_b,
          w_gu, b_gu, w_down, b_down, final_g, out):
    x = x.rearrange("b s d -> (b s) d")
    out = out.rearrange("b s d -> (b s) d")
    ada_w, w_in, w_o, router_w = ada_w[0], w_in[0], w_o[0], router_w[0]
    w_gu, b_gu, w_down, b_down = w_gu[0], b_gu[0], w_down[0], b_down[0]

    xn2_dram = nc.dram_tensor("xn2_rows", (S, D), F32, kind="Internal").ap()
    g_dram = nc.dram_tensor("g_rows", (2, D), F32, kind="Internal").ap()
    y_dram = nc.dram_tensor("expert_rows", (S * K, D), F32, kind="Internal").ap()

    ctx = ExitStack()
    with ctx:
        def sb(name, shape, dt=F32):
            return ctx.enter_context(nc.sbuf_tensor(name, shape, dt))

        def sem(name):
            return ctx.enter_context(nc.semaphore(name))

        bank = [ctx.enter_context(nc.psum_tensor(f"bank{i}", [P, 512], F32)) for i in range(8)]
        ring = sb("ring", [P, KEPT * SLOT])
        xs = sb("xs", [P, T, D])
        AREA = 18440
        area = sb("area", [P, AREA])

        def view(at, *dims):
            n = int(np.prod(dims))
            assert at + n <= AREA, (at, dims)
            v = area[:, at:at + n]
            if len(dims) == 2:
                v = v.rearrange("p (a b) -> p a b", a=dims[0])
            if len(dims) == 3:
                v = v.rearrange("p (a b c) -> p a b c", a=dims[0], b=dims[1])
            return v

        iqT = view(0, 4, S)
        rqT, rkT = view(0, 2, S), view(1024, 2, S)
        att = view(0, T, 512)
        ikT = view(2048, S)
        akT = view(2560, S)
        aqT = view(3072, 4, S)
        rv = view(5120, T, 512)
        rgs = view(7168, T, 512)
        av = view(9216, T, 128)
        iw = view(9728, T, IH)
        xn = view(3072, T, D)
        acc = view(9760, 4096)
        RS_W = [S - P * m for m in range(T)]
        RS_AT = [sum(RS_W[:m]) for m in range(T)]
        rs = view(9760, 2, sum(RS_W))
        lg = view(9760, 3, S)
        pr = view(9760 + 1536, 3, S)
        prT = view(9760 + 3072, 2, S)
        NEG_AT = [0, 128, 384, 768]
        neg = view(13856, 1280)
        rel = view(15136, 3, S)
        score = view(16672, 1152)
        SC_AT = [None, 0, 256, 640]
        work = view(17824, 512)
        decay = view(15136, RH, S)
        sq = view(17184, 512)
        g_row = view(17408, D)
        tmp = view(9760, 512)
        xn2 = view(0, T, D)
        rw = view(4096, KD, E)
        lgt = view(4400, T, E)
        isq = view(5800, T * K, P)
        isl = view(7900, T * K, P)
        xg = view(0, D)
        xgT = view(1024, KD, P)
        gc = view(2048, 2, 512)
        uc = view(3072, 2, 512)
        gu_ = view(4096, 2, 512)
        sg = view(5120, 2, 512)
        act = view(6144, D)
        actT = view(7168, KD, P)
        ys = view(8192, D)
        g2_row = view(9216, D)
        fg_row = view(10240, D)
        b_raw = view(11264, 3 * D)
        b_part = view(14336, 3 * D // 2).bitcast(BF16)[0:96, :]

        ident = sb("ident", [P, P])
        ones = sb("ones", [P, P])
        dist = sb("dist", [P, S])
        future = sb("future", [P, S])
        iota_p = dist[:, 0:P]
        after = dist[:, P:2 * P]
        q_mod = dist[:, 2 * P:2 * P + 96]
        hot_first = dist[:, 2 * P:2 * P + E]
        vec_in = view(0, P)[0:72, :]
        eid = sb("eid", [P, 1])
        tok4 = sb("tok4", [P, T * K])
        epsc = sb("epsc", [P, 1])
        vecT = sb("vecT", [P, 72])
        cs = sb("cs", [P, KD])
        csig = sb("csig", [P, KD])
        sc_c = sb("sc_c", [P, KD])
        modA = sb("modA", [P, 16])
        modB = sb("modB", [P, 16])
        a1 = sb("a1", [P, KD])
        a2 = sb("a2", [P, KD])
        ss = sb("ss", [P, 16])
        rt = sb("rt", [P, 16])
        ri = sb("ri", [P, 16])
        mx8 = sb("mx8", [P, 8])
        nmax = sb("nmax", [P, 4])
        psum_ = sb("psum_", [P, AH, T])
        pinv = sb("pinv", [P, AH, T])
        rb = sb("rb", [P, E])
        top8 = sb("top8", [P, T, 8])
        idx8 = sb("idx8", [P, T, 8], U32)
        idxf = sb("idxf", [P, T * K])
        dgate = sb("dgate", [P, T, K])
        gates = sb("gates", [P, T, K])
        rank = sb("rank", [P, T * K])
        blk = sb("blk", [P, T * K])
        flag = sb("flag", [P, 1])
        pos = sb("pos", [P, 1])
        sel16 = sb("sel16", [P, 16])
        hot96 = sb("hot96", [96, 48], BF16)
        over_i = sb("over_i", [1, 17], I32)
        sel = sb("sel", [96, P], BF16)
        gidx = sb("gidx", [P, 1], U32)
        sidx = sb("sidx", [P, 1], U32)

        with ExitStack() as mixer:
            ring_end = mixer.enter_context(nc.sbuf_tensor("ring_end", [P, (SLOTS - KEPT) * SLOT], F32))
            hT = mixer.enter_context(nc.sbuf_tensor("hT", [P, KD, S], F32))
            ro = hT[:, 0:4, :].rearrange("p t (h e) -> p t h e", h=RH)
            g_vals, g_bias = ring_end[0:1, 2 * SLOT:3 * SLOT], ring_end[0:1, 3 * SLOT:4 * SLOT]
        w_hi = sb("w_hi", [P, AHEAD, HALF], F32R)
        w_lo = sb("w_lo", [P, AHEAD, HALF], F32R)
        x_hi = sb("x_hi", [P, KD, P], F32R)
        x_lo = sb("x_lo", [P, KD, P], F32R)
        routes = sb("routes", [P, 1728])
        hot = routes[:, 0:512].rearrange("p (n e) -> p n e", e=E)
        hotC = routes[:, 512:1024].rearrange("p (n e) -> p n e", e=E)
        hot32 = routes[:, 1024:1152].rearrange("p (t e) -> p t e", e=E)
        cum = routes[:, 1152:1280].rearrange("p (t e) -> p t e", e=E)
        tabT = routes[:, 1280:1408]
        tab = routes[:, 1408:1536]
        dstf, empty = routes[:, 1536:1584], routes[:, 1584:1632]
        dst_i, tok_i = routes[:, 1632:1680].bitcast(I32), routes[:, 1680:1728].bitcast(I32)

        consts_ready, late_consts = sem("consts_ready"), sem("late_consts")
        small_in, key_in, query_in = sem("small_in"), sem("key_in"), sem("query_in")
        x_in = [sem(f"x_in{t}") for t in range(T)]
        landed = [sem(f"landed{i}") for i in range(SLOTS)]
        gu_in = [sem(f"gu_in{i}") for i in range(4)]
        down_in = [sem(f"down_in{i}") for i in range(DN)]
        hi_ready, lo_ready, half_used = sem("hi_ready"), sem("lo_ready"), sem("half_used")
        down_used = sem("down_used")
        xhi_ready, xlo_ready = sem("xhi_ready"), sem("xlo_ready")
        ada_used = sem("ada_used")
        wo_used = sem("wo_used")
        act_full, act_taken = sem("act_full"), sem("act_taken")
        dve_full, dve_taken = sem("dve_full"), sem("dve_taken")
        dve_step, act_step, pool_step = sem("dve_step"), sem("act_step"), sem("pool_step")
        csig_ready = sem("csig_ready")
        rms_root, rms_inv = sem("rms_root"), sem("rms_inv")
        xn_ready = sem("xn_ready")
        mod_full = sem("mod_full")
        affine_ready = sem("affine_ready")
        rel_added, rgsig_ready = sem("rel_added"), sem("rgsig_ready")
        decay_raw, decay_ready = sem("decay_raw"), sem("decay_ready")
        g_bias_in, g_rows_ready, g_stored = sem("g_bias_in"), sem("g_rows_ready"), sem("g_stored")
        g1_in = sem("g1_in")
        ro_full, ro_taken, ro_summed, ret_ready = (sem("ro_full"), sem("ro_taken"), sem("ro_summed"),
                                                   sem("ret_ready"))
        nmax_ready, prob_ready, pv_full, pv_taken = (sem("nmax_ready"), sem("prob_ready"),
                                                     sem("pv_full"), sem("pv_taken"))
        x2_ready, xn2_ready, xn2_stored = sem("x2_ready"), sem("xn2_ready"), sem("xn2_stored")
        router_in, router_full = sem("router_in"), sem("router_full")
        table_in, table_full = sem("table_in"), sem("table_full")
        gate_diff, gate_exp = sem("gate_diff"), sem("gate_exp")
        tables_ready, bias_in, bias_ready = sem("tables_ready"), sem("bias_in"), sem("bias_ready")
        gidx_ready, gathered = sem("gidx_ready"), sem("gathered")
        sidx_ready, scattered, sel_ready = sem("sidx_ready"), sem("scattered"), sem("sel_ready")
        turn_full, turn_taken = sem("turn_full"), sem("turn_taken")
        banks_free, gate_ready, sig_ready, act_ready = (sem("banks_free"), sem("gate_ready"),
                                                        sem("sig_ready"), sem("act_ready"))
        prod_ready, y_ready = sem("prod_ready"), sem("y_ready")
        all_scattered = sem("all_scattered")
        last_rows_in = sem("last_rows_in")
        x3_ready, last_root, out_ready, out_done = (sem("x3_ready"), sem("last_root"),
                                                    sem("out_ready"), sem("out_done"))

        def slot(n):
            s = n % SLOTS
            if s >= KEPT:
                return ring_end[:, (s - KEPT) * SLOT:(s - KEPT + 1) * SLOT]
            return ring[:, s * SLOT:(s + 1) * SLOT]

        def abank(j):
            return bank[j % 3]

        def dbank(j):
            return bank[3] if j == D_RG + T - 1 else bank[4 + j % 3]

        def wcols(n, width=256):
            return slot(n)[:, 0:KD * width].rearrange("p (k n) -> p k n", k=KD)

        def raw(w):
            return slot(w % 4)

        block = ctx.enter_context(nc.Block())

        @block.sync
        def _(sp):
            sp.dma_start(cs[:], c.rearrange("o (p k) -> p (o k)", p=P)).then_inc(small_in, 16)
            sp.dma_start(vec_in[0:48, :], ada_b.rearrange("o (j p) -> (o j) p", p=P)).then_inc(small_in, 16)
            sp.dma_start(vec_in[48:56, :], norm1_g.rearrange("o (j p) -> (o j) p", p=P)).then_inc(small_in, 16)
            sp.dma_start(vec_in[56:64, :], norm2_g.rearrange("o (j p) -> (o j) p", p=P)).then_inc(small_in, 16)
            sp.dma_start(vec_in[64:72, :], mix_scale.rearrange("o (j p) -> (o j) p", p=P)).then_inc(small_in, 16)
            for t in range(T):
                sp.dma_start(xs[:, t, :], x[t * P:(t + 1) * P, :]).then_inc(x_in[t], 16)

            def load(n, dst, src):
                sp.dma_start(dst, src).then_inc(landed[n % SLOTS], 16)

            ada = ada_w.rearrange("(p k) n -> p k n", k=KD)
            win = w_in.rearrange("(k p) n -> p k n", p=P)
            wo = w_o.rearrange("(k p) n -> p k n", p=P)
            WIN_COLS = [None, 2304, 2560, 2048, None, None, 0, 256, 1024, 1280, 512, 768]
            LAST = [A_IW, A_IQ + 1, A_IQ + 3, A_AV, A_AQ + 1, A_AQ + 3, A_RQ + 1, A_RK + 1]

            def slot_free(n):
                which = SEQUENCE[n]
                if which == "A":
                    sp.wait_ge(ada_used, LOAD_A.index(n) + 1)
                elif which == "B":
                    sp.wait_ge(ada_used, KD + LOAD_B.index(n) + 1)
                elif LOAD_W.index(n) >= len(LAST):
                    sp.wait_ge(dve_full, D_RG + T)
                else:
                    sp.wait_ge(act_full, LAST[LOAD_W.index(n)] + 1)

            def w_in_load(i, n):
                if i == 0:
                    d = wcols(n, 136)
                    sp.dma_start(d[:, :, 0:64], win[:, :, 2816:2880]).then_inc(key_in, 16)
                    sp.dma_start(d[:, :, 64:128], win[:, :, 2816:2880]).then_inc(key_in, 16)
                    load(n, d[:, :, 128:136], win[:, :, 2880:2888])
                elif i in (4, 5):
                    d = wcols(n)
                    for a in range(2):
                        for b in range(2):
                            at = 1536 + (4 * b + 2 * (i - 4) + a) * HD
                            q = sp.dma_start(d[:, :, (2 * a + b) * HD:(2 * a + b + 1) * HD],
                                             win[:, :, at:at + HD])
                            if (a, b) == (1, 1):
                                q.then_inc(landed[n % SLOTS], 16)
                            else:
                                q.then_inc(query_in, 16)
                else:
                    at = WIN_COLS[i]
                    load(n, wcols(n), win[:, :, at:at + 256])

            for n, which in enumerate(SEQUENCE):
                if n >= SLOTS:
                    slot_free(n - SLOTS)
                if which == "A":
                    k = LOAD_A.index(n)
                    load(n, slot(n), ada[:, k, 0:2048])
                elif which == "W":
                    w_in_load(LOAD_W.index(n), n)
                elif which == "B":
                    k, half = divmod(LOAD_B.index(n), 2)
                    load(n, slot(n), ada[:, k, 2048 * (half + 1):2048 * (half + 2)])
                else:
                    i = LOAD_O.index(n)
                    load(n, slot(n).rearrange("p (k n) -> p k n", k=2), wo[:, 2 * i:2 * i + 2, :])

            def gu_chunk(w, e):
                half, k4, g = w // 4, (w // 2) % 2, w % 2
                src = w_gu[e, 4 * k4 * P:(4 * k4 + 4) * P, g * FE + half * 512:g * FE + half * 512 + 512]
                sp.dma_start(raw(w).rearrange("p (k n) -> p k n", k=4),
                             src.rearrange("(k p) n -> p k n", p=P)).then_inc(gu_in[w % 4], 16)

            def down_chunk(q, e):
                src = w_down[e, 2 * q * P:(2 * q + 2) * P, :].rearrange("(k p) n -> p k n", p=P)
                sp.dma_start(slot(4 + q).rearrange("p (k n) -> p k n", k=2), src).then_inc(down_in[q], 16)

            for q in range(DN):
                slot_free(len(SEQUENCE) + q - SLOTS)
                down_chunk(q, 0)
            for w in range(4):
                if w < 3:
                    sp.wait_ge(wo_used, w + 1)
                else:
                    sp.wait_ge(dve_full, D_WO + 2 * T)
                gu_chunk(w, 0)

            def gu_later(w, i, e):
                sp.wait_ge(lo_ready, i * HALVES + (2 * (w - 4) + 2))
                gu_chunk(w % GU, e)

            def down_later(q, i, e):
                sp.wait_ge(down_used, i * DN + (q + 1 - DN))
                down_chunk(q, e)

            def item(i, e, e_next, ahead):
                gu_later(4, i, e)
                gu_later(5, i, e)
                for q in range(DN):
                    down_later(q, i, e)
                gu_later(6, i, e)
                gu_later(7, i, e)
                for w in range(ahead):
                    gu_later(w + GU, i, e_next)

            for w in range(4, GU):
                gu_later(w, 0, 0)
            for w in range(4):
                gu_later(w + GU, 0, 1)
            with sp.Fori(1, E - 1) as i:
                item(i, i, i + 1, 4)
            sp.wait_ge(tables_ready, 1)
            n_over = sp.value_load(over_i[0:1, 16:17], min_val=0, max_val=OVER)
            e32 = sp.value_load(over_i[0:1, 0:1], min_val=0, max_val=E - 1)
            item(E - 1, E - 1, e32, 2)
            with sp.If(n_over > 0):
                for w in range(2, 4):
                    gu_later(w + GU, E - 1, e32)
                with sp.Fori(E, ITEMS) as i:
                    e = sp.value_load(over_i[0:1, bass.ds(i - E, 1)], min_val=0, max_val=E - 1)
                    e_next = sp.value_load(over_i[0:1, bass.ds(i - (E - 1), 1)], min_val=0, max_val=E - 1)
                    item(i, e, e_next, 4)
                for w in range(2, 4):
                    sp.wait_ge(gu_in[w], 16 * (2 * ITEMS + 1))
            sp.wait_ge(all_scattered, 1)
            for t in range(T):
                sp.dma_start(ring[:, t * 4096:(t + 1) * 4096].rearrange("p (k d) -> p k d", k=K),
                             y_dram[t * P * K:(t + 1) * P * K, :].rearrange("(p k) d -> p k d", k=K)
                             ).then_inc(x_in[t], 16)
            for t in range(T):
                sp.wait_ge(out_ready, t + 1)
                sp.dma_start(out[t * P:(t + 1) * P, :], xs[:, t, :]).then_inc(out_done, 16)
            sp.wait_ge(out_done, 16 * T)

        @block.gpsimd
        def _(pool):
            steps = [0]

            def done(ins):
                steps[0] += 1
                ins.then_inc(pool_step, 1)
                pool.wait_ge(pool_step, steps[0])

            done(nc.gpsimd.memset(ones[:], 1.0))
            done(nc.gpsimd.memset(epsc[:], EPS))
            done(nc.gpsimd.memset(future[:], 0.0))
            done(nc.gpsimd.affine_select(out=ident[:], in_=ones[:], compare_op=ALU.is_equal, fill=0.0, base=0,
                                         pattern=[[1, P]], channel_multiplier=-1))
            done(nc.gpsimd.affine_select(out=future[:, 384:512], in_=future[:, 384:512], compare_op=ALU.is_ge,
                                         fill=MASKED, base=0, pattern=[[-1, P]], channel_multiplier=1))
            done(nc.gpsimd.iota(dist[:], pattern=[[1, S]], base=-384, channel_multiplier=-1,
                                allow_small_or_imprecise_dtypes=True))
            done(nc.gpsimd.iota(tok4[:], pattern=[[P * K, T], [1, K]], base=1, channel_multiplier=K,
                                allow_small_or_imprecise_dtypes=True))
            for b in range(4):
                done(nc.gpsimd.iota(eid[32 * b:32 * b + 32, :], pattern=[[0, 1]], base=0, channel_multiplier=1,
                                    allow_small_or_imprecise_dtypes=True))
            nc.gpsimd.memset(flag[0:32, :], 0.0).then_inc(consts_ready, 1)

            pool.wait_ge(ada_used, 3 * KD)
            pool.dma_start(g_bias[:, 0:D], ada_b[0:1, 2 * D:3 * D]).then_inc(g_bias_in, 16)
            pool.dma_start(g_bias[:, D:2 * D], ada_b[0:1, 5 * D:6 * D]).then_inc(g_bias_in, 16)

            pool.wait_ge(dve_taken, D_RG + T)
            nc.gpsimd.iota(decay[:, RH - 1, :], pattern=[[1, S]], base=0, channel_multiplier=-1,
                           allow_small_or_imprecise_dtypes=True).then_inc(decay_raw, 1)
            for h in range(RH):
                pool.wait_ge(decay_raw, 2 + h)
                nc.gpsimd.affine_select(out=decay[:, h, 0:P], in_=decay[:, h, 0:P], compare_op=ALU.is_ge, fill=0.0,
                                        base=0, pattern=[[1, P]], channel_multiplier=-1).then_inc(decay_ready, 1)
            done(nc.gpsimd.affine_select(out=after, in_=ones[:], compare_op=ALU.is_gt, fill=0.0, base=0,
                                         pattern=[[1, P]], channel_multiplier=-1))
            done(nc.gpsimd.iota(iota_p, pattern=[[1, P]], base=0, channel_multiplier=0,
                                allow_small_or_imprecise_dtypes=True))
            done(nc.gpsimd.memset(q_mod, 0.0))
            for off in (-64, -32, 0, 32, 64, 96):
                done(nc.gpsimd.affine_select(out=q_mod, in_=q_mod, compare_op=ALU.not_equal, fill=1.0,
                                             base=off, pattern=[[1, 96]], channel_multiplier=-1))
            nc.gpsimd.memset(flag[0:32, :], 0.0).then_inc(late_consts, 1)
            pool.wait_ge(dve_taken, D_GROW + 4)
            pool.dma_start(g_dram.rearrange("(o a) d -> o (a d)", o=1), g_vals).then_inc(g_stored, 16)
            pool.wait_ge(g_stored, 16)
            pool.wait_ge(ro_summed, 1)
            pool.dma_start(g_row, g_dram[0].partition_broadcast(P)).then_inc(g1_in, 16)

            pool.wait_ge(act_taken, A_MIX + KD)
            pool.dma_start(rw, router_w.rearrange("(k p) e -> p k e", p=P)).then_inc(router_in, 16)
            pool.dma_start(rb[:], router_b[0].partition_broadcast(P)).then_inc(router_in, 16)
            for j in range(3):
                pool.dma_start(b_raw[32 * j:32 * j + 32, 0:2048], b_gu).then_inc(bias_in, 16)
                pool.dma_start(b_raw[32 * j:32 * j + 32, 2048:3072], b_down).then_inc(bias_in, 16)

            for t in range(T):
                pool.wait_ge(xn2_ready, t + 1)
                pool.dma_start(xn2_dram[t * P:(t + 1) * P, :], xn2[:, t, :]).then_inc(xn2_stored, 16)
            pool.wait_ge(xn2_stored, 16 * T)
            pool.wait_ge(tables_ready, 1)

            done(nc.gpsimd.memset(xg, 0.0))
            pool.dma_start(g2_row, g_dram[1].partition_broadcast(P)).then_inc(last_rows_in, 16)
            pool.dma_start(fg_row, final_g.partition_broadcast(P)).then_inc(last_rows_in, 16)

            last_token, last_row = pool.to_reg(S - 1), pool.to_reg(S * K - 1)

            def gather():
                pool.indirect_dma_start(out=xg, out_offset=None, in_=xn2_dram,
                                        in_offset=bass.IndirectOffsetOnAxis(ap=gidx[:, 0:1], axis=0),
                                        bounds_check=last_token, oob_is_err=False).then_inc(gathered, 16)

            pool.tensor_copy(gidx[:].bitcast(I32), tok_i[:, 0:1]).then_inc(gidx_ready, 1)
            pool.wait_ge(gidx_ready, 1)
            gather()
            pool.sem_clear(gidx_ready)
            pool.tensor_copy(sel[:], hot96[:, 0:1].broadcast_to((96, P))).then_inc(sel_ready, 1)

            def item(i):
                nxt = pool.snap(i + 1)
                pool.wait_ge(turn_full, i * 4 + 2)
                pool.wait_ge(gathered, i * 16 + 16)
                pool.tensor_copy(gidx[:].bitcast(I32), tok_i[:, bass.ds(nxt, 1)]).then_inc(gidx_ready, 1)
                pool.wait_ge(gidx_ready, 1)
                gather()
                pool.sem_clear(gidx_ready)
                pool.wait_ge(down_used, i * DN + 1)
                pool.tensor_copy(sel[:], hot96[:, bass.ds(nxt, 1)].broadcast_to((96, P))).then_inc(sel_ready, 1)
                pool.wait_ge(y_ready, i + 1)
                pool.tensor_copy(sidx[:].bitcast(I32), dst_i[:, bass.ds(i, 1)]).then_inc(sidx_ready, 1)
                pool.wait_ge(sidx_ready, 1)
                pool.indirect_dma_start(out=y_dram,
                                        out_offset=bass.IndirectOffsetOnAxis(ap=sidx[:, 0:1], axis=0),
                                        in_=ys, in_offset=None,
                                        bounds_check=last_row, oob_is_err=False).then_inc(scattered, 16)
                pool.sem_clear(sidx_ready)
                pool.wait_ge(scattered, i * 16 + 16)

            with pool.Fori(0, E) as i:
                item(i)
            n_over = pool.value_load(over_i[0:1, 16:17], min_val=0, max_val=OVER)
            with pool.If(n_over > 0):
                with pool.Fori(E, ITEMS) as i:
                    item(i)
            nc.gpsimd.memset(sidx[:], 0).then_inc(all_scattered, 1)

        @block.scalar
        def _(a):
            steps = [0]

            def done(ins):
                steps[0] += 1
                ins.then_inc(act_step, 1)
                a.wait_ge(act_step, steps[0])

            def copy(dst, src, scale=1.0):
                return nc.scalar.activation(dst, src, ACT.Copy, scale=scale)

            def affine(dst, src, scale, bias):
                return nc.scalar.activation(dst, src, ACT.Identity, scale=scale, bias=bias)

            a.wait_ge(small_in, 16 * 5)
            nc.scalar.activation(csig[:], cs[:], ACT.Sigmoid).then_inc(csig_ready, 1)
            for t in range(T):
                a.wait_ge(x_in[t], 16)
                done(nc.scalar.activation(xn[:, t, :], xs[:, t, :], ACT.Square, accum_out=ss[:, t:t + 1]))
            a.wait_ge(consts_ready, 1)
            nc.scalar.activation(rt[:, 0:T], ss[:, 0:T], ACT.Sqrt, scale=1.0 / D, bias=epsc[:]).then_inc(rms_root, 1)
            a.wait_ge(rms_inv, 1)
            for t in range(T):
                copy(xn[:, t, :], xs[:, t, :], ri[:, t:t + 1]).then_inc(xn_ready, 1)
            j = A_VEC
            a.wait_ge(act_full, j + 1)
            copy(vecT[:], abank(j)[:, 0:72]).then_inc(act_taken, 1)
            a.wait_ge(affine_ready, 1)
            for k in range(KD):
                j = A_HT + k
                a.wait_ge(act_full, j + 1)
                affine(hT[:, k, :], abank(j)[:], a1[:, k:k + 1], modA[:, k:k + 1]).then_inc(act_taken, 1)

            def take(j, dst, scale=1.0, src=None):
                a.wait_ge(act_full, j + 1)
                copy(dst, abank(j)[:] if src is None else src, scale).then_inc(act_taken, 1)

            take(A_IK, ikT)
            take(A_IW, iw, W_IDX, abank(A_IW)[:, 0:T * IH].rearrange("p (t h) -> p t h", t=T))
            for m in range(4):
                take(A_IQ + m, iqT[:, m, :])
            for n in range(3 * IH):
                t = 1 + n // IH
                a.wait_ge(act_full, A_SC + n + 1)
                if n >= 3:
                    a.wait_ge(rel_added, n - 2)
                nc.scalar.activation(rel[:, n % 3, 0:(t + 1) * P], abank(A_SC + n)[:, 0:(t + 1) * P],
                                     ACT.Relu).then_inc(act_taken, 1)
            take(A_AK, akT)
            take(A_AV, av, 1.0, abank(A_AV)[:].rearrange("p (t n) -> p t n", t=T))
            for m in range(4):
                take(A_AQ + m, aqT[:, m, :], HD ** -0.5)
            for m in range(2):
                take(A_RQ + m, rqT[:, m, :])
            for m in range(2):
                take(A_RK + m, rkT[:, m, :], HD ** -0.5)
            a.wait_ge(rel_added, 3 * IH)
            for t in range(T):
                a.wait_ge(dve_full, D_RG + t + 1)
                if t >= 2:
                    a.wait_ge(dve_taken, D_RG + t - 1)
                nc.scalar.activation(rel[:, t % 2, :], dbank(D_RG + t)[:], ACT.Sigmoid).then_inc(rgsig_ready, 1)
            for t in range(2):
                take(A_RV + t, rv[:, t, :])
            a.wait_ge(decay_raw, 1)
            for h in range(RH):
                nc.scalar.activation(decay[:, h, :], decay[:, RH - 1, :], ACT.Exp,
                                     scale=LOG_G[h]).then_inc(decay_raw, 1)
            for t in range(2, T):
                take(A_RV + t, rv[:, t, :])
            for h in range(RH):
                b = bank[3 + 4 * (h % 2)]
                a.wait_ge(ro_full, h + 1)
                for n in range(T):
                    done(nc.scalar.activation(sq[:, 0:P], b[:, n * P:(n + 1) * P], ACT.Square,
                                              accum_out=ss[:, n * RH + h:n * RH + h + 1]))
                copy(ro[:, :, h, :], b[:].rearrange("p (t e) -> p t e", t=T)).then_inc(ro_taken, 1)


            order = [(t, h) for t in range(T) for h in range(AH)]

            def probs(n):
                t, h = order[n]
                w = (t + 1) * P
                a.wait_ge(nmax_ready, n + 1)
                if n >= 3:
                    a.wait_ge(act_full, A_PT + n - 3 + 1)
                nc.scalar.activation(pr[:, n % 3, 0:w], lg[:, n % 3, 0:w], ACT.Exp, bias=nmax[:, n % 4:n % 4 + 1],
                                     accum_out=psum_[:, h, t:t + 1]).then_inc(prob_ready, 1)

            def turned(n):
                w = (order[n][0] + 1) * P
                j = A_PT + n
                a.wait_ge(act_full, j + 1)
                if n >= 2:
                    a.wait_ge(pv_full, n - 1)
                copy(prT[:, n % 2, 0:w], abank(j)[:, 0:w]).then_inc(act_taken, 1)
            for n in range(len(order) + 1):
                if n == AH // 2:
                    nc.scalar.activation(rt[:], ss[:], ACT.Sqrt, scale=1.0 / RDV, bias=epsc[:]).then_inc(ro_summed, 1)
                if n < len(order):
                    probs(n)
                if n >= 1:
                    turned(n - 1)

            for k in range(KD):
                j = A_MIX + k
                a.wait_ge(act_full, j + 1)
                copy(hT[:, k, :], abank(j)[:], vecT[:, 64 + k:65 + k]).then_inc(act_taken, 1)
            for t in range(T):
                a.wait_ge(x2_ready, 2 * t + 2)
                done(nc.scalar.activation(xn2[:, t, :], xs[:, t, :], ACT.Square, accum_out=ss[:, t:t + 1]))
            nc.scalar.activation(rt[:, 0:T], ss[:, 0:T], ACT.Sqrt, scale=1.0 / D, bias=epsc[:]).then_inc(rms_root, 1)
            a.wait_ge(rms_inv, 2)
            for t in range(T):
                copy(xn2[:, t, :], xs[:, t, :], ri[:, t:t + 1]).then_inc(xn2_ready, 1)
            for k in range(KD):
                j = A_H2 + k
                a.wait_ge(act_full, j + 1)
                affine(hT[:, k, :], abank(j)[:], a2[:, k:k + 1], modB[:, k:k + 1]).then_inc(act_taken, 1)
            a.wait_ge(gate_diff, 1)
            nc.scalar.activation(gates[:], dgate[:], ACT.Exp).then_inc(gate_exp, 1)

            def turn(u, dst, bank_no, scales=None):
                a.wait_ge(turn_full, u + 1)
                if scales is None:
                    copy(dst, bank[bank_no][:].rearrange("p (k n) -> p k n", k=4)).then_inc(turn_taken, 1)
                    return
                for q in range(4):
                    k = scales + q
                    last = affine(dst[:, q, :], bank[bank_no][:, q * P:(q + 1) * P], a2[:, k:k + 1],
                                  modB[:, k:k + 1])
                last.then_inc(turn_taken, 1)

            def hi(i, h):
                w = h % HALVES // 2
                if h % 2 == 0:
                    a.wait_ge(gu_in[w % 4], i * 32 + (16 * (h // 8) + 16))
                if not (isinstance(i, int) and i == 0 and h < AHEAD):
                    a.wait_ge(half_used, i * HALVES + (h + 1 - AHEAD))
                copy(w_hi[:, h % AHEAD, :], raw(w)[:, (h % 2) * HALF:(h % 2 + 1) * HALF]).then_inc(hi_ready, 1)

            def x_turn(u, n, bank_no, half):
                turn(u, xgT[:, 4 * half:4 * half + 4, :], bank_no, 4 * half)
                a.wait_ge(turn_taken, u + 1)
                copy(x_hi[:, 4 * half:4 * half + 4, :], xgT[:, 4 * half:4 * half + 4, :]).then_inc(xhi_ready, 1)

            def item(i):
                def sigmoid(p):
                    a.wait_ge(gate_ready, i * 2 + (p + 1))
                    nc.scalar.activation(sg[:, p, :], gc[:, p, :], ACT.Sigmoid, scale=ALPHA).then_inc(sig_ready, 1)
                for h in range(AHEAD, 12):
                    hi(i, h)
                sigmoid(0)
                for h in range(12, HALVES + 3):
                    hi(i, h)
                turn(i * 4 + 2, actT[:, 0:4, :], 6)
                sigmoid(1)
                hi(i, HALVES + 3)
                x_turn(i * 4 + 3, i * 2 + 2, 7, 0)
                turn(i * 4 + 4, actT[:, 4:8, :], 6)
                x_turn(i * 4 + 5, i * 2 + 3, 7, 1)
                a.wait_ge(down_used, i * DN + DN)
                a.wait_ge(sel_ready, i + 2)
                copy(ys[:, 0:512], bank[4][:])
                copy(ys[:, 512:1024], bank[5][:]).then_inc(y_ready, 1)

            for h in range(AHEAD):
                hi(0, h)
            a.wait_ge(tables_ready, 1)
            x_turn(0, 0, 6, 0)
            x_turn(1, 1, 7, 1)
            with a.Fori(0, E) as i:
                item(i)
            n_over = a.value_load(over_i[0:1, 16:17], min_val=0, max_val=OVER)
            with a.If(n_over > 0):
                with a.Fori(E, ITEMS) as i:
                    item(i)

            for t in range(T):
                a.wait_ge(x3_ready, t + 1)
                done(nc.scalar.activation(ring[:, t * 4096:t * 4096 + D], xs[:, t, :], ACT.Square,
                                          accum_out=ss[:, t:t + 1]))
                nc.scalar.activation(rt[:, t:t + 1], ss[:, t:t + 1], ACT.Sqrt, scale=1.0 / D,
                                     bias=epsc[:]).then_inc(last_root, 1)

        @block.tensor
        def _(pe):
            def free(j):
                if j >= 3:
                    pe.wait_ge(act_taken, j - 2)

            def dfree(j):
                if j >= 3 and j != D_RG + T - 1:
                    pe.wait_ge(dve_taken, j - 2)

            def have(n):
                pe.wait_ge(landed[n % SLOTS], 16 * (n // SLOTS + 1))

            pe.wait_ge(consts_ready, 1)
            pe.wait_ge(small_in, 16 * 5)
            pe.transpose(abank(A_VEC)[:, 0:72], vec_in, ident[0:72, 0:72]).then_inc(act_full, 1)

            pe.wait_ge(ada_used, KD)
            for m in range(16):
                mm = pe.matmul(bank[7][:, m:m + 1], acc[:, m * P:(m + 1) * P], ones[:, 0:1], start=True, stop=True)
            mm.then_inc(mod_full, 1)

            pe.wait_ge(xn_ready, T)
            for k in range(KD):
                j = A_HT + k
                free(j)
                for t in range(T):
                    mm = pe.transpose(abank(j)[:, t * P:(t + 1) * P], xn[:, t, k * P:(k + 1) * P], ident[:])
                mm.then_inc(act_full, 1)

            def by_feature(j, w, at):
                free(j)
                for k in range(KD):
                    mm = pe.matmul(abank(j)[:], w[:, k, at:at + P], hT[:, k, :], start=(k == 0), stop=(k == KD - 1))
                mm.then_inc(act_full, 1)

            pe.wait_ge(act_taken, A_HT + KD)
            pe.wait_ge(key_in, 32)
            have(LOAD_W[0])
            w = wcols(LOAD_W[0], 136)
            by_feature(A_IK, w, 0)
            free(A_IW)
            for t in range(T):
                for k in range(KD):
                    mm = pe.matmul(abank(A_IW)[:, t * IH:(t + 1) * IH], hT[:, k, t * P:(t + 1) * P],
                                   w[:, k, 128:136], start=(k == 0), stop=(k == KD - 1))
            mm.then_inc(act_full, 1)
            for m in range(4):
                if m % 2 == 0:
                    have(LOAD_W[1 + m // 2])
                by_feature(A_IQ + m, wcols(LOAD_W[1 + m // 2]), (m % 2) * P)
            pe.wait_ge(act_taken, A_IQ + 4)
            for n in range(3 * IH):
                t, h = 1 + n // IH, n % IH
                j = A_SC + n
                lo = HD * (h % 2)
                free(j)
                pe.matmul(abank(j)[:, 0:(t + 1) * P], iqT[lo:lo + HD, h // 2, t * P:(t + 1) * P],
                          ikT[lo:lo + HD, 0:(t + 1) * P], start=True, stop=True).then_inc(act_full, 1)
            have(LOAD_W[3])
            w = wcols(LOAD_W[3])
            by_feature(A_AK, w, 0)
            free(A_AV)
            for t in range(T):
                for k in range(KD):
                    mm = pe.matmul(abank(A_AV)[:, t * P:(t + 1) * P], hT[:, k, t * P:(t + 1) * P],
                                   w[:, k, P:2 * P], start=(k == 0), stop=(k == KD - 1))
            mm.then_inc(act_full, 1)
            pe.wait_ge(query_in, 16 * 6)
            for first, n in ((A_AQ, LOAD_W[4]), (A_AQ + 2, LOAD_W[5]), (A_RQ, LOAD_W[6]), (A_RK, LOAD_W[7])):
                have(n)
                for m in range(2):
                    by_feature(first + m, wcols(n), m * P)
            for first, n in ((None, LOAD_W[8]), (A_RV, LOAD_W[10])):
                have(n)
                have(n + 1)
                s0 = n % SLOTS
                both = ring_end[:, (s0 - KEPT) * SLOT:(s0 - KEPT + 2) * SLOT] if s0 >= KEPT else \
                    ring[:, s0 * SLOT:(s0 + 2) * SLOT]
                w2 = both.rearrange("p (s k n) -> p k s n", s=2, k=KD)
                for t in range(T):
                    if first is None:
                        b = dbank(D_RG + t)
                        dfree(D_RG + t)
                    else:
                        b = abank(first + t)
                        free(first + t)
                    for k in range(KD):
                        mm = pe.matmul(b[:].rearrange("p (s n) -> p s n", s=2), hT[:, k, t * P:(t + 1) * P],
                                       w2[:, k], start=(k == 0), stop=(k == KD - 1))
                    mm.then_inc(act_full if first is not None else dve_full, 1)

            pe.wait_ge(ada_used, 3 * KD)
            for m in range(16):
                mm = pe.matmul(bank[7][:, m:m + 1], acc[:, 1024 + m * P:1024 + (m + 1) * P], ones[:, 0:1],
                               start=True, stop=True)
            mm.then_inc(mod_full, 1)
            for n, at in enumerate((0, 512, 3072, 3584)):
                j = D_GROW + n
                dfree(j)
                pe.matmul(dbank(j)[0:1, :], ones[:, 0:1], acc[:, at:at + 512], start=True,
                          stop=True).then_inc(dve_full, 1)

            pe.wait_ge(act_taken, A_RV + T)
            for h in range(RH):
                lo = HD * (h % 2)
                for m in range(T):
                    j = D_RS + h * T + m
                    dfree(j)
                    pe.matmul(dbank(j)[:, 0:RS_W[m]], rkT[lo:lo + HD, h // 2, m * P:(m + 1) * P],
                              rqT[lo:lo + HD, h // 2, m * P:S], start=True, stop=True).then_inc(dve_full, 1)
                b = bank[3 + 4 * (h % 2)]
                if h >= 2:
                    pe.wait_ge(ro_taken, h - 1)
                elif h == 1:
                    pe.wait_ge(affine_ready, 2)
                pe.wait_ge(dve_taken, D_RS + h * T + T)
                for n in range(T):
                    for m in range(n + 1):
                        at = RS_AT[m] + (n - m) * P
                        mm = pe.matmul(b[:, n * P:(n + 1) * P], rs[:, h % 2, at:at + P],
                                       rv[:, m, h * P:(h + 1) * P], start=(m == 0), stop=(m == n))
                mm.then_inc(ro_full, 1)

            order = [(t, h) for t in range(T) for h in range(AH)]

            def logits(n):
                t, h = order[n]
                lo = HD * (h // 4)
                dfree(D_QK + n)
                pe.matmul(dbank(D_QK + n)[:, 0:(t + 1) * P], aqT[lo:lo + HD, h % 4, t * P:(t + 1) * P],
                          akT[lo:lo + HD, 0:(t + 1) * P], start=True, stop=True).then_inc(dve_full, 1)

            def turn_probs(n):
                t, h = order[n]
                free(A_PT + n)
                pe.wait_ge(prob_ready, n + 1)
                for m in range(t + 1):
                    mm = pe.transpose(abank(A_PT + n)[:, m * P:(m + 1) * P], pr[:, n % 3, m * P:(m + 1) * P],
                                      ident[:])
                mm.then_inc(act_full, 1)

            def values(n):
                t, h = order[n]
                if h == 0 and t >= 2:
                    pe.wait_ge(pv_taken, t - 1)
                if n == 0:
                    pe.wait_ge(ro_taken, RH)
                pe.wait_ge(act_taken, A_PT + n + 1)
                g = h // 4
                for m in range(t + 1):
                    mm = pe.matmul(bank[3 + 4 * (t % 2)][:, h * HD:(h + 1) * HD], prT[:, n % 2, m * P:(m + 1) * P],
                                   av[:, m, g * HD:(g + 1) * HD], start=(m == 0), stop=(m == t))
                mm.then_inc(pv_full, 1)
            for n in range(len(order) + 3):
                if n < len(order):
                    logits(n)
                if 2 <= n < len(order) + 2:
                    turn_probs(n - 2)
                if n >= 3:
                    values(n - 3)

            for k in range(KD):
                j = A_MIX + k
                free(j)
                if k == 0:
                    pe.wait_ge(ret_ready, T * RH)
                if k == 4:
                    pe.wait_ge(pv_taken, T)
                for t in range(T):
                    src = rgs[:, t, k * P:(k + 1) * P] if k < 4 else att[:, t, (k - 4) * P:(k - 3) * P]
                    mm = pe.transpose(abank(j)[:, t * P:(t + 1) * P], src, ident[:])
                mm.then_inc(act_full, 1)
            pe.wait_ge(act_taken, A_MIX + KD)
            for t in range(T):
                for q in range(2):
                    j = D_WO + 2 * t + q
                    dfree(j)
                    for k in range(KD):
                        n = LOAD_O[k // 2]
                        if (t, q) == (0, 0) and k % 2 == 0:
                            have(n)
                        w = slot(n).rearrange("p (k n) -> p k n", k=2)
                        mm = pe.matmul(dbank(j)[:], hT[:, k, t * P:(t + 1) * P], w[:, k % 2, q * 512:(q + 1) * 512],
                                       start=(k == 0), stop=(k == KD - 1))
                        if (t, q) == (T - 1, 1) and k % 2 == 1 and k < KD - 1:
                            mm.then_inc(wo_used, 1)
                    mm.then_inc(dve_full, 1)

            pe.wait_ge(xn2_ready, T)
            for k in range(KD):
                j = A_H2 + k
                free(j)
                for t in range(T):
                    mm = pe.transpose(abank(j)[:, t * P:(t + 1) * P], xn2[:, t, k * P:(k + 1) * P], ident[:])
                mm.then_inc(act_full, 1)
            pe.wait_ge(act_taken, A_H2 + KD)
            pe.wait_ge(router_in, 32)
            for t in range(T):
                for k in range(KD):
                    mm = pe.matmul(bank[3][:, t * E:(t + 1) * E], hT[:, k, t * P:(t + 1) * P], rw[:, k, :],
                                   start=(k == 0), stop=(k == KD - 1))
            mm.then_inc(router_full, 1)

            pe.wait_ge(table_in, 1)
            for t in range(T):
                for u in range(t + 1):
                    mm = pe.matmul(bank[7][:, t * E:(t + 1) * E], after if u == t else ones[:], hot32[:, u, :],
                                   start=(u == 0), stop=(u == t))
            mm.then_inc(table_full, 1)
            pe.wait_ge(table_in, 2)
            for n in range(T * K):
                pe.matmul(bank[0][:, 0:P], isl[:, n, :], isq[:, n, :], start=(n == 0), stop=(n == T * K - 1))
            for n in range(T * K):
                mm = pe.matmul(bank[1][:, 0:P], isq[:, n, :], isl[:, n, :], start=(n == 0), stop=(n == T * K - 1))
            mm.then_inc(table_full, 1)
            pe.wait_ge(table_in, 3)
            pe.matmul(bank[2][:, 0:1], after, flag[:], start=True, stop=True).then_inc(table_full, 1)
            pe.wait_ge(table_in, 4)
            pe.matmul(bank[4][:, 0:16], tab, sel16[:], start=True, stop=True)
            pe.matmul(bank[5][0:96, 0:16], q_mod, sel16[:], start=True, stop=True)
            pe.matmul(bank[6][0:1, 0:16], eid[:], sel16[:], start=True, stop=True)
            pe.matmul(bank[6][0:1, 16:17], ones[:, 0:1], flag[:], start=True, stop=True).then_inc(table_full, 1)
            pe.wait_ge(tables_ready, 1)

            def turn(u, bank_no, src):
                for q in range(4):
                    mm = pe.transpose(bank[bank_no][:, q * P:(q + 1) * P], src[:, q * P:(q + 1) * P], ident[:])
                mm.then_inc(turn_full, 1)

            def item(i):
                pe.wait_ge(sel_ready, i + 1)
                pe.wait_ge(xlo_ready, i * 2 + 2)
                for p in range(2):
                    pe.wait_ge(banks_free, i * 2 + (p + 1))
                    gb, ub = bank[2 * p], bank[2 * p + 1]
                    pe.matmul(gb[:], sel[:], b_part[:, p * 512:p * 512 + 512], start=True, stop=False)
                    pe.matmul(ub[:], sel[:], b_part[:, 1024 + p * 512:1536 + p * 512], start=True, stop=False)
                    for h in range(8 * p, 8 * p + 8):
                        w = h // 2
                        pe.wait_ge(lo_ready, i * HALVES + (h + 1))
                        for k in range(2):
                            kk = 4 * ((w // 2) % 2) + 2 * (h % 2) + k
                            o = (gb, ub)[w % 2][:]
                            hi = w_hi[:, h % AHEAD, k * 512:(k + 1) * 512]
                            lo = w_lo[:, h % AHEAD, k * 512:(k + 1) * 512]
                            pe.matmul(o, x_hi[:, kk, :], hi, start=False, stop=False)
                            pe.matmul(o, x_hi[:, kk, :], lo, start=False, stop=False)
                            mm = pe.matmul(o, x_lo[:, kk, :], hi, start=False, stop=(kk == KD - 1))
                        mm.then_inc(half_used, 1)
                pe.wait_ge(act_ready, i * 2 + 1)
                pe.wait_ge(turn_taken, i * 4 + 1)
                turn(i * 4 + 2, 6, act[:, 0:512])
                pe.wait_ge(gathered, i * 16 + 32)
                pe.wait_ge(turn_taken, i * 4 + 2)
                turn(i * 4 + 3, 7, xg[:, 0:512])
                for half in range(2):
                    pe.wait_ge(turn_taken, i * 4 + 3 + 2 * half)
                    if half == 0:
                        for q in range(2):
                            pe.matmul(bank[4 + q][:], sel[:], b_part[:, 2048 + q * 512:2560 + q * 512], start=True,
                                      stop=False)
                    for c4 in range(2):
                        wq = 2 * half + c4
                        pe.wait_ge(down_in[wq], i * 16 + 16)
                        w = slot(4 + wq).rearrange("p (k n) -> p k n", k=2)
                        for k in range(2):
                            kk = 4 * half + 2 * c4 + k
                            for q in range(2):
                                mm = pe.matmul(bank[4 + q][:], actT[:, kk, :], w[:, k, q * 512:(q + 1) * 512],
                                               start=False, stop=(kk == KD - 1))
                        mm.then_inc(down_used, 1)
                    if half == 0:
                        pe.wait_ge(act_ready, i * 2 + 2)
                        turn(i * 4 + 4, 6, act[:, 512:1024])
                        pe.wait_ge(turn_taken, i * 4 + 4)
                        turn(i * 4 + 5, 7, xg[:, 512:1024])

            pe.wait_ge(gathered, 16)
            turn(0, 6, xg[:, 0:512])
            turn(1, 7, xg[:, 512:1024])
            pe.wait_ge(bias_ready, 1)
            with pe.Fori(0, E) as i:
                item(i)
            n_over = pe.value_load(over_i[0:1, 16:17], min_val=0, max_val=OVER)
            with pe.If(n_over > 0):
                with pe.Fori(E, ITEMS) as i:
                    item(i)

        @block.vector
        def _(v):
            steps = [0]

            def done(ins):
                steps[0] += 1
                ins.then_inc(dve_step, 1)
                v.wait_ge(dve_step, steps[0])

            tt, ts, stt = nc.vector.tensor_tensor, nc.vector.tensor_scalar, nc.vector.scalar_tensor_tensor

            v.wait_ge(csig_ready, 1)
            done(tt(sc_c[:], cs[:], csig[:], ALU.mult))
            v.wait_ge(rms_root, 1)
            nc.vector.reciprocal(ri[:, 0:T], rt[:, 0:T]).then_inc(rms_inv, 1)

            def modulate(n, at, k):
                v.wait_ge(landed[n % SLOTS], 16 * (n // SLOTS + 1))
                o = acc[:, at:at + 2048]
                if k == 0:
                    ins = ts(o, slot(n), sc_c[:, k:k + 1], None, ALU.mult)
                else:
                    ins = stt(out=o, in0=slot(n), scalar=sc_c[:, k:k + 1], in1=o, op0=ALU.mult, op1=ALU.add)
                ins.then_inc(ada_used, 1)
            for k in range(KD):
                modulate(LOAD_A[k], 0, k)
                v.wait_ge(ada_used, k + 1)
            v.wait_ge(act_taken, A_VEC + 1)
            v.wait_ge(mod_full, 1)
            done(tt(modA[:], bank[7][:, 0:16], vecT[:, 0:16], ALU.add))
            stt(out=a1[:], in0=modA[:, 8:16], scalar=1.0, in1=vecT[:, 48:56], op0=ALU.add,
                op1=ALU.mult).then_inc(affine_ready, 1)

            for n in range(3 * IH):
                t, h = 1 + n // IH, n % IH
                w = (t + 1) * P
                o = score[:, SC_AT[t]:SC_AT[t] + w]
                v.wait_ge(act_taken, A_SC + n + 1)
                stt(out=o, in0=rel[:, n % 3, 0:w], scalar=iw[:, t, h:h + 1],
                    in1=future[:, S - w:S] if h == 0 else o, op0=ALU.mult, op1=ALU.add).then_inc(rel_added, 1)
                v.wait_ge(rel_added, n + 1)
            def lo(i, h):
                v.wait_ge(hi_ready, i * HALVES + (h + 1))
                w = h % HALVES // 2
                tt(w_lo[:, h % AHEAD, :], raw(w)[:, (h % 2) * HALF:(h % 2 + 1) * HALF],
                   w_hi[:, h % AHEAD, :].bitcast(F32), ALU.subtract).then_inc(lo_ready, 1)

            def x_rest(n, half):
                v.wait_ge(xhi_ready, n + 1)
                at = slice(4 * half, 4 * half + 4)
                tt(x_lo[:, at, :], xgT[:, at, :], x_hi[:, at, :].bitcast(F32), ALU.subtract).then_inc(xlo_ready, 1)

            for t in range(1, T):
                w = (t + 1) * P
                o = score[:, SC_AT[t]:SC_AT[t] + w]
                for r in range(N_SEL // 8):
                    n, rest = divmod((t - 1) * (N_SEL // 8) + r, B_EVERY)
                    if rest == B_EVERY - 1 and n < 2 * KD:
                        modulate(LOAD_B[n], 2048 * (n % 2), n // 2)
                    cur = o if r == 0 else work[:, 0:w]
                    done(nc.vector.max(mx8[:], cur))
                    done(nc.vector.match_replace(work[:, 0:w], mx8[:], cur, TAKEN))
                done(ts(work[:, 0:w], work[:, 0:w], -2.0e38, UNSEEN, ALU.is_ge, ALU.mult))
                done(tt(neg[:, NEG_AT[t]:NEG_AT[t] + w], work[:, 0:w], dist[:, S - w:S], ALU.add))
            done(ts(work[:, 0:P], future[:, 384:512], 0.0, UNSEEN, ALU.is_lt, ALU.mult))
            done(tt(neg[:, 0:P], work[:, 0:P], dist[:, 384:512], ALU.add))

            for t in range(T):
                v.wait_ge(rgsig_ready, t + 1)
                tt(rgs[:, t, :], dbank(D_RG + t)[:], rel[:, t % 2, :], ALU.mult).then_inc(dve_taken, 1)
            v.wait_ge(mod_full, 2)
            done(tt(modB[:], bank[7][:, 0:16], vecT[:, 24:40], ALU.add))
            stt(out=a2[:], in0=modB[:, 8:16], scalar=1.0, in1=vecT[:, 56:64], op0=ALU.add,
                op1=ALU.mult).then_inc(affine_ready, 1)
            v.wait_ge(g_bias_in, 32)
            for n in range(4):
                j = D_GROW + n
                v.wait_ge(dve_full, j + 1)
                tt(g_vals[:, n * 512:(n + 1) * 512], dbank(j)[0:1, :], g_bias[:, n * 512:(n + 1) * 512],
                   ALU.add).then_inc(dve_taken, 1)

            v.wait_ge(decay_ready, RH)
            for h in range(RH):
                if h >= 2:
                    v.wait_ge(ro_full, h - 1)
                for m in range(T):
                    j = D_RS + h * T + m
                    v.wait_ge(dve_full, j + 1)
                    tt(rs[:, h % 2, RS_AT[m]:RS_AT[m] + RS_W[m]], dbank(j)[:, 0:RS_W[m]],
                       decay[:, h, 0:RS_W[m]], ALU.mult).then_inc(dve_taken, 1)
            order = [(t, h) for t in range(T) for h in range(AH)]

            def rows(t):
                v.wait_ge(prob_ready, AH * (t + 1))
                done(nc.vector.reciprocal(pinv[:, :, t:t + 1], psum_[:, :, t:t + 1]))
                v.wait_ge(pv_full, AH * (t + 1))
                tt(att[:, t, :].rearrange("p (h d) -> p h d", h=AH),
                   bank[3 + 4 * (t % 2)][:].rearrange("p (h d) -> p h d", h=AH),
                   pinv[:, :, t:t + 1].broadcast_to((P, AH, HD)), ALU.mult).then_inc(pv_taken, 1)
            v.wait_ge(ro_full, RH)
            for n, (t, h) in enumerate(order):
                w = (t + 1) * P
                v.wait_ge(dve_full, D_QK + n + 1)
                if n >= 3:
                    v.wait_ge(prob_ready, n - 2)
                stt(out=lg[:, n % 3, 0:w], in0=neg[:, NEG_AT[t]:NEG_AT[t] + w], scalar=SLOPE[h],
                    in1=dbank(D_QK + n)[:, 0:w], op0=ALU.mult, op1=ALU.add).then_inc(dve_taken, 1)
                v.wait_ge(dve_taken, D_QK + n + 1)
                nc.vector.tensor_reduce(nmax[:, n % 4:n % 4 + 1], lg[:, n % 3, 0:w], AX.X, ALU.max,
                                        negate=True).then_inc(nmax_ready, 1)
                if n == AH:
                    v.wait_ge(ro_summed, 1)
                    done(nc.vector.reciprocal(ri[:], rt[:]))
                if n >= AH and n - AH < T * RH:
                    ret_t, ret_h = divmod(n - AH, RH)
                    o = rgs[:, ret_t, ret_h * P:(ret_h + 1) * P]
                    stt(out=o, in0=ro[:, ret_t, ret_h, :], scalar=ri[:, n - AH:n - AH + 1], in1=o,
                        op0=ALU.mult, op1=ALU.mult).then_inc(ret_ready, 1)
                if h == 4 and t >= 1:
                    rows(t - 1)
            rows(T - 1)

            v.wait_ge(g1_in, 16)
            for t in range(T):
                for q in range(2):
                    j = D_WO + 2 * t + q
                    o = xs[:, t, q * 512:(q + 1) * 512]
                    v.wait_ge(dve_full, j + 1)
                    tt(tmp, dbank(j)[:], g_row[:, q * 512:(q + 1) * 512], ALU.mult).then_inc(dve_taken, 1)
                    v.wait_ge(dve_taken, j + 1)
                    tt(o, o, tmp, ALU.add).then_inc(x2_ready, 1)
                    v.wait_ge(x2_ready, 2 * t + q + 1)
            v.wait_ge(rms_root, 2)
            nc.vector.reciprocal(ri[:, 0:T], rt[:, 0:T]).then_inc(rms_inv, 1)

            v.wait_ge(router_full, 1)
            v.wait_ge(late_consts, 1)
            done(tt(lgt, bank[3][:, 0:T * E].rearrange("p (t e) -> p t e", t=T),
                    rb[:].unsqueeze(1).broadcast_to((P, T, E)), ALU.add))
            for t in range(T):
                done(nc.vector.max(top8[:, t, :], lgt[:, t, :]))
            for t in range(T):
                done(nc.vector.max_index(idx8[:, t, :], top8[:, t, :], lgt[:, t, :]))
            tt(dgate[:], top8[:, :, 0:K], top8[:, :, 0:1].broadcast_to((P, T, K)), ALU.subtract).then_inc(gate_diff, 1)
            done(nc.vector.tensor_copy(idxf[:].rearrange("p (t k) -> p t k", t=T), idx8[:, :, 0:K]))
            done(tt(hot, iota_p[:, 0:E].unsqueeze(1).broadcast_to((P, T * K, E)),
                    idxf[:].unsqueeze(2).broadcast_to((P, T * K, E)), ALU.is_equal))
            nc.vector.tensor_reduce(hot32, hot.rearrange("p (t k) e -> p t e k", t=T), AX.X,
                                    ALU.add).then_inc(table_in, 1)
            v.wait_ge(gate_exp, 1)
            done(nc.vector.tensor_reduce(ss[:, 0:T], gates[:], AX.X, ALU.add))
            done(nc.vector.reciprocal(ri[:, 0:T], ss[:, 0:T]))
            done(tt(gates[:], gates[:], ri[:, 0:T].unsqueeze(2).broadcast_to((P, T, K)), ALU.mult))
            v.wait_ge(table_full, 1)
            done(nc.vector.tensor_copy(cum, bank[7][:, 0:T * E].rearrange("p (t e) -> p t e", t=T)))
            for t in range(T):
                done(tt(hotC[:, t * K:(t + 1) * K, :], hot[:, t * K:(t + 1) * K, :],
                        cum[:, t, :].unsqueeze(1).broadcast_to((P, K, E)), ALU.mult))
            done(nc.vector.tensor_reduce(rank[:], hotC, AX.X, ALU.add))
            done(ts(blk[:], rank[:], float(CAP), None, ALU.is_ge))
            for b in range(2, BLOCKS):
                done(stt(out=blk[:], in0=rank[:], scalar=float(CAP * b), in1=blk[:], op0=ALU.is_ge, op1=ALU.add))
            done(stt(out=rank[:], in0=blk[:], scalar=-float(CAP), in1=rank[:], op0=ALU.mult, op1=ALU.add))
            done(stt(out=blk[:], in0=blk[:], scalar=float(E), in1=idxf[:], op0=ALU.mult, op1=ALU.add))
            wide = (P, T * K, P)
            done(tt(isq, iota_p.unsqueeze(1).broadcast_to(wide), blk[:].unsqueeze(2).broadcast_to(wide),
                    ALU.is_equal))
            done(tt(isl, iota_p.unsqueeze(1).broadcast_to(wide), rank[:].unsqueeze(2).broadcast_to(wide),
                    ALU.is_equal))
            tt(isl, isl, tok4[:].unsqueeze(2).broadcast_to(wide), ALU.mult).then_inc(table_in, 1)
            v.wait_ge(bias_in, 16 * 6)
            done(nc.vector.tensor_copy(b_part, b_raw[0:96, :]))
            done(tt(b_raw[0:96, :], b_raw[0:96, :], b_part, ALU.subtract))
            done(nc.vector.tensor_copy(b_part[32:64, :], b_raw[32:64, :]))
            done(nc.vector.tensor_copy(b_part[64:96, :], b_raw[64:96, :]))
            done(tt(b_raw[64:96, :], b_raw[64:96, :], b_part[64:96, :], ALU.subtract))
            nc.vector.tensor_copy(b_part[64:96, :], b_raw[64:96, :]).then_inc(bias_ready, 1)
            for h in range(AHEAD):
                lo(0, h)
            v.wait_ge(table_full, 2)
            done(nc.vector.tensor_copy(tabT, bank[0][:, 0:P]))
            done(nc.vector.tensor_copy(tab, bank[1][:, 0:P]))
            done(nc.vector.tensor_reduce(pos[:], tab, AX.X, ALU.max))
            done(ts(flag[:], pos[:], 0.0, None, ALU.is_gt))
            nc.vector.memset(flag[0:E, :], 0.0).then_inc(table_in, 1)
            v.wait_ge(table_full, 3)
            done(nc.vector.tensor_copy(pos[:], bank[2][:, 0:1]))
            ts(sel16[:], iota_p[:, 0:16], pos[:, 0:1], flag[:, 0:1], ALU.is_equal, ALU.mult).then_inc(table_in, 1)
            v.wait_ge(table_full, 4)
            done(nc.vector.tensor_copy(dstf[:, 0:E], tabT[:, 0:E]))
            done(nc.vector.tensor_copy(dstf[:, E:48], bank[4][:, 0:16]))
            done(nc.vector.tensor_copy(hot96[:, 0:E], hot_first[0:96, :]))
            done(nc.vector.tensor_copy(hot96[:, E:48], bank[5][0:96, 0:16]))
            done(nc.vector.tensor_copy(over_i[:], bank[6][0:1, 0:17]))
            done(ts(empty, dstf, 0.0, float(8 * S), ALU.is_equal, ALU.mult))
            done(stt(out=dstf, in0=dstf, scalar=-1.0, in1=empty, op0=ALU.add, op1=ALU.add))
            done(nc.vector.tensor_copy(dst_i, dstf))
            for scratch in (pos, blk):
                nc.vector.memset(scratch[:], 0.0).then_inc(banks_free, 1)
            ts(tok_i, dst_i, 2, None, ALU.arith_shift_right).then_inc(tables_ready, 1)

            def item(i):
                def clip_gate(p):
                    v.wait_ge(half_used, i * HALVES + 8 * (p + 1))
                    ts(gc[:, p, :], bank[2 * p][:], LIMIT, None, ALU.min).then_inc(gate_ready, 1)
                    ts(uc[:, p, :], bank[2 * p + 1][:], LIMIT, -LIMIT, ALU.min, ALU.max).then_inc(banks_free, 1)

                def product(p):
                    v.wait_ge(banks_free, i * 2 + (p + 3))
                    stt(out=gu_[:, p, :], in0=uc[:, p, :], scalar=1.0, in1=gc[:, p, :], op0=ALU.add,
                        op1=ALU.mult).then_inc(prod_ready, 1)

                def activation(p):
                    v.wait_ge(prod_ready, i * 2 + (p + 1))
                    v.wait_ge(sig_ready, i * 2 + (p + 1))
                    tt(act[:, p * 512:(p + 1) * 512], gu_[:, p, :], sg[:, p, :], ALU.mult).then_inc(act_ready, 1)
                for h in range(AHEAD, 11):
                    lo(i, h)
                clip_gate(0)
                lo(i, 11)
                product(0)
                lo(i, 12)
                activation(0)
                for h in range(13, HALVES + 3):
                    lo(i, h)
                clip_gate(1)
                product(1)
                lo(i, HALVES + 3)
                activation(1)
                for half in range(2):
                    x_rest(i * 2 + 2 + half, half)

            for half in range(2):
                x_rest(half, half)
            with v.Fori(0, E) as i:
                item(i)
            n_over = v.value_load(over_i[0:1, 16:17], min_val=0, max_val=OVER)
            with v.If(n_over > 0):
                with v.Fori(E, ITEMS) as i:
                    item(i)

            v.wait_ge(last_rows_in, 32)
            for t in range(T):
                z = ring[:, t * 4096:(t + 1) * 4096].rearrange("p (k d) -> p k d", k=K)
                v.wait_ge(x_in[t], 32)
                done(ts(z[:, 0, :], z[:, 0, :], gates[:, t, 0:1], None, ALU.mult))
                for k in range(1, K):
                    done(stt(out=z[:, 0, :], in0=z[:, k, :], scalar=gates[:, t, k:k + 1], in1=z[:, 0, :],
                             op0=ALU.mult, op1=ALU.add))
                done(tt(z[:, 0, :], z[:, 0, :], g2_row, ALU.mult))
                tt(xs[:, t, :], xs[:, t, :], z[:, 0, :], ALU.add).then_inc(x3_ready, 1)
            for t in range(T):
                v.wait_ge(last_root, t + 1)
                done(nc.vector.reciprocal(ri[:, t:t + 1], rt[:, t:t + 1]))
                stt(out=xs[:, t, :], in0=xs[:, t, :], scalar=ri[:, t:t + 1], in1=fg_row, op0=ALU.mult,
                    op1=ALU.mult).then_inc(out_ready, 1)


_INS = ["x", "c", "ada_w", "ada_b", "norm1_g", "w_in", "mix_scale", "w_o", "norm2_g", "router_w",
        "router_b", "w_gu", "b_gu", "w_down", "b_down", "final_g"]
_OUTS = [((1, S, D), "float32")]


def kernel(**inputs):
    import concourse.bacc as bacc
    from concourse.bass_utils import run_bass_kernel_spmd as run

    nc = bacc.Bacc("TRN2", target_bir_lowering=False, num_devices=1)
    arrays, args = {}, []
    for name in _INS:
        a = np.ascontiguousarray(inputs[name])
        arrays[f"in_{name}"] = a
        args.append(nc.dram_tensor(f"in_{name}", a.shape, mybir.dt.from_np(a.dtype), kind="ExternalInput").ap())
    for i, (shape, dtype) in enumerate(_OUTS):
        args.append(nc.dram_tensor(f"out_{i}", shape, mybir.dt.from_np(np.dtype(dtype)),
                                   kind="ExternalOutput").ap())
    build(nc, *args)
    r = run(nc, [arrays], core_ids=[0])
    return r.results[0]["out_0"]
```

```python
import math
from contextlib import ExitStack

import numpy as np

import concourse.bass as bass
from concourse import mybir

ALU = mybir.AluOpType
ACT = mybir.ActivationFunctionType
AX = mybir.AxisListType
F32 = mybir.dt.float32
F32R = mybir.dt.float32r
BF16 = mybir.dt.bfloat16
I32 = mybir.dt.int32
U32 = mybir.dt.uint32

P = 128
D = 1024
S = 512
T = S // P
KD = D // P
EPS = 1e-6
RH, RDV = 4, 128
AH, AG, HD = 8, 2, 64
IH = 8
N_SEL = min(256, S // 4)
E = 32
K = 4
FE = 1024
LIMIT, ALPHA = 7.0, 1.702
CAP = P
BLOCKS = S // CAP
OVER = (S * K) // (CAP + 1)
ITEMS = E + OVER
MASKED, TAKEN = -1.0e38, -3.0e38
UNSEEN = -1.0e30
LOG_G = [math.log1p(-2.0 ** (-5 - h)) for h in range(RH)]
SLOPE = [2.0 ** (-8.0 * (h + 1) / AH) for h in range(AH)]
W_IDX = (HD ** -0.5) * (IH ** -0.5)

SLOTS, SLOT = 12, 2048
KEPT = 8
SEQUENCE = "A" * 8 + "WWWWBBBBWWBBWWBBBBWWBBBBWWBBOOOO"
LOAD_A, LOAD_W, LOAD_B, LOAD_O = [[n for n, m in enumerate(SEQUENCE) if m == which] for which in "AWBO"]
GU, DN = 8, 4
HALVES = 2 * GU
HALF = SLOT // 2
B_EVERY = 3
AHEAD = 4

A_VEC = 0
A_HT = A_VEC + 1
H_ACT = 5
A_IK = A_HT + H_ACT
A_IW = A_IK + 1
A_IQ = A_IW + 1
A_SC = A_IQ + 4
A_AK = A_SC + 3 * IH
A_AV = A_AK + 1
A_AQ = A_AV + 1
A_RQ = A_AQ + 4
A_RK = A_RQ + 2
A_RV = A_RK + 2
A_PT = A_RV + T
A_MIX = A_PT + T * AH
A_H2 = A_MIX + KD
D_RG = 0
D_GROW = D_RG + T
D_RS = D_GROW + 4
D_QK = D_RS + T * RH
D_WO = D_QK + T * AH
AFTER_MIX = [f"o{t}{q}" for t in range(T - 1) for q in range(2)] + ["l0", "o30", "c0", "l1", "o31"]
AFTER_MIX += ["c1", "l2", "l3", "c2", "c3"]
D_ = {name: D_WO + n for n, name in enumerate(AFTER_MIX)}


def build(nc, x, c, ada_w, ada_b, norm1_g, w_in, mix_scale, w_o, norm2_g, router_w, router_b,
          w_gu, b_gu, w_down, b_down, final_g, out):
    x = x.rearrange("b s d -> (b s) d")
    out = out.rearrange("b s d -> (b s) d")
    ada_w, w_in, w_o, router_w = ada_w[0], w_in[0], w_o[0], router_w[0]
    w_gu, b_gu, w_down, b_down = w_gu[0], b_gu[0], w_down[0], b_down[0]

    xn2_dram = nc.dram_tensor("xn2_rows", (S, D), F32, kind="Internal").ap()
    g_dram = nc.dram_tensor("g_rows", (2, D), F32, kind="Internal").ap()
    y_dram = nc.dram_tensor("expert_rows", (S * K, D), F32, kind="Internal").ap()

    ctx = ExitStack()
    with ctx:
        def sb(name, shape, dt=F32):
            return ctx.enter_context(nc.sbuf_tensor(name, shape, dt))

        def sem(name):
            return ctx.enter_context(nc.semaphore(name))

        bank = [ctx.enter_context(nc.psum_tensor(f"bank{i}", [P, 512], F32)) for i in range(8)]
        ring = sb("ring", [P, KEPT * SLOT])
        xs = sb("xs", [P, T, D])
        AREA = 18440
        area = sb("area", [P, AREA])

        def view(at, *dims):
            n = int(np.prod(dims))
            assert at + n <= AREA, (at, dims)
            v = area[:, at:at + n]
            if len(dims) == 2:
                v = v.rearrange("p (a b) -> p a b", a=dims[0])
            if len(dims) == 3:
                v = v.rearrange("p (a b c) -> p a b c", a=dims[0], b=dims[1])
            return v

        iqT = view(0, 4, S)
        rqT, rkT = view(0, 2, S), view(1024, 2, S)
        att = view(0, T, 512)
        ikT = view(2048, S)
        akT = view(2560, S)
        aqT = view(3072, 4, S)
        rv = view(5120, T, 512)
        rgs = view(7168, T, 512)
        av = view(9216, T, 128)
        iw = view(9728, T, IH)
        xn = view(3072, T, D)
        acc = view(9760, 4096)
        RS_W = [S - P * m for m in range(T)]
        RS_AT = [sum(RS_W[:m]) for m in range(T)]
        rs = view(9760, 2, sum(RS_W))
        lg = view(9760, 3, S)
        pr = view(9760 + 1536, 3, S)
        prT = view(9760 + 3072, 2, S)
        NEG_AT = [0, 128, 384, 768]
        neg = view(13856, 1280)
        rel = view(15136, 3, S)
        score = view(16672, 1152)
        SC_AT = [None, 0, 256, 640]
        work = view(17824, 512)
        decay = view(15136, RH, S)
        sq = view(17184, 512)
        g_row = view(17408, D)
        tmp = view(7168, 512)
        xn2 = view(0, T, D)
        rw = view(4096, KD, E)
        lgt = view(4352, T, E)
        isq = view(4608, 2 * K, P)
        isl = view(5632, 2 * K, P)
        xg = view(16384, D)
        xgT = view(1024, KD, P)
        gc = view(2048, 2, 512)
        uc = view(3072, 2, 512)
        gu_ = view(4096, 2, 512)
        sg = view(5120, 2, 512)
        act = view(6144, D)
        actT = view(7168, KD, P)
        ys = view(8192, D)
        diag = view(2048, T * (K - 1), P)
        g2_row = view(9216, D)
        fg_row = view(10240, D)
        b_raw = view(11264, 3 * D)
        b_part = view(14336, 3 * D // 2).bitcast(BF16)[0:96, :]

        ident = sb("ident", [P, P])
        ones = sb("ones", [P, P])
        dist = sb("dist", [P, S])
        future = sb("future", [P, S])
        iota_p = dist[:, 0:P]
        after = dist[:, P:2 * P]
        q_mod = dist[:, 2 * P:2 * P + 96]
        hot_first = dist[:, 2 * P:2 * P + E]
        vec_in = view(0, P)[0:72, :]
        eid = sb("eid", [P, 1])
        tok4 = sb("tok4", [P, T * K])
        epsc = sb("epsc", [P, 1])
        vecT = sb("vecT", [P, 72])
        cs = sb("cs", [P, KD])
        csig = sb("csig", [P, KD])
        sc_c = sb("sc_c", [P, KD])
        modA = sb("modA", [P, 16])
        modB = sb("modB", [P, 16])
        a1 = sb("a1", [P, KD])
        a2 = sb("a2", [P, KD])
        ss = sb("ss", [P, 16])
        rt = sb("rt", [P, 16])
        ri = sb("ri", [P, 16])
        mx8 = sb("mx8", [P, 8])
        nmax = sb("nmax", [P, 4])
        psum_ = sb("psum_", [P, AH, T])
        pinv = sb("pinv", [P, AH, T])
        rb = sb("rb", [P, E])
        top8 = sb("top8", [P, T, 8])
        idx8 = sb("idx8", [P, T, 8], U32)
        idxf = sb("idxf", [P, T * K])
        dgate = sb("dgate", [P, T, K])
        gates = sb("gates", [P, T, K])
        rank = sb("rank", [P, T * K])
        blk = sb("blk", [P, T * K])
        flag = sb("flag", [P, 1])
        pos = sb("pos", [P, 1])
        sel16 = sb("sel16", [P, 16])
        hot96 = sb("hot96", [96, 48], BF16)
        over_i = sb("over_i", [1, 17], I32)
        sel = sb("sel", [96, P], BF16)
        gidx = sb("gidx", [P, 1], U32)
        sidx = sb("sidx", [P, 1], U32)

        with ExitStack() as mixer:
            ring_end = mixer.enter_context(nc.sbuf_tensor("ring_end", [P, (SLOTS - KEPT) * SLOT], F32))
            hT = mixer.enter_context(nc.sbuf_tensor("hT", [P, KD, S], F32))
            ro = hT[:, 0:4, :].rearrange("p t (h e) -> p t h e", h=RH)
            g_vals, g_bias = ring_end[0:1, 2 * SLOT:3 * SLOT], ring_end[0:1, 3 * SLOT:4 * SLOT]
        w_hi = sb("w_hi", [P, AHEAD, HALF], F32R)
        w_lo = sb("w_lo", [P, AHEAD, HALF], F32R)
        x_hi = sb("x_hi", [P, KD, P], F32R)
        x_lo = sb("x_lo", [P, KD, P], F32R)
        routes = sb("routes", [P, 1728])
        hot = routes[:, 0:512].rearrange("p (n e) -> p n e", e=E)
        hotC = routes[:, 512:640].rearrange("p (n e) -> p n e", e=E)
        hot32 = routes[:, 1024:1152].rearrange("p (t e) -> p t e", e=E)
        tabT = routes[:, 1280:1408]
        tab = routes[:, 1408:1536]
        dstf, empty = routes[:, 1536:1584], routes[:, 1584:1632]
        dst_i, tok_i = routes[:, 1632:1680].bitcast(I32), routes[:, 1680:1728].bitcast(I32)

        consts_ready, late_consts = sem("consts_ready"), sem("late_consts")
        small_in, key_in, query_in = sem("small_in"), sem("key_in"), sem("query_in")
        x_in = [sem(f"x_in{t}") for t in range(T)]
        landed = [sem(f"landed{i}") for i in range(SLOTS)]
        gu_in = [sem(f"gu_in{i}") for i in range(4)]
        down_in = [sem(f"down_in{i}") for i in range(DN)]
        hi_ready, lo_ready, half_used = sem("hi_ready"), sem("lo_ready"), sem("half_used")
        down_used = sem("down_used")
        xhi_ready, xlo_ready = sem("xhi_ready"), sem("xlo_ready")
        ada_used = sem("ada_used")
        wo_used = sem("wo_used")
        act_full, act_taken = sem("act_full"), sem("act_taken")
        dve_full, dve_taken = sem("dve_full"), sem("dve_taken")
        dve_step, act_step, pool_step = sem("dve_step"), sem("act_step"), sem("pool_step")
        csig_ready = sem("csig_ready")
        rms_root, rms_inv = sem("rms_root"), sem("rms_inv")
        xn_ready, h_full, h_taken = sem("xn_ready"), sem("h_full"), sem("h_taken")
        mod_full = sem("mod_full")
        affine_ready = sem("affine_ready")
        rel_added, rgsig_ready = sem("rel_added"), sem("rgsig_ready")
        decay_raw, decay_ready = sem("decay_raw"), sem("decay_ready")
        g_bias_in, g_rows_ready, g_stored = sem("g_bias_in"), sem("g_rows_ready"), sem("g_stored")
        g1_in = sem("g1_in")
        ro_full, ro_taken, ro_summed, ret_ready = (sem("ro_full"), sem("ro_taken"), sem("ro_summed"),
                                                   sem("ret_ready"))
        nmax_ready, prob_ready, pv_full, pv_taken = (sem("nmax_ready"), sem("prob_ready"),
                                                     sem("pv_full"), sem("pv_taken"))
        x2_ready, xn2_ready, xn2_stored = sem("x2_ready"), sem("xn2_ready"), sem("xn2_stored")
        router_in = sem("router_in")
        hot_ready = sem("hot_ready")
        places_ready, places_used = sem("places_ready"), sem("places_used")
        table_in, table_full = sem("table_in"), sem("table_full")
        lists_ready = sem("lists_ready")
        gate_diff, gate_exp = sem("gate_diff"), sem("gate_exp")
        tables_ready, bias_in, bias_ready = sem("tables_ready"), sem("bias_in"), sem("bias_ready")
        gidx_ready, gathered = sem("gidx_ready"), sem("gathered")
        sidx_ready, scattered, sel_ready = sem("sidx_ready"), sem("scattered"), sem("sel_ready")
        turn_full, turn_taken = sem("turn_full"), sem("turn_taken")
        banks_free, gate_ready, sig_ready, act_ready = (sem("banks_free"), sem("gate_ready"),
                                                        sem("sig_ready"), sem("act_ready"))
        prod_ready, y_ready = sem("prod_ready"), sem("y_ready")
        all_scattered = sem("all_scattered")
        last_rows_in = sem("last_rows_in")
        y_in = [sem(f"y_in{n}") for n in range(2 * T)]
        diag_ready, sum_full, sum_taken = sem("diag_ready"), sem("sum_full"), sem("sum_taken")
        x3_ready, last_root, out_ready, out_done = (sem("x3_ready"), sem("last_root"),
                                                    sem("out_ready"), sem("out_done"))

        def slot(n):
            s = n % SLOTS
            if s >= KEPT:
                return ring_end[:, (s - KEPT) * SLOT:(s - KEPT + 1) * SLOT]
            return ring[:, s * SLOT:(s + 1) * SLOT]

        def abank(j):
            return bank[j % 3]

        def hbank(k):
            return bank[(A_HT + k) % 7]

        def dbank(j):
            return bank[3] if j == D_RG + T - 1 else bank[4 + j % 3]

        def wcols(n, width=256):
            return slot(n)[:, 0:KD * width].rearrange("p (k n) -> p k n", k=KD)

        def raw(w):
            return slot(w % 4)

        def rows_of(t):
            return ring[:, t * K * D:(t + 1) * K * D].rearrange("p (k d) -> p k d", k=K)

        def half_cols(n):
            return slice((n % 2) * 512, (n % 2) * 512 + 512)

        block = ctx.enter_context(nc.Block())

        @block.sync
        def _(sp):
            sp.dma_start(cs[:], c.rearrange("o (p k) -> p (o k)", p=P)).then_inc(small_in, 16)
            sp.dma_start(vec_in[0:48, :], ada_b.rearrange("o (j p) -> (o j) p", p=P)).then_inc(small_in, 16)
            sp.dma_start(vec_in[48:56, :], norm1_g.rearrange("o (j p) -> (o j) p", p=P)).then_inc(small_in, 16)
            sp.dma_start(vec_in[56:64, :], norm2_g.rearrange("o (j p) -> (o j) p", p=P)).then_inc(small_in, 16)
            sp.dma_start(vec_in[64:72, :], mix_scale.rearrange("o (j p) -> (o j) p", p=P)).then_inc(small_in, 16)
            for t in range(T):
                sp.dma_start(xs[:, t, :], x[t * P:(t + 1) * P, :]).then_inc(x_in[t], 16)

            def load(n, dst, src):
                sp.dma_start(dst, src).then_inc(landed[n % SLOTS], 16)

            ada = ada_w.rearrange("(p k) n -> p k n", k=KD)
            win = w_in.rearrange("(k p) n -> p k n", p=P)
            wo = w_o.rearrange("(k p) n -> p k n", p=P)
            WIN_COLS = [None, 2304, 2560, 2048, None, None, 0, 256, 1024, 1280, 512, 768]
            LAST = [A_IW, A_IQ + 1, A_IQ + 3, A_AV, A_AQ + 1, A_AQ + 3, A_RQ + 1, A_RK + 1]

            def slot_free(n):
                which = SEQUENCE[n]
                if which == "A":
                    sp.wait_ge(ada_used, LOAD_A.index(n) + 1)
                elif which == "B":
                    sp.wait_ge(ada_used, KD + LOAD_B.index(n) + 1)
                elif LOAD_W.index(n) >= len(LAST):
                    sp.wait_ge(dve_full, D_RG + T)
                else:
                    sp.wait_ge(act_full, LAST[LOAD_W.index(n)] + 1)

            def w_in_load(i, n):
                if i == 0:
                    d = wcols(n, 136)
                    sp.dma_start(d[:, :, 0:64], win[:, :, 2816:2880]).then_inc(key_in, 16)
                    sp.dma_start(d[:, :, 64:128], win[:, :, 2816:2880]).then_inc(key_in, 16)
                    load(n, d[:, :, 128:136], win[:, :, 2880:2888])
                elif i in (4, 5):
                    d = wcols(n)
                    for a in range(2):
                        for b in range(2):
                            at = 1536 + (4 * b + 2 * (i - 4) + a) * HD
                            q = sp.dma_start(d[:, :, (2 * a + b) * HD:(2 * a + b + 1) * HD],
                                             win[:, :, at:at + HD])
                            if (a, b) == (1, 1):
                                q.then_inc(landed[n % SLOTS], 16)
                            else:
                                q.then_inc(query_in, 16)
                else:
                    at = WIN_COLS[i]
                    load(n, wcols(n), win[:, :, at:at + 256])

            for n, which in enumerate(SEQUENCE):
                if n >= SLOTS:
                    slot_free(n - SLOTS)
                if which == "A":
                    k = LOAD_A.index(n)
                    load(n, slot(n), ada[:, k, 0:2048])
                elif which == "W":
                    w_in_load(LOAD_W.index(n), n)
                elif which == "B":
                    k, half = divmod(LOAD_B.index(n), 2)
                    load(n, slot(n), ada[:, k, 2048 * (half + 1):2048 * (half + 2)])
                else:
                    i = LOAD_O.index(n)
                    load(n, slot(n).rearrange("p (k n) -> p k n", k=2), wo[:, 2 * i:2 * i + 2, :])

            def gu_chunk(w, e):
                half, k4, g = w // 4, (w // 2) % 2, w % 2
                src = w_gu[e, 4 * k4 * P:(4 * k4 + 4) * P, g * FE + half * 512:g * FE + half * 512 + 512]
                sp.dma_start(raw(w).rearrange("p (k n) -> p k n", k=4),
                             src.rearrange("(k p) n -> p k n", p=P)).then_inc(gu_in[w % 4], 16)

            def down_chunk(q, e):
                src = w_down[e, 2 * q * P:(2 * q + 2) * P, :].rearrange("(k p) n -> p k n", p=P)
                sp.dma_start(slot(4 + q).rearrange("p (k n) -> p k n", k=2), src).then_inc(down_in[q], 16)

            for q in range(DN):
                slot_free(len(SEQUENCE) + q - SLOTS)
                down_chunk(q, 0)
            for w in range(4):
                if w < 3:
                    sp.wait_ge(wo_used, w + 1)
                else:
                    sp.wait_ge(dve_full, D_["o31"] + 1)
                gu_chunk(w, 0)

            def gu_later(w, i, e):
                sp.wait_ge(lo_ready, i * HALVES + (2 * (w - 4) + 2))
                gu_chunk(w % GU, e)

            def down_later(q, i, e):
                sp.wait_ge(down_used, i * DN + (q + 1 - DN))
                down_chunk(q, e)

            def item(i, e, e_next, ahead):
                gu_later(4, i, e)
                gu_later(5, i, e)
                for q in range(DN):
                    down_later(q, i, e)
                gu_later(6, i, e)
                gu_later(7, i, e)
                for w in range(ahead):
                    gu_later(w + GU, i, e_next)

            for w in range(4, GU):
                gu_later(w, 0, 0)
            for w in range(4):
                gu_later(w + GU, 0, 1)
            with sp.Fori(1, E - 1) as i:
                item(i, i, i + 1, 4)
            sp.wait_ge(tables_ready, 1)
            n_over = sp.value_load(over_i[0:1, 16:17], min_val=0, max_val=OVER)
            e32 = sp.value_load(over_i[0:1, 0:1], min_val=0, max_val=E - 1)
            item(E - 1, E - 1, e32, 2)
            with sp.If(n_over > 0):
                for w in range(2, 4):
                    gu_later(w + GU, E - 1, e32)
                with sp.Fori(E, ITEMS) as i:
                    e = sp.value_load(over_i[0:1, bass.ds(i - E, 1)], min_val=0, max_val=E - 1)
                    e_next = sp.value_load(over_i[0:1, bass.ds(i - (E - 1), 1)], min_val=0, max_val=E - 1)
                    item(i, e, e_next, 4)
                for w in range(2, 4):
                    sp.wait_ge(gu_in[w], 16 * (2 * ITEMS + 1))
            sp.wait_ge(all_scattered, 1)
            for n in range(2 * T):
                t, cols = n // 2, half_cols(n)
                sp.dma_start(rows_of(t)[:, :, cols], y_dram[t * P * K:(t + 1) * P * K, cols]
                             .rearrange("(p k) d -> p k d", k=K)).then_inc(y_in[n], 16)
            for n in range(2 * T):
                t, cols = n // 2, half_cols(n)
                sp.wait_ge(out_ready, n + 1)
                sp.dma_start(out[t * P:(t + 1) * P, cols], xs[:, t, cols]).then_inc(out_done, 16)
            sp.wait_ge(out_done, 16 * 2 * T)

        @block.gpsimd
        def _(pool):
            steps = [0]

            def done(ins):
                steps[0] += 1
                ins.then_inc(pool_step, 1)
                pool.wait_ge(pool_step, steps[0])

            done(nc.gpsimd.memset(ones[:], 1.0))
            done(nc.gpsimd.memset(epsc[:], EPS))
            done(nc.gpsimd.memset(future[:], 0.0))
            done(nc.gpsimd.affine_select(out=ident[:], in_=ones[:], compare_op=ALU.is_equal, fill=0.0, base=0,
                                         pattern=[[1, P]], channel_multiplier=-1))
            done(nc.gpsimd.affine_select(out=future[:, 384:512], in_=future[:, 384:512], compare_op=ALU.is_ge,
                                         fill=MASKED, base=0, pattern=[[-1, P]], channel_multiplier=1))
            done(nc.gpsimd.iota(dist[:], pattern=[[1, S]], base=-384, channel_multiplier=-1,
                                allow_small_or_imprecise_dtypes=True))
            done(nc.gpsimd.iota(tok4[:], pattern=[[P * K, T], [1, K]], base=1, channel_multiplier=K,
                                allow_small_or_imprecise_dtypes=True))
            for b in range(4):
                done(nc.gpsimd.iota(eid[32 * b:32 * b + 32, :], pattern=[[0, 1]], base=0, channel_multiplier=1,
                                    allow_small_or_imprecise_dtypes=True))
            nc.gpsimd.memset(flag[0:32, :], 0.0).then_inc(consts_ready, 1)

            pool.wait_ge(ada_used, 3 * KD)
            pool.dma_start(g_bias[:, 0:D], ada_b[0:1, 2 * D:3 * D]).then_inc(g_bias_in, 16)
            pool.dma_start(g_bias[:, D:2 * D], ada_b[0:1, 5 * D:6 * D]).then_inc(g_bias_in, 16)

            pool.wait_ge(dve_taken, D_RG + T)
            nc.gpsimd.iota(decay[:, RH - 1, :], pattern=[[1, S]], base=0, channel_multiplier=-1,
                           allow_small_or_imprecise_dtypes=True).then_inc(decay_raw, 1)
            for h in range(RH):
                pool.wait_ge(decay_raw, 2 + h)
                nc.gpsimd.affine_select(out=decay[:, h, 0:P], in_=decay[:, h, 0:P], compare_op=ALU.is_ge, fill=0.0,
                                        base=0, pattern=[[1, P]], channel_multiplier=-1).then_inc(decay_ready, 1)
            done(nc.gpsimd.affine_select(out=after, in_=ones[:], compare_op=ALU.is_gt, fill=0.0, base=0,
                                         pattern=[[1, P]], channel_multiplier=-1))
            done(nc.gpsimd.iota(iota_p, pattern=[[1, P]], base=0, channel_multiplier=0,
                                allow_small_or_imprecise_dtypes=True))
            done(nc.gpsimd.memset(q_mod, 0.0))
            for off in (-64, -32, 0, 32, 64, 96):
                done(nc.gpsimd.affine_select(out=q_mod, in_=q_mod, compare_op=ALU.not_equal, fill=1.0,
                                             base=off, pattern=[[1, 96]], channel_multiplier=-1))
            nc.gpsimd.memset(flag[0:32, :], 0.0).then_inc(late_consts, 1)
            pool.wait_ge(dve_taken, D_GROW + 4)
            pool.dma_start(g_dram.rearrange("(o a) d -> o (a d)", o=1), g_vals).then_inc(g_stored, 16)
            pool.wait_ge(g_stored, 16)
            pool.wait_ge(ro_summed, 1)
            pool.dma_start(g_row, g_dram[0].partition_broadcast(P)).then_inc(g1_in, 16)

            pool.wait_ge(act_taken, A_MIX + KD)
            pool.dma_start(rw, router_w.rearrange("(k p) e -> p k e", p=P)).then_inc(router_in, 16)
            pool.dma_start(rb[:], router_b[0].partition_broadcast(P)).then_inc(router_in, 16)
            for j in range(3):
                pool.dma_start(b_raw[32 * j:32 * j + 32, 0:2048], b_gu).then_inc(bias_in, 16)
                pool.dma_start(b_raw[32 * j:32 * j + 32, 2048:3072], b_down).then_inc(bias_in, 16)
            done(nc.gpsimd.memset(xg, 0.0))
            pool.dma_start(g2_row, g_dram[1].partition_broadcast(P)).then_inc(last_rows_in, 16)
            pool.dma_start(fg_row, final_g.partition_broadcast(P)).then_inc(last_rows_in, 16)

            for t in range(T):
                pool.wait_ge(xn2_ready, t + 1)
                pool.dma_start(xn2_dram[t * P:(t + 1) * P, :], xn2[:, t, :]).then_inc(xn2_stored, 16)
            pool.wait_ge(xn2_stored, 16 * T)
            pool.wait_ge(lists_ready, 1)

            last_token, last_row = pool.to_reg(S - 1), pool.to_reg(S * K - 1)

            def gather():
                pool.indirect_dma_start(out=xg, out_offset=None, in_=xn2_dram,
                                        in_offset=bass.IndirectOffsetOnAxis(ap=gidx[:, 0:1], axis=0),
                                        bounds_check=last_token, oob_is_err=False).then_inc(gathered, 16)

            pool.tensor_copy(gidx[:].bitcast(I32), tok_i[:, 0:1]).then_inc(gidx_ready, 1)
            pool.wait_ge(gidx_ready, 1)
            gather()
            pool.sem_clear(gidx_ready)
            pool.tensor_copy(sel[:], hot96[:, 0:1].broadcast_to((96, P))).then_inc(sel_ready, 1)

            def item(i):
                nxt = pool.snap(i + 1)
                pool.wait_ge(turn_full, i * 4 + 2)
                pool.wait_ge(gathered, i * 16 + 16)
                pool.tensor_copy(gidx[:].bitcast(I32), tok_i[:, bass.ds(nxt, 1)]).then_inc(gidx_ready, 1)
                pool.wait_ge(gidx_ready, 1)
                gather()
                pool.sem_clear(gidx_ready)
                pool.wait_ge(down_used, i * DN + 1)
                pool.tensor_copy(sel[:], hot96[:, bass.ds(nxt, 1)].broadcast_to((96, P))).then_inc(sel_ready, 1)
                pool.wait_ge(y_ready, i + 1)
                pool.tensor_copy(sidx[:].bitcast(I32), dst_i[:, bass.ds(i, 1)]).then_inc(sidx_ready, 1)
                pool.wait_ge(sidx_ready, 1)
                pool.indirect_dma_start(out=y_dram,
                                        out_offset=bass.IndirectOffsetOnAxis(ap=sidx[:, 0:1], axis=0),
                                        in_=ys, in_offset=None,
                                        bounds_check=last_row, oob_is_err=False).then_inc(scattered, 16)
                pool.sem_clear(sidx_ready)
                pool.wait_ge(scattered, i * 16 + 16)

            with pool.Fori(0, E) as i:
                item(i)
            n_over = pool.value_load(over_i[0:1, 16:17], min_val=0, max_val=OVER)
            with pool.If(n_over > 0):
                with pool.Fori(E, ITEMS) as i:
                    item(i)
            nc.gpsimd.memset(sidx[:], 0).then_inc(all_scattered, 1)

        @block.scalar
        def _(a):
            steps = [0]

            def done(ins):
                steps[0] += 1
                ins.then_inc(act_step, 1)
                a.wait_ge(act_step, steps[0])

            def copy(dst, src, scale=1.0):
                return nc.scalar.activation(dst, src, ACT.Copy, scale=scale)

            def affine(dst, src, scale, bias):
                return nc.scalar.activation(dst, src, ACT.Identity, scale=scale, bias=bias)

            a.wait_ge(small_in, 16 * 5)
            nc.scalar.activation(csig[:], cs[:], ACT.Sigmoid).then_inc(csig_ready, 1)
            for t in range(T):
                a.wait_ge(x_in[t], 16)
                done(nc.scalar.activation(xn[:, t, :], xs[:, t, :], ACT.Square, accum_out=ss[:, t:t + 1]))
            a.wait_ge(consts_ready, 1)
            nc.scalar.activation(rt[:, 0:T], ss[:, 0:T], ACT.Sqrt, scale=1.0 / D, bias=epsc[:]).then_inc(rms_root, 1)
            a.wait_ge(rms_inv, 1)
            for t in range(T):
                copy(xn[:, t, :], xs[:, t, :], ri[:, t:t + 1]).then_inc(xn_ready, 1)
            j = A_VEC
            a.wait_ge(act_full, j + 1)
            copy(vecT[:], abank(j)[:, 0:72]).then_inc(act_taken, 1)
            a.wait_ge(affine_ready, 1)
            for k in range(H_ACT):
                j = A_HT + k
                a.wait_ge(act_full, j + 1)
                affine(hT[:, k, :], hbank(k)[:], a1[:, k:k + 1], modA[:, k:k + 1]).then_inc(act_taken, 1)

            def take(j, dst, scale=1.0, src=None):
                a.wait_ge(act_full, j + 1)
                copy(dst, abank(j)[:] if src is None else src, scale).then_inc(act_taken, 1)

            take(A_IK, ikT)
            take(A_IW, iw, W_IDX, abank(A_IW)[:, 0:T * IH].rearrange("p (t h) -> p t h", t=T))
            for m in range(4):
                take(A_IQ + m, iqT[:, m, :])
            for n in range(3 * IH):
                t = 1 + n // IH
                a.wait_ge(act_full, A_SC + n + 1)
                if n >= 3:
                    a.wait_ge(rel_added, n - 2)
                nc.scalar.activation(rel[:, n % 3, 0:(t + 1) * P], abank(A_SC + n)[:, 0:(t + 1) * P],
                                     ACT.Relu).then_inc(act_taken, 1)
            take(A_AK, akT)
            take(A_AV, av, 1.0, abank(A_AV)[:].rearrange("p (t n) -> p t n", t=T))
            for m in range(4):
                take(A_AQ + m, aqT[:, m, :], HD ** -0.5)
            for m in range(2):
                take(A_RQ + m, rqT[:, m, :])
            for m in range(2):
                take(A_RK + m, rkT[:, m, :], HD ** -0.5)
            a.wait_ge(rel_added, 3 * IH)
            for t in range(T):
                a.wait_ge(dve_full, D_RG + t + 1)
                if t >= 2:
                    a.wait_ge(dve_taken, D_RG + t - 1)
                nc.scalar.activation(rel[:, t % 2, :], dbank(D_RG + t)[:], ACT.Sigmoid).then_inc(rgsig_ready, 1)
            for t in range(2):
                take(A_RV + t, rv[:, t, :])
            a.wait_ge(decay_raw, 1)
            for h in range(RH):
                nc.scalar.activation(decay[:, h, :], decay[:, RH - 1, :], ACT.Exp,
                                     scale=LOG_G[h]).then_inc(decay_raw, 1)
            for t in range(2, T):
                take(A_RV + t, rv[:, t, :])
            for h in range(RH):
                b = bank[3 + 4 * (h % 2)]
                a.wait_ge(ro_full, h + 1)
                for n in range(T):
                    done(nc.scalar.activation(sq[:, 0:P], b[:, n * P:(n + 1) * P], ACT.Square,
                                              accum_out=ss[:, n * RH + h:n * RH + h + 1]))
                copy(ro[:, :, h, :], b[:].rearrange("p (t e) -> p t e", t=T)).then_inc(ro_taken, 1)


            order = [(t, h) for t in range(T) for h in range(AH)]

            def probs(n):
                t, h = order[n]
                w = (t + 1) * P
                a.wait_ge(nmax_ready, n + 1)
                if n >= 3:
                    a.wait_ge(act_full, A_PT + n - 3 + 1)
                nc.scalar.activation(pr[:, n % 3, 0:w], lg[:, n % 3, 0:w], ACT.Exp, bias=nmax[:, n % 4:n % 4 + 1],
                                     accum_out=psum_[:, h, t:t + 1]).then_inc(prob_ready, 1)

            def turned(n):
                w = (order[n][0] + 1) * P
                j = A_PT + n
                a.wait_ge(act_full, j + 1)
                if n >= 2:
                    a.wait_ge(pv_full, n - 1)
                copy(prT[:, n % 2, 0:w], abank(j)[:, 0:w]).then_inc(act_taken, 1)
            for n in range(len(order) + 1):
                if n == AH // 2:
                    nc.scalar.activation(rt[:], ss[:], ACT.Sqrt, scale=1.0 / RDV, bias=epsc[:]).then_inc(ro_summed, 1)
                if n < len(order):
                    probs(n)
                if n >= 1:
                    turned(n - 1)

            for k in range(KD):
                j = A_MIX + k
                a.wait_ge(act_full, j + 1)
                copy(hT[:, k, :], abank(j)[:], vecT[:, 64 + k:65 + k]).then_inc(act_taken, 1)
            def normal(t):
                a.wait_ge(x2_ready, 2 * t + 2)
                done(nc.scalar.activation(xn2[:, t, :], xs[:, t, :], ACT.Square, accum_out=ss[:, t:t + 1]))
                nc.scalar.activation(rt[:, t:t + 1], ss[:, t:t + 1], ACT.Sqrt, scale=1.0 / D,
                                     bias=epsc[:]).then_inc(rms_root, 1)
                a.wait_ge(rms_inv, 2 + t)
                copy(xn2[:, t, :], xs[:, t, :], ri[:, t:t + 1]).then_inc(xn2_ready, 1)

            def h2(t):
                for half in range(2):
                    j = A_H2 + 2 * t + half
                    a.wait_ge(act_full, j + 1)
                    for q in range(4):
                        k = 4 * half + q
                        last = affine(hT[:, k, t * P:(t + 1) * P], abank(j)[:, q * P:(q + 1) * P], a2[:, k:k + 1],
                                      modB[:, k:k + 1])
                    last.then_inc(act_taken, 1)
            normal(0)
            normal(1)
            h2(0)
            h2(1)
            normal(2)
            h2(2)
            normal(3)
            h2(3)

            def turn(u, dst, bank_no, scales=None):
                a.wait_ge(turn_full, u + 1)
                if scales is None:
                    copy(dst, bank[bank_no][:].rearrange("p (k n) -> p k n", k=4)).then_inc(turn_taken, 1)
                    return
                for q in range(4):
                    k = scales + q
                    last = affine(dst[:, q, :], bank[bank_no][:, q * P:(q + 1) * P], a2[:, k:k + 1],
                                  modB[:, k:k + 1])
                last.then_inc(turn_taken, 1)

            def hi(i, h):
                w = h % HALVES // 2
                if h % 2 == 0:
                    a.wait_ge(gu_in[w % 4], i * 32 + (16 * (h // 8) + 16))
                if not (isinstance(i, int) and i == 0 and h < AHEAD):
                    a.wait_ge(half_used, i * HALVES + (h + 1 - AHEAD))
                copy(w_hi[:, h % AHEAD, :], raw(w)[:, (h % 2) * HALF:(h % 2 + 1) * HALF]).then_inc(hi_ready, 1)

            def x_turn(u, n, bank_no, half):
                turn(u, xgT[:, 4 * half:4 * half + 4, :], bank_no, 4 * half)
                a.wait_ge(turn_taken, u + 1)
                copy(x_hi[:, 4 * half:4 * half + 4, :], xgT[:, 4 * half:4 * half + 4, :]).then_inc(xhi_ready, 1)

            def item(i):
                def sigmoid(p):
                    a.wait_ge(gate_ready, i * 2 + (p + 1))
                    nc.scalar.activation(sg[:, p, :], gc[:, p, :], ACT.Sigmoid, scale=ALPHA).then_inc(sig_ready, 1)
                for h in range(AHEAD, 12):
                    hi(i, h)
                sigmoid(0)
                for h in range(12, HALVES + 3):
                    hi(i, h)
                turn(i * 4 + 2, actT[:, 0:4, :], 6)
                sigmoid(1)
                hi(i, HALVES + 3)
                x_turn(i * 4 + 3, i * 2 + 2, 7, 0)
                turn(i * 4 + 4, actT[:, 4:8, :], 6)
                x_turn(i * 4 + 5, i * 2 + 3, 7, 1)
                a.wait_ge(down_used, i * DN + DN)
                a.wait_ge(sel_ready, i + 2)
                copy(ys[:, 0:512], bank[4][:])
                copy(ys[:, 512:1024], bank[5][:]).then_inc(y_ready, 1)

            for h in range(AHEAD):
                hi(0, h)
            x_turn(0, 0, 6, 0)
            x_turn(1, 1, 7, 1)
            a.wait_ge(gate_diff, 1)
            nc.scalar.activation(gates[:], dgate[:], ACT.Exp).then_inc(gate_exp, 1)
            a.wait_ge(tables_ready, 1)
            with a.Fori(0, E) as i:
                item(i)
            n_over = a.value_load(over_i[0:1, 16:17], min_val=0, max_val=OVER)
            with a.If(n_over > 0):
                with a.Fori(E, ITEMS) as i:
                    item(i)

            for t in range(T):
                a.wait_ge(x3_ready, 2 * t + 2)
                done(nc.scalar.activation(rows_of(t)[:, 1, :], xs[:, t, :], ACT.Square, accum_out=ss[:, t:t + 1]))
                nc.scalar.activation(rt[:, t:t + 1], ss[:, t:t + 1], ACT.Sqrt, scale=1.0 / D,
                                     bias=epsc[:]).then_inc(last_root, 1)

        @block.tensor
        def _(pe):
            def free(j):
                if j >= 3:
                    pe.wait_ge(act_taken, j - 2)

            def dfree(j):
                if j >= 3 and j != D_RG + T - 1:
                    pe.wait_ge(dve_taken, j - 2)

            def have(n):
                pe.wait_ge(landed[n % SLOTS], 16 * (n // SLOTS + 1))

            pe.wait_ge(consts_ready, 1)
            pe.wait_ge(small_in, 16 * 5)
            pe.transpose(abank(A_VEC)[:, 0:72], vec_in, ident[0:72, 0:72]).then_inc(act_full, 1)

            pe.wait_ge(xn_ready, T)
            for k in range(KD):
                if k == KD - 2:
                    pe.wait_ge(act_taken, A_VEC + 1)
                if k == KD - 1:
                    pe.wait_ge(ada_used, KD)
                    for m in range(16):
                        mm = pe.matmul(bank[7][:, m:m + 1], acc[:, m * P:(m + 1) * P], ones[:, 0:1], start=True,
                                       stop=True)
                    mm.then_inc(mod_full, 1)
                    pe.wait_ge(act_taken, A_HT + 1)
                for t in range(T):
                    mm = pe.transpose(hbank(k)[:, t * P:(t + 1) * P], xn[:, t, k * P:(k + 1) * P], ident[:])
                mm.then_inc(act_full if k < H_ACT else h_full, 1)

            def by_feature(j, w, at):
                free(j)
                for k in range(KD):
                    mm = pe.matmul(abank(j)[:], w[:, k, at:at + P], hT[:, k, :], start=(k == 0), stop=(k == KD - 1))
                mm.then_inc(act_full, 1)

            pe.wait_ge(act_taken, A_HT + H_ACT)
            pe.wait_ge(h_taken, KD - H_ACT)
            pe.wait_ge(key_in, 32)
            have(LOAD_W[0])
            w = wcols(LOAD_W[0], 136)
            by_feature(A_IK, w, 0)
            free(A_IW)
            for t in range(T):
                for k in range(KD):
                    mm = pe.matmul(abank(A_IW)[:, t * IH:(t + 1) * IH], hT[:, k, t * P:(t + 1) * P],
                                   w[:, k, 128:136], start=(k == 0), stop=(k == KD - 1))
            mm.then_inc(act_full, 1)
            for m in range(4):
                if m % 2 == 0:
                    have(LOAD_W[1 + m // 2])
                by_feature(A_IQ + m, wcols(LOAD_W[1 + m // 2]), (m % 2) * P)
            pe.wait_ge(act_taken, A_IQ + 4)
            for n in range(3 * IH):
                t, h = 1 + n // IH, n % IH
                j = A_SC + n
                lo = HD * (h % 2)
                free(j)
                pe.matmul(abank(j)[:, 0:(t + 1) * P], iqT[lo:lo + HD, h // 2, t * P:(t + 1) * P],
                          ikT[lo:lo + HD, 0:(t + 1) * P], start=True, stop=True).then_inc(act_full, 1)
            have(LOAD_W[3])
            w = wcols(LOAD_W[3])
            by_feature(A_AK, w, 0)
            free(A_AV)
            for t in range(T):
                for k in range(KD):
                    mm = pe.matmul(abank(A_AV)[:, t * P:(t + 1) * P], hT[:, k, t * P:(t + 1) * P],
                                   w[:, k, P:2 * P], start=(k == 0), stop=(k == KD - 1))
            mm.then_inc(act_full, 1)
            pe.wait_ge(query_in, 16 * 6)
            for first, n in ((A_AQ, LOAD_W[4]), (A_AQ + 2, LOAD_W[5]), (A_RQ, LOAD_W[6]), (A_RK, LOAD_W[7])):
                have(n)
                for m in range(2):
                    by_feature(first + m, wcols(n), m * P)
            for first, n in ((None, LOAD_W[8]), (A_RV, LOAD_W[10])):
                have(n)
                have(n + 1)
                s0 = n % SLOTS
                both = ring_end[:, (s0 - KEPT) * SLOT:(s0 - KEPT + 2) * SLOT] if s0 >= KEPT else \
                    ring[:, s0 * SLOT:(s0 + 2) * SLOT]
                w2 = both.rearrange("p (s k n) -> p k s n", s=2, k=KD)
                for t in range(T):
                    if first is None:
                        b = dbank(D_RG + t)
                        dfree(D_RG + t)
                    else:
                        b = abank(first + t)
                        free(first + t)
                    for k in range(KD):
                        mm = pe.matmul(b[:].rearrange("p (s n) -> p s n", s=2), hT[:, k, t * P:(t + 1) * P],
                                       w2[:, k], start=(k == 0), stop=(k == KD - 1))
                    mm.then_inc(act_full if first is not None else dve_full, 1)

            pe.wait_ge(ada_used, 3 * KD)
            for m in range(16):
                mm = pe.matmul(bank[7][:, m:m + 1], acc[:, 1024 + m * P:1024 + (m + 1) * P], ones[:, 0:1],
                               start=True, stop=True)
            mm.then_inc(mod_full, 1)
            for n, at in enumerate((0, 512, 3072, 3584)):
                j = D_GROW + n
                dfree(j)
                pe.matmul(dbank(j)[0:1, :], ones[:, 0:1], acc[:, at:at + 512], start=True,
                          stop=True).then_inc(dve_full, 1)

            pe.wait_ge(act_taken, A_RV + T)
            for h in range(RH):
                lo = HD * (h % 2)
                for m in range(T):
                    j = D_RS + h * T + m
                    dfree(j)
                    pe.matmul(dbank(j)[:, 0:RS_W[m]], rkT[lo:lo + HD, h // 2, m * P:(m + 1) * P],
                              rqT[lo:lo + HD, h // 2, m * P:S], start=True, stop=True).then_inc(dve_full, 1)
                b = bank[3 + 4 * (h % 2)]
                if h >= 2:
                    pe.wait_ge(ro_taken, h - 1)
                elif h == 1:
                    pe.wait_ge(affine_ready, 2)
                pe.wait_ge(dve_taken, D_RS + h * T + T)
                for n in range(T):
                    for m in range(n + 1):
                        at = RS_AT[m] + (n - m) * P
                        mm = pe.matmul(b[:, n * P:(n + 1) * P], rs[:, h % 2, at:at + P],
                                       rv[:, m, h * P:(h + 1) * P], start=(m == 0), stop=(m == n))
                mm.then_inc(ro_full, 1)

            order = [(t, h) for t in range(T) for h in range(AH)]

            def logits(n):
                t, h = order[n]
                lo = HD * (h // 4)
                dfree(D_QK + n)
                pe.matmul(dbank(D_QK + n)[:, 0:(t + 1) * P], aqT[lo:lo + HD, h % 4, t * P:(t + 1) * P],
                          akT[lo:lo + HD, 0:(t + 1) * P], start=True, stop=True).then_inc(dve_full, 1)

            def turn_probs(n):
                t, h = order[n]
                free(A_PT + n)
                pe.wait_ge(prob_ready, n + 1)
                for m in range(t + 1):
                    mm = pe.transpose(abank(A_PT + n)[:, m * P:(m + 1) * P], pr[:, n % 3, m * P:(m + 1) * P],
                                      ident[:])
                mm.then_inc(act_full, 1)

            def values(n):
                t, h = order[n]
                if h == 0 and t >= 2:
                    pe.wait_ge(pv_taken, t - 1)
                if n == 0:
                    pe.wait_ge(ro_taken, RH)
                pe.wait_ge(act_taken, A_PT + n + 1)
                g = h // 4
                for m in range(t + 1):
                    mm = pe.matmul(bank[3 + 4 * (t % 2)][:, h * HD:(h + 1) * HD], prT[:, n % 2, m * P:(m + 1) * P],
                                   av[:, m, g * HD:(g + 1) * HD], start=(m == 0), stop=(m == t))
                mm.then_inc(pv_full, 1)
            for n in range(len(order) + 3):
                if n < len(order):
                    logits(n)
                if 2 <= n < len(order) + 2:
                    turn_probs(n - 2)
                if n >= 3:
                    values(n - 3)

            for k in range(KD):
                j = A_MIX + k
                free(j)
                if k == 0:
                    pe.wait_ge(ret_ready, T * RH)
                if k == 4:
                    pe.wait_ge(pv_taken, T)
                for t in range(T):
                    src = rgs[:, t, k * P:(k + 1) * P] if k < 4 else att[:, t, (k - 4) * P:(k - 3) * P]
                    mm = pe.transpose(abank(j)[:, t * P:(t + 1) * P], src, ident[:])
                mm.then_inc(act_full, 1)
            pe.wait_ge(act_taken, A_MIX + KD)

            def mixed(t, q):
                j = D_[f"o{t}{q}"]
                dfree(j)
                for k in range(KD):
                    n = LOAD_O[k // 2]
                    if (t, q) == (0, 0) and k % 2 == 0:
                        have(n)
                    w = slot(n).rearrange("p (k n) -> p k n", k=2)
                    mm = pe.matmul(dbank(j)[:], hT[:, k, t * P:(t + 1) * P], w[:, k % 2, q * 512:(q + 1) * 512],
                                   start=(k == 0), stop=(k == KD - 1))
                    if (t, q) == (T - 1, 1) and k % 2 == 1 and k < KD - 1:
                        mm.then_inc(wo_used, 1)
                mm.then_inc(dve_full, 1)

            def turn_rows(t):
                pe.wait_ge(xn2_ready, t + 1)
                for half in range(2):
                    j = A_H2 + 2 * t + half
                    free(j)
                    for q in range(4):
                        mm = pe.transpose(abank(j)[:, q * P:(q + 1) * P], xn2[:, t, (4 * half + q) * P:(4 * half + q + 1) * P],
                                          ident[:])
                    mm.then_inc(act_full, 1)

            def router_logits(t):
                pe.wait_ge(act_taken, A_H2 + 2 * t + 2)
                if t == 0:
                    pe.wait_ge(router_in, 32)
                j = D_[f"l{t}"]
                dfree(j)
                for k in range(KD):
                    mm = pe.matmul(dbank(j)[:, 0:E], hT[:, k, t * P:(t + 1) * P], rw[:, k, :],
                                   start=(k == 0), stop=(k == KD - 1))
                mm.then_inc(dve_full, 1)

            def counts(t):
                pe.wait_ge(hot_ready, t + 1)
                j = D_[f"c{t}"]
                dfree(j)
                for u in range(t + 1):
                    mm = pe.matmul(dbank(j)[:, 0:E], after if u == t else ones[:], hot32[:, u, :], start=(u == 0), stop=(u == t))
                mm.then_inc(dve_full, 1)

            def places(t):
                pe.wait_ge(places_ready, t + 1)
                for k in range(K):
                    n = (t % 2) * K + k
                    mm = pe.matmul(bank[7][:, 0:P], isl[:, n, :], isq[:, n, :], start=(t == 0 and k == 0),
                                   stop=(t == T - 1 and k == K - 1))
                mm.then_inc(places_used, 1)

            mixed(0, 0)
            mixed(0, 1)
            mixed(1, 0)
            mixed(1, 1)
            turn_rows(0)
            mixed(2, 0)
            mixed(2, 1)
            router_logits(0)
            turn_rows(1)
            mixed(3, 0)
            turn_rows(2)
            counts(0)
            router_logits(1)
            mixed(3, 1)
            places(0)
            counts(1)
            router_logits(2)
            turn_rows(3)
            places(1)
            router_logits(3)
            counts(2)
            counts(3)
            places(2)
            places(3)

            pe.wait_ge(table_in, 1)
            pe.transpose(bank[1][:, 0:P], tabT, ident[:]).then_inc(table_full, 1)
            pe.wait_ge(table_in, 2)
            pe.matmul(bank[2][:, 0:1], after, flag[:], start=True, stop=True).then_inc(table_full, 1)
            pe.wait_ge(table_in, 3)
            pe.matmul(bank[4][:, 0:16], tab, sel16[:], start=True, stop=True)
            pe.matmul(bank[5][0:96, 0:16], q_mod, sel16[:], start=True, stop=True)
            pe.matmul(bank[4][0:1, 32:48], eid[:], sel16[:], start=True, stop=True)
            pe.matmul(bank[4][0:1, 48:49], ones[:, 0:1], flag[:], start=True, stop=True).then_inc(table_full, 1)

            def turn(u, bank_no, src):
                for q in range(4):
                    mm = pe.transpose(bank[bank_no][:, q * P:(q + 1) * P], src[:, q * P:(q + 1) * P], ident[:])
                mm.then_inc(turn_full, 1)

            def item(i):
                pe.wait_ge(sel_ready, i + 1)
                pe.wait_ge(xlo_ready, i * 2 + 2)
                for p in range(2):
                    pe.wait_ge(banks_free, i * 2 + (p + 1))
                    gb, ub = bank[2 * p], bank[2 * p + 1]
                    pe.matmul(gb[:], sel[:], b_part[:, p * 512:p * 512 + 512], start=True, stop=False)
                    pe.matmul(ub[:], sel[:], b_part[:, 1024 + p * 512:1536 + p * 512], start=True, stop=False)
                    for h in range(8 * p, 8 * p + 8):
                        w = h // 2
                        pe.wait_ge(lo_ready, i * HALVES + (h + 1))
                        for k in range(2):
                            kk = 4 * ((w // 2) % 2) + 2 * (h % 2) + k
                            o = (gb, ub)[w % 2][:]
                            hi = w_hi[:, h % AHEAD, k * 512:(k + 1) * 512]
                            lo = w_lo[:, h % AHEAD, k * 512:(k + 1) * 512]
                            pe.matmul(o, x_hi[:, kk, :], hi, start=False, stop=False)
                            pe.matmul(o, x_hi[:, kk, :], lo, start=False, stop=False)
                            mm = pe.matmul(o, x_lo[:, kk, :], hi, start=False, stop=(kk == KD - 1))
                        mm.then_inc(half_used, 1)
                pe.wait_ge(act_ready, i * 2 + 1)
                pe.wait_ge(turn_taken, i * 4 + 1)
                turn(i * 4 + 2, 6, act[:, 0:512])
                pe.wait_ge(gathered, i * 16 + 32)
                pe.wait_ge(turn_taken, i * 4 + 2)
                turn(i * 4 + 3, 7, xg[:, 0:512])
                for half in range(2):
                    pe.wait_ge(turn_taken, i * 4 + 3 + 2 * half)
                    if half == 0:
                        for q in range(2):
                            pe.matmul(bank[4 + q][:], sel[:], b_part[:, 2048 + q * 512:2560 + q * 512], start=True,
                                      stop=False)
                    for c4 in range(2):
                        wq = 2 * half + c4
                        pe.wait_ge(down_in[wq], i * 16 + 16)
                        w = slot(4 + wq).rearrange("p (k n) -> p k n", k=2)
                        for k in range(2):
                            kk = 4 * half + 2 * c4 + k
                            for q in range(2):
                                mm = pe.matmul(bank[4 + q][:], actT[:, kk, :], w[:, k, q * 512:(q + 1) * 512],
                                               start=False, stop=(kk == KD - 1))
                        mm.then_inc(down_used, 1)
                    if half == 0:
                        pe.wait_ge(act_ready, i * 2 + 2)
                        turn(i * 4 + 4, 6, act[:, 512:1024])
                        pe.wait_ge(turn_taken, i * 4 + 4)
                        turn(i * 4 + 5, 7, xg[:, 512:1024])

            pe.wait_ge(gathered, 16)
            pe.wait_ge(table_in, 1)
            turn(0, 6, xg[:, 0:512])
            turn(1, 7, xg[:, 512:1024])
            pe.wait_ge(bias_ready, 1)
            pe.wait_ge(tables_ready, 1)
            with pe.Fori(0, E) as i:
                item(i)
            n_over = pe.value_load(over_i[0:1, 16:17], min_val=0, max_val=OVER)
            with pe.If(n_over > 0):
                with pe.Fori(E, ITEMS) as i:
                    item(i)

            pe.wait_ge(diag_ready, 1)
            for n in range(2 * T):
                t = n // 2
                pe.wait_ge(y_in[n], 16)
                if n >= 4:
                    pe.wait_ge(sum_taken, n - 3)
                for k in range(K - 1):
                    mm = pe.matmul(bank[n % 4][:], diag[:, t * (K - 1) + k, :], rows_of(t)[:, k, half_cols(n)],
                                   start=(k == 0), stop=(k == K - 2))
                mm.then_inc(sum_full, 1)

        @block.vector
        def _(v):
            steps = [0]

            def done(ins):
                steps[0] += 1
                ins.then_inc(dve_step, 1)
                v.wait_ge(dve_step, steps[0])

            tt, ts, stt = nc.vector.tensor_tensor, nc.vector.tensor_scalar, nc.vector.scalar_tensor_tensor

            v.wait_ge(csig_ready, 1)
            done(tt(sc_c[:], cs[:], csig[:], ALU.mult))
            v.wait_ge(rms_root, 1)
            nc.vector.reciprocal(ri[:, 0:T], rt[:, 0:T]).then_inc(rms_inv, 1)

            def modulate(n, at, k):
                v.wait_ge(landed[n % SLOTS], 16 * (n // SLOTS + 1))
                o = acc[:, at:at + 2048]
                if k == 0:
                    ins = ts(o, slot(n), sc_c[:, k:k + 1], None, ALU.mult)
                else:
                    ins = stt(out=o, in0=slot(n), scalar=sc_c[:, k:k + 1], in1=o, op0=ALU.mult, op1=ALU.add)
                ins.then_inc(ada_used, 1)
            for k in range(KD):
                modulate(LOAD_A[k], 0, k)
                v.wait_ge(ada_used, k + 1)
            v.wait_ge(act_taken, A_VEC + 1)
            v.wait_ge(mod_full, 1)
            done(tt(modA[:], bank[7][:, 0:16], vecT[:, 0:16], ALU.add))
            stt(out=a1[:], in0=modA[:, 8:16], scalar=1.0, in1=vecT[:, 48:56], op0=ALU.add,
                op1=ALU.mult).then_inc(affine_ready, 1)
            v.wait_ge(affine_ready, 1)
            for k in range(H_ACT, KD):
                v.wait_ge(h_full, k - H_ACT + 1)
                ts(hT[:, k, :], hbank(k)[:], a1[:, k:k + 1], modA[:, k:k + 1], ALU.mult, ALU.add).then_inc(h_taken, 1)

            for n in range(3 * IH):
                t, h = 1 + n // IH, n % IH
                w = (t + 1) * P
                o = score[:, SC_AT[t]:SC_AT[t] + w]
                v.wait_ge(act_taken, A_SC + n + 1)
                stt(out=o, in0=rel[:, n % 3, 0:w], scalar=iw[:, t, h:h + 1],
                    in1=future[:, S - w:S] if h == 0 else o, op0=ALU.mult, op1=ALU.add).then_inc(rel_added, 1)
                v.wait_ge(rel_added, n + 1)
            def lo(i, h):
                v.wait_ge(hi_ready, i * HALVES + (h + 1))
                w = h % HALVES // 2
                tt(w_lo[:, h % AHEAD, :], raw(w)[:, (h % 2) * HALF:(h % 2 + 1) * HALF],
                   w_hi[:, h % AHEAD, :].bitcast(F32), ALU.subtract).then_inc(lo_ready, 1)

            def x_rest(n, half):
                v.wait_ge(xhi_ready, n + 1)
                at = slice(4 * half, 4 * half + 4)
                tt(x_lo[:, at, :], xgT[:, at, :], x_hi[:, at, :].bitcast(F32), ALU.subtract).then_inc(xlo_ready, 1)

            for t in range(1, T):
                w = (t + 1) * P
                o = score[:, SC_AT[t]:SC_AT[t] + w]
                for r in range(N_SEL // 8):
                    n, rest = divmod((t - 1) * (N_SEL // 8) + r, B_EVERY)
                    if rest == B_EVERY - 1 and n < 2 * KD:
                        modulate(LOAD_B[n], 2048 * (n % 2), n // 2)
                    cur = o if r == 0 else work[:, 0:w]
                    done(nc.vector.max(mx8[:], cur))
                    done(nc.vector.match_replace(work[:, 0:w], mx8[:], cur, TAKEN))
                done(ts(work[:, 0:w], work[:, 0:w], -2.0e38, UNSEEN, ALU.is_ge, ALU.mult))
                done(tt(neg[:, NEG_AT[t]:NEG_AT[t] + w], work[:, 0:w], dist[:, S - w:S], ALU.add))
            done(ts(work[:, 0:P], future[:, 384:512], 0.0, UNSEEN, ALU.is_lt, ALU.mult))
            done(tt(neg[:, 0:P], work[:, 0:P], dist[:, 384:512], ALU.add))

            for t in range(T):
                v.wait_ge(rgsig_ready, t + 1)
                tt(rgs[:, t, :], dbank(D_RG + t)[:], rel[:, t % 2, :], ALU.mult).then_inc(dve_taken, 1)
            v.wait_ge(mod_full, 2)
            done(tt(modB[:], bank[7][:, 0:16], vecT[:, 24:40], ALU.add))
            stt(out=a2[:], in0=modB[:, 8:16], scalar=1.0, in1=vecT[:, 56:64], op0=ALU.add,
                op1=ALU.mult).then_inc(affine_ready, 1)
            v.wait_ge(g_bias_in, 32)
            for n in range(4):
                j = D_GROW + n
                v.wait_ge(dve_full, j + 1)
                tt(g_vals[:, n * 512:(n + 1) * 512], dbank(j)[0:1, :], g_bias[:, n * 512:(n + 1) * 512],
                   ALU.add).then_inc(dve_taken, 1)

            v.wait_ge(decay_ready, RH)
            for h in range(RH):
                if h >= 2:
                    v.wait_ge(ro_full, h - 1)
                for m in range(T):
                    j = D_RS + h * T + m
                    v.wait_ge(dve_full, j + 1)
                    tt(rs[:, h % 2, RS_AT[m]:RS_AT[m] + RS_W[m]], dbank(j)[:, 0:RS_W[m]],
                       decay[:, h, 0:RS_W[m]], ALU.mult).then_inc(dve_taken, 1)
            order = [(t, h) for t in range(T) for h in range(AH)]

            def rows(t):
                v.wait_ge(prob_ready, AH * (t + 1))
                done(nc.vector.reciprocal(pinv[:, :, t:t + 1], psum_[:, :, t:t + 1]))
                v.wait_ge(pv_full, AH * (t + 1))
                tt(att[:, t, :].rearrange("p (h d) -> p h d", h=AH),
                   bank[3 + 4 * (t % 2)][:].rearrange("p (h d) -> p h d", h=AH),
                   pinv[:, :, t:t + 1].broadcast_to((P, AH, HD)), ALU.mult).then_inc(pv_taken, 1)
            v.wait_ge(ro_full, RH)
            for n, (t, h) in enumerate(order):
                w = (t + 1) * P
                v.wait_ge(dve_full, D_QK + n + 1)
                if n >= 3:
                    v.wait_ge(prob_ready, n - 2)
                stt(out=lg[:, n % 3, 0:w], in0=neg[:, NEG_AT[t]:NEG_AT[t] + w], scalar=SLOPE[h],
                    in1=dbank(D_QK + n)[:, 0:w], op0=ALU.mult, op1=ALU.add).then_inc(dve_taken, 1)
                v.wait_ge(dve_taken, D_QK + n + 1)
                nc.vector.tensor_reduce(nmax[:, n % 4:n % 4 + 1], lg[:, n % 3, 0:w], AX.X, ALU.max,
                                        negate=True).then_inc(nmax_ready, 1)
                if n == AH:
                    v.wait_ge(ro_summed, 1)
                    done(nc.vector.reciprocal(ri[:], rt[:]))
                if n >= AH and n - AH < T * RH:
                    ret_t, ret_h = divmod(n - AH, RH)
                    o = rgs[:, ret_t, ret_h * P:(ret_h + 1) * P]
                    stt(out=o, in0=ro[:, ret_t, ret_h, :], scalar=ri[:, n - AH:n - AH + 1], in1=o,
                        op0=ALU.mult, op1=ALU.mult).then_inc(ret_ready, 1)
                if h == 4 and t >= 1:
                    rows(t - 1)
            rows(T - 1)

            v.wait_ge(g1_in, 16)
            def residual(t, q):
                j = D_[f"o{t}{q}"]
                o = xs[:, t, q * 512:(q + 1) * 512]
                v.wait_ge(dve_full, j + 1)
                tt(tmp, dbank(j)[:], g_row[:, q * 512:(q + 1) * 512], ALU.mult).then_inc(dve_taken, 1)
                v.wait_ge(dve_taken, j + 1)
                tt(o, o, tmp, ALU.add).then_inc(x2_ready, 1)
                v.wait_ge(x2_ready, 2 * t + q + 1)

            def inverse(t):
                v.wait_ge(rms_root, 2 + t)
                nc.vector.reciprocal(ri[:, t:t + 1], rt[:, t:t + 1]).then_inc(rms_inv, 1)

            def choose(t):
                j = D_[f"l{t}"]
                v.wait_ge(dve_full, j + 1)
                tt(lgt[:, t, :], dbank(j)[:, 0:E], rb[:], ALU.add).then_inc(dve_taken, 1)
                v.wait_ge(dve_taken, j + 1)
                done(nc.vector.max(top8[:, t, :], lgt[:, t, :]))
                done(nc.vector.max_index(idx8[:, t, :], top8[:, t, :], lgt[:, t, :]))
                done(nc.vector.tensor_copy(idxf[:, t * K:(t + 1) * K], idx8[:, t, 0:K]))
                o = hot[:, t * K:(t + 1) * K, :]
                done(tt(o, iota_p[:, 0:E].unsqueeze(1).broadcast_to((P, K, E)),
                        idxf[:, t * K:(t + 1) * K].unsqueeze(2).broadcast_to((P, K, E)), ALU.is_equal))
                nc.vector.tensor_reduce(hot32[:, t, :], o.rearrange("p k e -> p e k"), AX.X,
                                        ALU.add).then_inc(hot_ready, 1)

            def place(t):
                c4 = slice(t * K, (t + 1) * K)
                j = D_[f"c{t}"]
                v.wait_ge(dve_full, j + 1)
                tt(hotC, hot[:, c4, :], dbank(j)[:, 0:E].unsqueeze(1).broadcast_to((P, K, E)),
                   ALU.mult).then_inc(dve_taken, 1)
                v.wait_ge(dve_taken, j + 1)
                done(nc.vector.tensor_reduce(rank[:, c4], hotC, AX.X, ALU.add))
                done(ts(blk[:, c4], rank[:, c4], float(CAP), None, ALU.is_ge))
                for b in range(2, BLOCKS):
                    done(stt(out=blk[:, c4], in0=rank[:, c4], scalar=float(CAP * b), in1=blk[:, c4], op0=ALU.is_ge,
                             op1=ALU.add))
                done(stt(out=rank[:, c4], in0=blk[:, c4], scalar=-float(CAP), in1=rank[:, c4], op0=ALU.mult,
                         op1=ALU.add))
                done(stt(out=blk[:, c4], in0=blk[:, c4], scalar=float(E), in1=idxf[:, c4], op0=ALU.mult,
                         op1=ALU.add))
                if t >= 2:
                    v.wait_ge(places_used, t - 1)
                at = (t % 2) * K
                tt(isq[:, at:at + K, :], iota_p.unsqueeze(1).broadcast_to((P, K, P)),
                   blk[:, c4].unsqueeze(2).broadcast_to((P, K, P)), ALU.is_equal)
                for k in range(K):
                    n = t * K + k
                    last = ts(isl[:, at + k, :], iota_p, rank[:, n:n + 1], tok4[:, n:n + 1], ALU.is_equal, ALU.mult)
                last.then_inc(places_ready, 1)

            def bias_parts():
                v.wait_ge(bias_in, 16 * 6)
                done(nc.vector.tensor_copy(b_part, b_raw[0:96, :]))
                done(tt(b_raw[0:96, :], b_raw[0:96, :], b_part, ALU.subtract))
                done(nc.vector.tensor_copy(b_part[32:64, :], b_raw[32:64, :]))
                done(nc.vector.tensor_copy(b_part[64:96, :], b_raw[64:96, :]))
                done(tt(b_raw[64:96, :], b_raw[64:96, :], b_part[64:96, :], ALU.subtract))
                nc.vector.tensor_copy(b_part[64:96, :], b_raw[64:96, :]).then_inc(bias_ready, 1)

            residual(0, 0)
            residual(0, 1)
            inverse(0)
            residual(1, 0)
            residual(1, 1)
            inverse(1)
            bias_parts()
            v.wait_ge(late_consts, 1)
            residual(2, 0)
            residual(2, 1)
            choose(0)
            inverse(2)
            residual(3, 0)
            place(0)
            choose(1)
            residual(3, 1)
            inverse(3)
            place(1)
            choose(2)
            choose(3)
            place(2)
            place(3)
            v.wait_ge(places_used, T)
            nc.vector.tensor_copy(tabT, bank[7][:, 0:P]).then_inc(table_in, 1)
            v.wait_ge(table_in, 1)

            def lists(at, end):
                r = slice(at, end)
                done(ts(empty[:, r], dstf[:, r], 0.0, float(8 * S), ALU.is_equal, ALU.mult))
                done(stt(out=dstf[:, r], in0=dstf[:, r], scalar=-1.0, in1=empty[:, r], op0=ALU.add, op1=ALU.add))
                done(nc.vector.tensor_copy(dst_i[:, r], dstf[:, r]))
                return ts(tok_i[:, r], dst_i[:, r], 2, None, ALU.arith_shift_right)
            done(nc.vector.tensor_copy(dstf[:, 0:E], tabT[:, 0:E]))
            done(nc.vector.tensor_copy(hot96[:, 0:E], hot_first[0:96, :]))
            lists(0, E).then_inc(lists_ready, 1)
            v.wait_ge(table_full, 1)
            done(nc.vector.tensor_copy(tab, bank[1][:, 0:P]))
            done(nc.vector.tensor_reduce(pos[:], tab, AX.X, ALU.max))
            done(ts(flag[:], pos[:], 0.0, None, ALU.is_gt))
            nc.vector.memset(flag[0:E, :], 0.0).then_inc(table_in, 1)
            lo(0, 0)
            v.wait_ge(table_full, 2)
            done(nc.vector.tensor_copy(pos[:], bank[2][:, 0:1]))
            ts(sel16[:], iota_p[:, 0:16], pos[:, 0:1], flag[:, 0:1], ALU.is_equal, ALU.mult).then_inc(table_in, 1)
            tt(dgate[:], top8[:, :, 0:K], top8[:, :, 0:1].broadcast_to((P, T, K)), ALU.subtract).then_inc(gate_diff, 1)
            lo(0, 1)
            v.wait_ge(table_full, 3)
            done(nc.vector.tensor_copy(dstf[:, E:48], bank[4][:, 0:16]))
            done(nc.vector.tensor_copy(hot96[:, E:48], bank[5][0:96, 0:16]))
            done(nc.vector.tensor_copy(over_i[:], bank[4][0:1, 32:49]))
            for scratch in (pos, blk):
                nc.vector.memset(scratch[:], 0.0).then_inc(banks_free, 1)
            lists(E, 48).then_inc(tables_ready, 1)
            lo(0, 2)
            lo(0, 3)
            for half in range(2):
                x_rest(half, half)
            v.wait_ge(gate_exp, 1)
            done(nc.vector.tensor_reduce(ss[:, 0:T], gates[:], AX.X, ALU.add))
            done(nc.vector.reciprocal(ri[:, 0:T], ss[:, 0:T]))
            done(tt(gates[:], gates[:], ri[:, 0:T].unsqueeze(2).broadcast_to((P, T, K)), ALU.mult))

            def item(i):
                def clip_gate(p):
                    v.wait_ge(half_used, i * HALVES + 8 * (p + 1))
                    ts(gc[:, p, :], bank[2 * p][:], LIMIT, None, ALU.min).then_inc(gate_ready, 1)
                    ts(uc[:, p, :], bank[2 * p + 1][:], LIMIT, -LIMIT, ALU.min, ALU.max).then_inc(banks_free, 1)

                def product(p):
                    v.wait_ge(banks_free, i * 2 + (p + 3))
                    stt(out=gu_[:, p, :], in0=uc[:, p, :], scalar=1.0, in1=gc[:, p, :], op0=ALU.add,
                        op1=ALU.mult).then_inc(prod_ready, 1)

                def activation(p):
                    v.wait_ge(prod_ready, i * 2 + (p + 1))
                    v.wait_ge(sig_ready, i * 2 + (p + 1))
                    tt(act[:, p * 512:(p + 1) * 512], gu_[:, p, :], sg[:, p, :], ALU.mult).then_inc(act_ready, 1)
                for h in range(AHEAD, 11):
                    lo(i, h)
                clip_gate(0)
                lo(i, 11)
                product(0)
                lo(i, 12)
                activation(0)
                for h in range(13, HALVES + 3):
                    lo(i, h)
                clip_gate(1)
                product(1)
                lo(i, HALVES + 3)
                activation(1)
                for half in range(2):
                    x_rest(i * 2 + 2 + half, half)

            with v.Fori(0, E) as i:
                item(i)
            n_over = v.value_load(over_i[0:1, 16:17], min_val=0, max_val=OVER)
            with v.If(n_over > 0):
                with v.Fori(E, ITEMS) as i:
                    item(i)

            for t in range(T):
                for k in range(K - 1):
                    last = ts(diag[:, t * (K - 1) + k, :], ident[:], gates[:, t, k:k + 1], None, ALU.mult)
            last.then_inc(diag_ready, 1)
            v.wait_ge(last_rows_in, 32)

            def final(t):
                v.wait_ge(last_root, t + 1)
                done(nc.vector.reciprocal(ri[:, t:t + 1], rt[:, t:t + 1]))
                for n in (2 * t, 2 * t + 1):
                    o = xs[:, t, half_cols(n)]
                    stt(out=o, in0=o, scalar=ri[:, t:t + 1], in1=fg_row[:, half_cols(n)], op0=ALU.mult,
                        op1=ALU.mult).then_inc(out_ready, 1)
            for n in range(2 * T):
                t, cols = n // 2, half_cols(n)
                z, o = rows_of(t)[:, K - 1, cols], xs[:, t, cols]
                v.wait_ge(sum_full, n + 1)
                stt(out=z, in0=z, scalar=gates[:, t, K - 1:K], in1=bank[n % 4][:], op0=ALU.mult,
                    op1=ALU.add).then_inc(sum_taken, 1)
                v.wait_ge(sum_taken, n + 1)
                done(tt(z, z, g2_row[:, cols], ALU.mult))
                tt(o, o, z, ALU.add).then_inc(x3_ready, 1)
                if n % 2 == 0 and n > 0:
                    final(t - 1)
            final(T - 1)


_INS = ["x", "c", "ada_w", "ada_b", "norm1_g", "w_in", "mix_scale", "w_o", "norm2_g", "router_w",
        "router_b", "w_gu", "b_gu", "w_down", "b_down", "final_g"]
_OUTS = [((1, S, D), "float32")]


def kernel(**inputs):
    import concourse.bacc as bacc
    from concourse.bass_utils import run_bass_kernel_spmd as run

    nc = bacc.Bacc("TRN2", target_bir_lowering=False, num_devices=1)
    arrays, args = {}, []
    for name in _INS:
        a = np.ascontiguousarray(inputs[name])
        arrays[f"in_{name}"] = a
        args.append(nc.dram_tensor(f"in_{name}", a.shape, mybir.dt.from_np(a.dtype), kind="ExternalInput").ap())
    for i, (shape, dtype) in enumerate(_OUTS):
        args.append(nc.dram_tensor(f"out_{i}", shape, mybir.dt.from_np(np.dtype(dtype)),
                                   kind="ExternalOutput").ap())
    build(nc, *args)
    r = run(nc, [arrays], core_ids=[0])
    return r.results[0]["out_0"]
```
